# Optimizing a Trainium2 kernel written in Bass

```python
import jax, jax.numpy as jnp
from jax import lax
import numpy as np

D_MODEL = 1024
BATCH = 1
SEQ = 512
DEPTH = 2
DEC_BATCH = 8
DEC_SEQ = 1
PAST_LEN = 1024
PAGE_SIZE = 128

N_HEADS = 8
N_KV = 2
HEAD_DIM = 64
GROUP = N_HEADS // N_KV
WINDOW = 128
BLOCK = WINDOW
GLA_HEADS = 4
GLA_DK = 64
GLA_DV = 128
GATE_RANK = 16
GATE_TAU = 16.0
CHUNK = 16
D_FF = 2816
N_EXPERTS = 8
TOP_K = 2
D_FF_EXPERT = 1408
N_DENSE = (DEPTH + 1) // 2
N_MOE = DEPTH // 2
EPS = 1e-6

Q_W = N_HEADS * HEAD_DIM
KV_W = N_KV * HEAD_DIM
GK_W = GLA_HEADS * GLA_DK
GV_W = GLA_HEADS * GLA_DV
PROJ_W = Q_W + 2 * KV_W + 2 * GK_W + 2 * GV_W + GATE_RANK + 2 * D_MODEL

kernel_name = 'hybrid_swa_gla_adaln_decode_step'

def _split_points():
    sizes = (Q_W, KV_W, KV_W, GK_W, GK_W, GV_W, GATE_RANK, GV_W, D_MODEL, D_MODEL)
    pts, acc = [], 0
    for sz in sizes[:-1]:
        acc += sz
        pts.append(acc)
    return pts

def _alibi_slopes():
    return jnp.asarray(2.0 ** (-8.0 * np.arange(1, N_HEADS + 1) / N_HEADS), dtype=jnp.float32)

def _rms(x, g):
    x32 = x.astype(jnp.float32)
    y = x32 * lax.rsqrt(jnp.mean(x32 * x32, axis=-1, keepdims=True) + EPS)
    return (y * g.astype(jnp.float32)).astype(x.dtype)

def _sink_attend(scores, valid, sink, v, eq):
    scores = jnp.where(valid, scores, -jnp.inf)
    m = jnp.maximum(jnp.max(scores, axis=-1, keepdims=True), sink)
    p = jnp.exp(scores - m)
    denom = jnp.sum(p, axis=-1, keepdims=True) + jnp.exp(sink - m)
    return jnp.einsum(eq, (p / denom).astype(v.dtype), v)

def _swa_prompt(q, k, v, sinks):
    b, s = q.shape[0], q.shape[1]
    nb = s // BLOCK
    qb = q.reshape(b, nb, BLOCK, N_KV, GROUP, HEAD_DIM)
    kb = k.reshape(b, nb, BLOCK, N_KV, HEAD_DIM)
    vb = v.reshape(b, nb, BLOCK, N_KV, HEAD_DIM)
    pad = ((0, 0), (1, 0), (0, 0), (0, 0), (0, 0))
    kk = jnp.concatenate([jnp.pad(kb, pad)[:, :-1], kb], axis=2)
    vv = jnp.concatenate([jnp.pad(vb, pad)[:, :-1], vb], axis=2)
    scores = jnp.einsum('bnqkgd,bnskd->bnkgqs', qb, kk).astype(jnp.float32) * (HEAD_DIM ** -0.5)
    qpos = jnp.arange(BLOCK) + BLOCK
    kpos = jnp.arange(2 * BLOCK)
    dist = qpos[:, None] - kpos[None, :]
    slopes = _alibi_slopes().reshape(N_KV, GROUP)
    scores = scores - slopes[:, :, None, None] * dist.astype(jnp.float32)
    valid = ((dist >= 0) & (dist <= WINDOW))[None] & ((kpos[None, None, :] >= BLOCK) | (jnp.arange(nb)[:, None, None] > 0))
    sink = sinks.astype(jnp.float32).reshape(N_KV, GROUP)[None, None, :, :, None, None]
    out = _sink_attend(scores, valid[None, :, None, None], sink, vv, 'bnkgqs,bnskd->bnqkgd')
    return out.reshape(b, s, Q_W)

def _swa_sample(q, k, v, buf_k, buf_v, sinks):
    b, t = q.shape[0], q.shape[1]
    w = buf_k.shape[1]
    kk = jnp.concatenate([buf_k, k.astype(buf_k.dtype)], axis=1)
    vv = jnp.concatenate([buf_v, v.astype(buf_v.dtype)], axis=1)
    qg = q.reshape(b, t, N_KV, GROUP, HEAD_DIM)
    scores = jnp.einsum('btkgd,bskd->bkgts', qg, kk).astype(jnp.float32) * (HEAD_DIM ** -0.5)
    dist = (jnp.arange(t) + w)[:, None] - jnp.arange(w + t)[None, :]
    slopes = _alibi_slopes().reshape(N_KV, GROUP)
    scores = scores - slopes[:, :, None, None] * dist.astype(jnp.float32)
    valid = ((dist >= 0) & (dist <= WINDOW))[None, None, None]
    sink = sinks.astype(jnp.float32).reshape(N_KV, GROUP)[None, :, :, None, None]
    out = _sink_attend(scores, valid, sink, vv, 'bkgts,bskd->btkgd')
    return out.reshape(b, t, Q_W), kk[:, t:], vv[:, t:]

def _gla_chunked(q, k, v, log_a, S0):
    b, s, h = q.shape[0], q.shape[1], q.shape[2]
    nc = s // CHUNK

    def blk(t):
        return t.reshape(b, nc, CHUNK, h, t.shape[-1]).transpose(0, 3, 1, 2, 4)

    q, k, v, la = blk(q), blk(k), blk(v), blk(log_a)
    cum = jnp.cumsum(la, axis=3)
    causal = jnp.tril(jnp.ones((CHUNK, CHUNK), dtype=bool))
    diff = cum[:, :, :, :, None, :] - cum[:, :, :, None, :, :]
    decay_ij = jnp.exp(jnp.where(causal[:, :, None], diff, -jnp.inf))
    attn = jnp.einsum('bhnik,bhnjk,bhnijk->bhnij', q, k, decay_ij)
    o = jnp.einsum('bhnij,bhnjv->bhniv', attn, v)
    last = cum[:, :, :, -1:, :]
    ds = jnp.einsum('bhnjk,bhnjv->bhnkv', k * jnp.exp(last - cum), v)
    dec = jnp.exp(last[:, :, :, 0, :])

    def step(S, inp):
        d, u = inp
        return d[..., None] * S + u, S

    S_fin, S_in = lax.scan(step, S0, (jnp.moveaxis(dec, 2, 0), jnp.moveaxis(ds, 2, 0)))
    S_in = jnp.moveaxis(S_in, 0, 2)
    o = o + jnp.einsum('bhnik,bhnkv->bhniv', q * jnp.exp(cum), S_in)
    return o.transpose(0, 2, 3, 1, 4).reshape(b, s, h, GLA_DV), S_fin

def _gla_recurrent(q, k, v, log_a, S0):
    def step(S, inp):
        qt, kt, vt, lat = inp
        S = jnp.exp(lat)[..., None] * S + kt[..., :, None] * vt[..., None, :]
        return S, jnp.einsum('bhk,bhkv->bhv', qt, S)

    S, o = lax.scan(step, S0, (jnp.moveaxis(q, 1, 0), jnp.moveaxis(k, 1, 0), jnp.moveaxis(v, 1, 0), jnp.moveaxis(log_a, 1, 0)))
    return jnp.moveaxis(o, 0, 1), S

def _mixer(h, w_in, q_g, k_g, sinks, wa2, ba, gn_g, wpa, wpb, w_out, cache):
    b, s, _ = h.shape
    z = h @ w_in
    qa, ka, va, qb_, kb_, vb_, ga, rb, gate_a, gate_b = jnp.split(z, _split_points(), axis=-1)
    q = _rms(qa.reshape(b, s, N_HEADS, HEAD_DIM), q_g)
    k = _rms(ka.reshape(b, s, N_KV, HEAD_DIM), k_g)
    v = va.reshape(b, s, N_KV, HEAD_DIM)
    gq = qb_.reshape(b, s, GLA_HEADS, GLA_DK).astype(jnp.float32) * (GLA_DK ** -0.5)
    gk = kb_.reshape(b, s, GLA_HEADS, GLA_DK).astype(jnp.float32)
    gv = vb_.reshape(b, s, GLA_HEADS, GLA_DV).astype(jnp.float32)
    log_a = (jax.nn.log_sigmoid((ga @ wa2 + ba).astype(jnp.float32)) / GATE_TAU).reshape(b, s, GLA_HEADS, GLA_DK)
    if cache is None:
        a_out = _swa_prompt(q, k, v, sinks)
        cw = min(WINDOW, s)
        new_k, new_v = k[:, s - cw:], v[:, s - cw:]
        S0 = jnp.zeros((b, GLA_HEADS, GLA_DK, GLA_DV), jnp.float32)
        g_out, S = _gla_chunked(gq, gk, gv, log_a, S0)
        state_dtype = h.dtype
    else:
        buf_k, buf_v, S_prev = cache
        a_out, new_k, new_v = _swa_sample(q, k, v, buf_k, buf_v, sinks)
        g_out, S = _gla_recurrent(gq, gk, gv, log_a, S_prev.astype(jnp.float32))
        state_dtype = S_prev.dtype
    g_out = _rms(g_out, gn_g).reshape(b, s, GV_W).astype(h.dtype) * jax.nn.silu(rb)
    merged = jax.nn.sigmoid(gate_a) * (a_out @ wpa) + jax.nn.sigmoid(gate_b) * (g_out @ wpb)
    return merged @ w_out, (new_k, new_v, S.astype(state_dtype))

def _swiglu(h, wg, wu, wd):
    return (jax.nn.silu(h @ wg) * (h @ wu)) @ wd

def _moe(h, rw, rb, wg, wu, wd):
    logits = (h @ rw + rb).astype(jnp.float32)
    top_v, top_i = lax.top_k(logits, TOP_K)
    probs = jax.nn.softmax(top_v, axis=-1)
    gates = jnp.sum(jax.nn.one_hot(top_i, N_EXPERTS, dtype=jnp.float32) * probs[..., None], axis=1).astype(h.dtype)
    out = jnp.zeros_like(h)
    for e in range(N_EXPERTS):
        out = out + gates[:, e:e + 1] * _swiglu(h, wg[e], wu[e], wd[e])
    return out

def _layer(x, c, ada_w, ada_b, n1, n2, mix_params, ffn_params, is_moe, cache):
    mod = (jax.nn.silu(c) @ ada_w + ada_b)[:, None, :]
    sh1, sc1, g1, sh2, sc2, g2 = jnp.split(mod, 6, axis=-1)
    h = _rms(x, n1) * (1 + sc1) + sh1
    mix, new_state = _mixer(h, *mix_params, cache)
    x = x + g1 * mix
    h = _rms(x, n2) * (1 + sc2) + sh2
    b, s, d = h.shape
    h2 = h.reshape(b * s, d)
    f = _moe(h2, *ffn_params) if is_moe else _swiglu(h2, *ffn_params)
    x = x + g2 * f.reshape(b, s, d)
    return x, new_state

def setup_inputs(seed: int = 0) -> dict:
    key = jax.random.key(seed)
    ks = jax.random.split(key, 32)
    f32 = jnp.float32

    def nrm(k, shape, scale):
        return jax.random.normal(k, shape, f32) * scale

    cw = min(WINDOW, PAST_LEN)
    D = D_MODEL
    return {
        'x_prompt': nrm(ks[0], (BATCH, SEQ, D), 1.0),
        'x_sample': nrm(ks[1], (DEC_BATCH, DEC_SEQ, D), 1.0),
        'cache_k': nrm(ks[2], (DEPTH, DEC_BATCH, cw, N_KV, HEAD_DIM), 1.0),
        'cache_v': nrm(ks[3], (DEPTH, DEC_BATCH, cw, N_KV, HEAD_DIM), 1.0),
        'state_gla': nrm(ks[4], (DEPTH, DEC_BATCH, GLA_HEADS, GLA_DK, GLA_DV), 4.0),
        'c_prompt': nrm(ks[5], (BATCH, D), 1.0),
        'c_sample': nrm(ks[6], (DEC_BATCH, D), 1.0),
        'ada_w': nrm(ks[7], (DEPTH, D, 6 * D), 0.5 * D ** -0.5),
        'ada_b': nrm(ks[8], (DEPTH, 6 * D), 0.02),
        'norm1_g': 1.0 + nrm(ks[9], (DEPTH, D), 0.05),
        'norm2_g': 1.0 + nrm(ks[10], (DEPTH, D), 0.05),
        'w_in': nrm(ks[11], (DEPTH, D, PROJ_W), D ** -0.5),
        'q_norm_g': 1.0 + nrm(ks[12], (DEPTH, HEAD_DIM), 0.05),
        'k_norm_g': 1.0 + nrm(ks[13], (DEPTH, HEAD_DIM), 0.05),
        'attn_sinks': nrm(ks[14], (DEPTH, N_HEADS), 1.0),
        'gla_wa2': nrm(ks[15], (DEPTH, GATE_RANK, GK_W), GATE_RANK ** -0.5),
        'gla_ba': nrm(ks[16], (DEPTH, GK_W), 0.1),
        'gla_norm_g': 1.0 + nrm(ks[17], (DEPTH, GLA_DV), 0.05),
        'w_branch_a': nrm(ks[18], (DEPTH, Q_W, D), Q_W ** -0.5),
        'w_branch_b': nrm(ks[19], (DEPTH, GV_W, D), GV_W ** -0.5),
        'w_out': nrm(ks[20], (DEPTH, D, D), D ** -0.5),
        'ffn_w_gate': nrm(ks[21], (N_DENSE, D, D_FF), D ** -0.5),
        'ffn_w_up': nrm(ks[22], (N_DENSE, D, D_FF), D ** -0.5),
        'ffn_w_down': nrm(ks[23], (N_DENSE, D_FF, D), D_FF ** -0.5),
        'router_w': nrm(ks[24], (N_MOE, D, N_EXPERTS), D ** -0.5),
        'router_b': nrm(ks[25], (N_MOE, N_EXPERTS), 0.01),
        'moe_w_gate': nrm(ks[26], (N_MOE, N_EXPERTS, D, D_FF_EXPERT), D ** -0.5),
        'moe_w_up': nrm(ks[27], (N_MOE, N_EXPERTS, D, D_FF_EXPERT), D ** -0.5),
        'moe_w_down': nrm(ks[28], (N_MOE, N_EXPERTS, D_FF_EXPERT, D), D_FF_EXPERT ** -0.5),
    }

def reference(x_prompt, x_sample, cache_k, cache_v, state_gla, c_prompt, c_sample, ada_w, ada_b, norm1_g, norm2_g, w_in, q_norm_g, k_norm_g, attn_sinks, gla_wa2, gla_ba, gla_norm_g, w_branch_a, w_branch_b, w_out, ffn_w_gate, ffn_w_up, ffn_w_down, router_w, router_b, moe_w_gate, moe_w_up, moe_w_down):
    xp, xs = x_prompt, x_sample
    kp_l, vp_l, sp_l, ks_l, vs_l, ss_l = [], [], [], [], [], []
    for l in range(DEPTH):
        mix_params = (w_in[l], q_norm_g[l], k_norm_g[l], attn_sinks[l], gla_wa2[l], gla_ba[l], gla_norm_g[l], w_branch_a[l], w_branch_b[l], w_out[l])
        i = l // 2
        if l % 2 == 0:
            ffn_params, is_moe = (ffn_w_gate[i], ffn_w_up[i], ffn_w_down[i]), False
        else:
            ffn_params, is_moe = (router_w[i], router_b[i], moe_w_gate[i], moe_w_up[i], moe_w_down[i]), True
        xp, (kp, vp, sp) = _layer(xp, c_prompt, ada_w[l], ada_b[l], norm1_g[l], norm2_g[l], mix_params, ffn_params, is_moe, None)
        xs, (ksn, vsn, ssn) = _layer(xs, c_sample, ada_w[l], ada_b[l], norm1_g[l], norm2_g[l], mix_params, ffn_params, is_moe, (cache_k[l], cache_v[l], state_gla[l]))
        kp_l.append(kp); vp_l.append(vp); sp_l.append(sp)
        ks_l.append(ksn); vs_l.append(vsn); ss_l.append(ssn)
    return (xp, xs, jnp.stack(kp_l), jnp.stack(vp_l), jnp.stack(sp_l), jnp.stack(ks_l), jnp.stack(vs_l), jnp.stack(ss_l))


_drawn_inputs = setup_inputs


def setup_inputs(seed=0):
    import zlib

    import numpy as np

    out = dict(_drawn_inputs(seed))
    spreads = {}
    factors = {'q_norm_g': 8.0, 'attn_sinks': 20.65, 'gla_norm_g': 4.816, 'router_b': 5.544}
    for name, (base, spread) in spreads.items():
        noise = np.random.default_rng([zlib.crc32(name.encode()), seed]).standard_normal(out[name].shape)
        drawn = base * np.exp(spread * noise) if base else spread * noise
        out[name] = __import__('jax').numpy.asarray(drawn.astype(out[name].dtype))
    for name, factor in factors.items():
        out[name] = (out[name] * factor).astype(out[name].dtype)
    return out
```

```python
from contextlib import ExitStack

import numpy as np

import concourse.bass as bass
from concourse import mybir

F32 = mybir.dt.float32
F32R = mybir.dt.float32r
ACT = mybir.ActivationFunctionType
ALU = mybir.AluOpType
AX = mybir.AxisListType.X

P = 128
D = 1024
KT = D // P
T = 512
NS = 8
N = T + NS
HN = N // 2
L = 2
NB = T // P
NH, NKV, HD = 8, 2, 64
GH, GK, GV = 4, 64, 128
RANK = 16
BROW = 32
E = 8
FE = 11
SUB = 32
NI = P // SUB
EPS = 1e-6
SLOTS = 3
PAIRS = 3
ADA = 6 * KT
W1 = 15
W3 = 20
Z_GA, Z_Q, Z_K, Z_V, Z_GQ, Z_GK, Z_GV = 0, 1, 5, 6, 7, 9, 11
EXP_SLABS = 3 * FE
LAYER_SLABS = [W1 + W3 + 8 + 8 + 2 * EXP_SLABS, W1 + W3 + 8 + 8 + E * EXP_SLABS]
TOTAL = L * ADA + sum(LAYER_SLABS)
LEAD = 2

C_ID, C_ONE, C_BLK, C_U, C_M, C_BIAS, C_BS, C_RANK = 0, 128, 256, 384, 512, 640, 2688, 2824
C_END = C_RANK + 8
S_ADAB = 0
S_N = S_ADAB + L * ADA
S_QK = S_N + L * 2 * KT
S_GN = S_QK + L * 2
S_SINK = S_GN + L
S_SINKC = S_SINK + L * NH
S_RW = S_SINKC + L
S_RB = S_RW + KT * E
S_END = S_RB + E


def build(nc, xT, cT, wst, cst, sml, wa2, kcT, vc, st, yT, kp, vp, sp_, ks, vs, ss):
    ctx = ExitStack()
    with ctx:
        sems = {}
        def sem(name):
            if name not in sems:
                sems[name] = ctx.enter_context(nc.semaphore(name))
            return sems[name]

        pos = [(nc.sbuf_base + 31) // 32 * 32]

        def at(name, shape, dt, offset):
            return nc.alloc_sbuf_tensor_at(name, shape, dt, offset=offset)

        def fixed(name, shape, dt=F32):
            t = at(name, shape, dt, pos[0])
            n = 4 * int(np.prod(shape[1:]))
            pos[0] += (n + 31) // 32 * 32
            return t

        x = fixed("x", [P, KT, N])
        Hh = fixed("Hh", [P, KT, N], F32R)
        Hl = fixed("Hl", [P, KT, N], F32R)
        raw = fixed("raw", [P, SLOTS, 1024])
        wh = fixed("wh", [P, SLOTS, 1024], F32R)
        wl = fixed("wl", [P, SLOTS, 1024], F32R)
        B0 = pos[0]
        Bh = fixed("Bh", [P, 8, N], F32R)
        Bl = fixed("Bl", [P, 8, N], F32R)
        Z0 = pos[0]
        z = fixed("z", [P, W1, N])
        G0 = pos[0]
        g = fixed("g", [P, W3, N])
        cs = fixed("cs", [P, C_END])
        sm = fixed("sm", [P, S_END])
        wa = fixed("wa", [BROW + 1, L, 256])
        mod = fixed("mod", [P, L, ADA, 9])
        eps = fixed("eps", [P, 1])
        qg8 = fixed("qg8", [P, L])
        osmp = fixed("osmp", [P, GH, NS])
        xs_tmp = fixed("xs_tmp", [P, 2, NS])
        mx = fixed("mx", [P, NH]); nmx = fixed("nmx", [P, NH]); sk = fixed("sk", [P, NH])
        esk = fixed("esk", [P, NH]); rs = fixed("rs", [P, NH]); den = fixed("den", [P, NH])
        rec = fixed("rec", [P, NH])
        assert pos[0] <= nc.sbuf_usable_end, pos[0]

        c_in = at("c_in", [P, KT, 9], F32, G0)
        c_act = at("c_act", [P, KT, 9], F32, G0 + 288)
        sq = at("sq", [P, KT, N], F32, Z0)
        rt = at("rt", [P, N], F32, Z0 + 16640)
        ri = at("ri", [P, N], F32, Z0 + 18720)
        tn = at("tn", [P, KT, N], F32, G0)
        hf = at("hf", [P, KT, N], F32, G0 + 16640)
        hidh = at("hidh", [P, FE, N], F32R, Z0)
        hidl = at("hidl", [P, FE, N], F32R, Z0 + 22880)
        sg = at("sg", [P, 2, N], F32, Z0 + 45760)
        hm = at("hm", [P, 3, N], F32, Z0 + 49920)
        gbc = at("gbc", [P, E, N], F32, B0)
        GT = at("GT", [E, N], F32, B0 + 16640)
        GTm = at("GTm", [E, E, N], F32, Z0)
        lg = at("lg", [P, 5, E], F32, Z0 + 20800)
        rr = [at(f"rr{i}", [P, 5, E], F32, Z0 + 21000 + 160 * i + 88) for i in range(8)]
        r1 = [at(f"r1{i}", [P, 5, 1], F32, Z0 + 22624 + 32 * i) for i in range(10)]
        qsq = at("qsq", [P, 5, N], F32, G0)
        qrt = at("qrt", [P, 5, N], F32, G0 + 10400)
        sc = at("sc", [P, NH, 256], F32, G0)
        PT = at("PT", [P, 4, 512], F32, G0 + 8192)
        vtok = at("vtok", [P, NB, P], F32, G0 + 16384)
        kc = at("kc", [P, NS, 129], F32, G0 + 20800)
        vcs = at("vcs", [P, NS, P], F32, G0 + 24928)
        Sst = at("Sst", [P, NS, 2, GV], F32, G0 + 29024)
        scs = at("scs", [NS, NS, 129], F32, G0 + 37216)
        qs = at("qs", [P, NS, NH], F32, G0)
        pT = at("pT", [P, NS, NH], F32, G0 + 256)
        prow = at("prow", [1, NS, NH], F32, G0 + 512)
        vrow = at("vrow", [1, NS, P], F32, G0 + 768)
        smx = at("smx", [NS, NS], F32, G0 + 4864)
        sts = at("sts", [NS, NS], F32, G0 + 4896)
        ses = at("ses", [NS, NS], F32, G0 + 4928)
        srs = at("srs", [NS, NS], F32, G0 + 4960)
        sdn = at("sdn", [NS, NS], F32, G0 + 4992)
        srec = at("srec", [NS, NS], F32, G0 + 5024)
        kts = at("kts", [NS, 256], F32, G0 + 5120)
        vts = at("vts", [NS, 512], F32, G0 + 6144)
        kms = at("kms", [NS, NS, 256], F32, G0 + 8192)
        las = at("las", [NS, 256], F32, G0 + 16384)
        lab = at("lab", [NS, 256], F32, G0 + 17408)
        lac = at("lac", [NS, 256], F32, G0 + 18432)
        dcs = at("dcs", [P, 2, NS], F32, G0 + 19456)
        la = at("la", [P, NB, 256], F32, Z0 + 2080)
        lt = at("lt", [P, NB, 256], F32, Z0 + 2080 + 4096)
        cum = at("cum", [P, 2, T], F32, G0)
        qt = at("qt", [P, 2, T], F32, G0 + 4096)
        qe = at("qe", [P, 2, T], F32, G0 + 8192)
        KW = SUB * NI * (NI + 1) // 2
        kt = at("kt", [P, 2, NB, KW], F32, G0 + 12288)
        kd = at("kd", [P, 2, T], F32, G0 + 22528)
        kdt = at("kdt", [P, NB, 256], F32, G0 + 26624)
        att = at("att", [P, NB, GH, P], F32, G0 + 30720)
        dec = at("dec", [P, 2, NB], F32, G0 + 38912)
        gvt = at("gvt", [P, NB, 512], F32, B0 + 8320)
        S = at("S", [P, NB, 2, 2, GV], F32, B0 + 16640 + 8320)
        ta = at("ta", [P, 2, N], F32, Z0 + 27040)
        mf = at("mf", [P, KT, N], F32, Z0 + 10400)

        ident = cs[:, C_ID:C_ID + P]
        ones = cs[:, C_ONE:C_ONE + P]
        blk = cs[:, C_BLK:C_BLK + P]
        U16 = cs[:, C_U:C_U + P]
        MSK = cs[:, C_M:C_M + P]
        biasT = cs[:, C_BIAS:C_BIAS + 2048].rearrange("p (h s) -> p h s", h=NH)
        biasS = cs[0:NS, C_BS:C_BS + 129]
        rank8 = cs[:, C_RANK:C_RANK + E]

        ps = ctx.enter_context(nc.psum_tensor("ps", [P, 8, 512], F32))

        def pair(p):
            return ps[:, 2 * p:2 * p + 2, 0:HN]

        def two(ap):
            return ap.rearrange("p (a b) -> p a b", a=2)

        base = {}
        jobs = {}
        njobs = {}
        s = L * ADA
        j = 0
        for l in range(L):
            ne = 2 if l == 0 else E
            for name, ns_, nj in (("n1", 0, 1), ("w1", W1, W1), ("qk", 0, 5), ("w3", W3, W3), ("gn", 0, 4),
                                  ("br", 8, 16), ("wo", 8, 8), ("n2", 0, 1), ("rt", 0, 8 if l else 0),
                                  ("ff", ne * EXP_SLABS, ne * 30)):
                base[name, l] = s
                jobs[name, l] = j
                njobs[name, l] = nj
                s += ns_
                j += nj
        assert s == TOTAL

        def slot(s0, k, i=0):
            return (s0 + k) % SLOTS, (s0 + k) // SLOTS + i

        def r_use(s0, k, i=0):
            return (s0 - L * ADA + k) // SLOTS + i

        def psj(j0, k, i=0):
            return (j0 + k) % PAIRS, (j0 + k) // PAIRS + i

        def products_read(eng, name, l):
            end = jobs[name, l] + njobs[name, l]
            for p in range(PAIRS):
                if (end - p + 2) // PAIRS:
                    eng.wait_ge(acc_free[p], (end - p + 2) // PAIRS)

        raw_full = [sem(f"raw_full{i}") for i in range(SLOTS)]
        ada_used = [sem(f"ada_used{i}") for i in range(SLOTS)]
        hi_made = [sem(f"hi_made{i}") for i in range(SLOTS)]
        split_made = [sem(f"split_made{i}") for i in range(SLOTS)]
        split_used = [sem(f"split_used{i}") for i in range(SLOTS)]
        acc_full = [sem(f"acc_full{i}") for i in range(PAIRS)]
        acc_free = [sem(f"acc_free{i}") for i in range(PAIRS)]


        PER_LAYER = dict(sq_made=2 * KT, tn_made=2 * KT, hf_made=2 * KT, hfs_made=2, Hh_made=2 * KT, H_made=2 * KT,
                         qsq_made=5, qk_made=5, kc_in=16, vc_in=16, st_in=16, cache_out=6 * 16, S_out=2 * 16,
                         sc_done=NB, soft_in=NB, exp_done=NB, p_made=NB, pt_done=NB, pta_copied=NB, ptb_copied=NB,
                         av_done=NB, avh_made=NB, av_read=NB, pT_made=2, dah_made=2, gvt_made=2, S_made=NB,
                         osq_made=GH, og_made=GH, Bh_made=GH, B_made=GH, mf_made=KT, Mh_made=KT, M_made=KT,
                         xs_made=3 * KT, hidh_made=2 * FE, hid_made=2 * FE,
                         gated=0, rl_done=0, gate_made=0, gT_done=0, GTm_made=0, rt_exp_in=0, rt_exp=0)

        def upto(name, l, n):
            return n + l * PER_LAYER.get(name, 1)

        block = ctx.enter_context(nc.Block())

        @block.sync
        def _(sp):
            def slab(idx, j):
                sp.dma_start(raw[:, j, :], wst[idx, :, :]).then_inc(raw_full[j], 16)

            for j in range(SLOTS):
                slab(j, j)
            with sp.Fori(1, L * ADA // SLOTS) as i:
                for j in range(SLOTS):
                    sp.wait_ge(ada_used[j], i)
                    slab(i * SLOTS + j, j)
            n0 = L * ADA // SLOTS
            for j in range(SLOTS):
                sp.wait_ge(ada_used[j], n0)
                slab(L * ADA + j, j)
            nr = (TOTAL - L * ADA) // SLOTS
            with sp.Fori(1, nr) as i:
                for j in range(SLOTS):
                    sp.wait_ge(split_made[j], i)
                    slab((i + n0) * SLOTS + j, j)
            for j in range(LEAD):
                sp.wait_ge(split_made[j], nr)
                slab(TOTAL + j, j)
            for j in range(LEAD):
                sp.wait_ge(split_made[j], nr + 1)

        @block.gpsimd
        def _(pool):
            pool.dma_start(x[:], xT).then_inc(sem("x_in"), 16)
            pool.dma_start(c_in[:], cT).then_inc(sem("c_landed"), 16)
            pool.dma_start(sm[:], sml).then_inc(sem("small_in"), 16)
            pool.dma_start(cs[:], cst).then_inc(sem("const_in"), 16)
            pool.dma_start(wa[:], wa2).then_inc(sem("wa_in"), 16)
            outs = 0
            for l in range(L):
                pool.wait_ge(sem("Hh_made"), upto("Hh_made", l, KT))
                pool.wait_ge(sem("H_made"), upto("H_made", l, KT))
                pool.dma_start(kc[:, :, 0:P], kcT[l]).then_inc(sem("kc_in"), 16)
                pool.dma_start(vcs[:], vc[l]).then_inc(sem("vc_in"), 16)
                pool.dma_start(Sst[:], st[l]).then_inc(sem("st_in"), 16)
                pool.wait_ge(sem("qk_made"), upto("qk_made", l, 5))
                pool.dma_start(kp[l], z[:, Z_K, T - P:T]).then_inc(sem("cache_out"), 16)
                products_read(pool, "w1", l)
                pool.dma_start(vp[l], z[:, Z_V, T - P:T]).then_inc(sem("cache_out"), 16)
                pool.wait_ge(sem("kc_made"), upto("kc_made", l, 1))
                pool.dma_start(ks[l], kc[:, :, 1:1 + P]).then_inc(sem("cache_out"), 16)
                pool.wait_ge(sem("vc_in"), upto("vc_in", l, 16))
                pool.dma_start(vs[l, 0:P - 1], vcs[1:P, :, :]).then_inc(sem("cache_out"), 16)
                pool.wait_ge(sem("vrow_made"), upto("vrow_made", l, 1))
                pool.dma_start(vs[l, P - 1:P], vrow[:]).then_inc(sem("cache_out"), 16)
                pool.wait_ge(sem("Sst_made"), upto("Sst_made", l, 1))
                pool.dma_start(ss[l], Sst[:]).then_inc(sem("cache_out"), 16)
                pool.wait_ge(sem("S_made"), upto("S_made", l, NB))
                for r in range(2):
                    hp = slice(64 * r, 64 * r + 64)
                    pool.dma_start(sp_[l, hp], S[hp, NB - 1, :, r, :]).then_inc(sem("S_out"), 16)
            products_read(pool, "ff", L - 1)
            pool.dma_start(yT, x[:]).then_inc(sem("y_out"), 16)
            for l in range(L):
                pool.wait_ge(sem("cache_out"), upto("cache_out", l, 6 * 16))
                pool.wait_ge(sem("S_out"), upto("S_out", l, 32))
            pool.wait_ge(sem("y_out"), 16)

        @block.tensor
        def _(pe):
            def blocks(todo):
                for sl, b, xh, xl, p, first, last, s_first, s_last in todo:
                    w_h, w_l = wh[:, sl, b * P:b * P + P], wl[:, sl, b * P:b * P + P]
                    for h in range(2):
                        out = ps[:, 2 * p + h, 0:HN]
                        cols = slice(h * HN, h * HN + HN)
                        for q, (w, v) in enumerate(((w_h, xh), (w_h, xl), (w_l, xh))):
                            mm = pe.matmul(out, w, v[:, cols], start=first and q == 0, stop=last and q == 2)
                            if h == 0 and q == 0 and s_first is not None:
                                mm.then_inc(s_first, 1)
                    if last and s_last is not None:
                        mm.then_inc(s_last, 1)

            def slab_ready(s0, k, i):
                sl, _ = slot(s0, k)
                pe.wait_ge(split_made[sl], r_use(s0, k, i) + 1)
                return sl, split_used[(sl - 1) % SLOTS]

            def free_pair(j0, k, i=0):
                p, u = psj(j0, k, i)
                if not (isinstance(u, int) and u == 0):
                    pe.wait_ge(acc_free[p], u)
                return p

            def product8(s0, j0, k, i, xh, xl):
                sl, before = slab_ready(s0, k, i)
                p = free_pair(j0, k, i)
                blocks([(sl, b, xh[:, b, :], xl[:, b, :], p, b == 0, b == KT - 1, before if b == 0 else None, acc_full[p])
                        for b in range(KT)])

            def products8(name, l, n, xh, xl):
                s0, j0 = base[name, l], jobs[name, l]
                peel = 1 if j0 < PAIRS else 0
                for k in range(3 * peel):
                    product8(s0, j0, k, 0, xh, xl)
                with pe.Fori(peel, n // 3) as i:
                    for j in range(3):
                        product8(s0, j0, j, i, xh, xl)
                for k in range(n // 3 * 3, n):
                    product8(s0, j0, k, 0, xh, xl)

            def plain(out_pair, lhsT, rhs, first, last):
                for h in range(2):
                    mm = pe.matmul(ps[0:lhsT.shape[1], 2 * out_pair + h, 0:HN], lhsT, rhs[:, h * HN:h * HN + HN],
                                   start=first, stop=last)
                return mm

            pe.wait_ge(sem("c_made"), 1)
            for l in range(L):
                with pe.Fori(0, ADA // SLOTS) as i:
                    for j in range(SLOTS):
                        pe.wait_ge(raw_full[j], 16 * i + 16 * (l * ADA // SLOTS + 1))
                        for b in range(KT):
                            mm = pe.matmul(ps[:, 6 + l, bass.ds(27 * i + 9 * j, 9)], raw[:, j, b * P:b * P + P],
                                           c_act[:, b, :], start=b == 0, stop=b == KT - 1)
                        mm.then_inc(ada_used[j], 1)

            pe.wait_ge(sem("const_in"), 16)
            for l in range(L):
                def norm_sum(name, which):
                    j0 = jobs[name, l]
                    p = free_pair(j0, 0)
                    for k in range(KT):
                        pe.wait_ge(sem("sq_made"), upto("sq_made", l, which * KT + k + 1))
                        mm = plain(p, ones, sq[:, k, :], k == 0, k == KT - 1)
                    mm.then_inc(acc_full[p], 1)

                norm_sum("n1", 0)
                pe.wait_ge(sem("H_made"), upto("H_made", l, KT))
                products8("w1", l, W1, Hh, Hl)
                for i in range(5):
                    p = free_pair(jobs["qk", l], i)
                    pe.wait_ge(sem("qsq_made"), upto("qsq_made", l, i + 1))
                    plain(p, blk, qsq[:, i, :], True, True).then_inc(acc_full[p], 1)
                products_read(pe, "w1", l)
                pe.wait_ge(sem("mod_made"), 2 * L)
                for n in range(NB):
                    mm = pe.transpose(ps[:, 6, n * P:n * P + P], z[:, Z_V, n * P:n * P + P], ident)
                mm.then_inc(sem("vt_done"), 1)
                pe.wait_ge(sem("qk_made"), upto("qk_made", l, 5))
                for n in range(NB):
                    W = 2 * P if n else P
                    if n:
                        pe.wait_ge(sem("av_read"), upto("av_read", l, n))
                    for kv in range(NKV):
                        hp = slice(64 * kv, 64 * kv + 64)
                        for t in range(4):
                            mm = pe.matmul(ps[:, 2 * kv + t // 2, (t % 2) * 256:(t % 2) * 256 + W],
                                           z[hp, Z_Q + t, n * P:n * P + P], z[hp, Z_K, (n + 1) * P - W:(n + 1) * P],
                                           start=True, stop=True)
                    mm.then_inc(sem("sc_done"), 1)
                    pe.wait_ge(sem("p_made"), upto("p_made", l, n + 1))
                    if n == 0:
                        pe.wait_ge(sem("vtok_made"), upto("vtok_made", l, 1))
                    else:
                        pe.wait_ge(sem("pta_copied"), upto("pta_copied", l, n))
                        pe.wait_ge(sem("ptb_copied"), upto("ptb_copied", l, n))
                    for c in range(2 if n else 1):
                        for h in range(NH):
                            mm = pe.transpose(ps[:, 4 + 2 * c + h // 4, (h % 4) * P:(h % 4) * P + P],
                                              sc[:, h, c * P:c * P + P], ident)
                    mm.then_inc(sem("pt_done"), 1)
                    pe.wait_ge(sem("pta_copied"), upto("pta_copied", l, n + 1))
                    pe.wait_ge(sem("ptb_copied"), upto("ptb_copied", l, n + 1))
                    nc_ = 2 if n else 1
                    for kv in range(NKV):
                        for c in range(nc_):
                            mm = pe.matmul(ps[64 * kv:64 * kv + 64, 0, :], vtok[:, n - (nc_ - 1) + c, 64 * kv:64 * kv + 64],
                                           PT[:, 2 * c + kv, :], start=c == 0, stop=c == nc_ - 1)
                    mm.then_inc(sem("av_done"), 1)
                pe.wait_ge(sem("av_read"), upto("av_read", l, NB))
                pe.wait_ge(sem("qs_made"), upto("qs_made", l, 1))
                pe.wait_ge(sem("kc_made"), upto("kc_made", l, 1))
                for b in range(NS):
                    mm = pe.matmul(ps[0:NS, b // 2, (b % 2) * 256:(b % 2) * 256 + 129], qs[:, b, :], kc[:, b, :],
                                   start=True, stop=True)
                mm.then_inc(sem("dsc_done"), 1)
                pe.wait_ge(sem("dp_made"), upto("dp_made", l, 1))
                for b in range(NS):
                    pe.transpose(ps[:, 4, b * NH:b * NH + NH], scs[:, b, 0:P], ident[0:NS, 0:NS])
                for b in range(NS):
                    pe.matmul(ps[0:1, 5, b * NH:b * NH + NH], scs[:, b, P:P + 1], ident[0:NS, 0:NS], start=True, stop=True)
                for b in range(NS):
                    mm = pe.matmul(ps[0:1, 6 + b // 4, (b % 4) * P:(b % 4) * P + P], z[:, Z_V, T + b:T + b + 1], ident,
                                   start=True, stop=True)
                mm.then_inc(sem("dpt_done"), 1)
                pe.wait_ge(sem("vrow_made"), upto("vrow_made", l, 1))
                pe.wait_ge(sem("pT_made"), upto("pT_made", l, 2))
                pe.wait_ge(sem("vc_in"), upto("vc_in", l, 16))
                for b in range(NS):
                    pe.matmul(ps[:, 0, b * NH:b * NH + NH], vcs[:, b, :], pT[:, b, :], start=True, stop=False)
                    mm = pe.matmul(ps[:, 0, b * NH:b * NH + NH], vrow[0:1, b, :], prow[0:1, b, :], start=False, stop=True)
                mm.then_inc(sem("dav_done"), 1)
                for q in range(2):
                    pe.transpose(ps[0:NS, 4, q * P:q * P + P], z[:, Z_GK + q, T:N], ident)
                for h in range(GH):
                    mm = pe.transpose(ps[0:NS, 5, h * P:h * P + P], z[:, Z_GV + h, T:N], ident)
                mm.then_inc(sem("kvt_done"), 1)
                if l == 0:
                    pe.wait_ge(sem("wa_in"), 16)
                pe.wait_ge(sem("ones_made"), upto("ones_made", l, 1))
                pe.matmul(ps[0:NS, 6, 0:256], z[0:BROW + 1, Z_GA, T:N], wa[:, l, :], start=True, stop=True
                          ).then_inc(sem("dlg_done"), 1)
                pe.wait_ge(sem("las_made"), upto("las_made", l, 1))
                for q in range(2):
                    mm = pe.matmul(ps[:, 7, q * NS:q * NS + NS], las[:, q * P:q * P + P], ident[0:NS, 0:NS],
                                   start=True, stop=True)
                mm.then_inc(sem("dla_done"), 1)
                pe.wait_ge(sem("kms_made"), upto("kms_made", l, 1))
                pe.wait_ge(sem("da_read"), upto("da_read", l, 1))
                for b in range(NS):
                    for h in range(GH):
                        q, r = h // 2, h % 2
                        c0 = (b * 2 + q) * GV
                        mm = pe.matmul(ps[64 * r:64 * r + 64, c0 // 512, c0 % 512:c0 % 512 + GV],
                                       kms[:, b, 64 * h:64 * h + 64], vts[:, h * GV:h * GV + GV], start=True, stop=True)
                mm.then_inc(sem("kv_done"), 1)
                pe.wait_ge(sem("Sst_made"), upto("Sst_made", l, 1))
                for r in range(2):
                    for q in range(2):
                        for b in range(NS):
                            mm = pe.matmul(ps[:, 4 + r, q * NS + b:q * NS + b + 1], Sst[64 * r:64 * r + 64, b, q, :],
                                           z[64 * r:64 * r + 64, Z_GQ + q, T + b:T + b + 1], start=True, stop=True)
                mm.then_inc(sem("do_done"), 1)
                for n in range(NB):
                    mm = pe.matmul(ps[:, n // 2, (n % 2) * 256:(n % 2) * 256 + 256], z[0:BROW + 1, Z_GA, n * P:n * P + P],
                                   wa[:, l, :], start=True, stop=True)
                mm.then_inc(sem("lg_done"), 1)
                pe.wait_ge(sem("la_made"), upto("la_made", l, 1))
                for q in range(2):
                    for n in range(NB):
                        mm = pe.matmul(ps[:, 2 + q, n * P:n * P + P], la[:, n, q * P:q * P + P], U16, start=True, stop=True)
                mm.then_inc(sem("cum_done"), 1)
                pe.wait_ge(sem("osmp_made"), upto("osmp_made", l, 1))
                for n in range(NB):
                    for h in range(GH):
                        mm = pe.transpose(ps[:, 4 + n, h * P:h * P + P], z[:, Z_GV + h, n * P:n * P + P], ident)
                mm.then_inc(sem("gvt_done"), 1)
                pe.wait_ge(sem("kd_made"), upto("kd_made", l, 1))
                for n in range(NB):
                    for q in range(2):
                        mm = pe.transpose(ps[:, n // 2, (n % 2) * 256 + q * P:(n % 2) * 256 + q * P + P],
                                          kd[:, q, n * P:n * P + P], ident)
                mm.then_inc(sem("kdt_done"), 1)
                pe.wait_ge(sem("kdt_made"), upto("kdt_made", l, 1))
                pe.wait_ge(sem("gvt_made"), upto("gvt_made", l, 2))
                for n in range(NB):
                    for h in range(GH):
                        q, r = h // 2, h % 2
                        c0 = (n % 2) * 256 + q * GV
                        mm = pe.matmul(ps[64 * r:64 * r + 64, 2 + n // 2, c0:c0 + GV], kdt[:, n, h * 64:h * 64 + 64],
                                       gvt[:, n, h * GV:h * GV + GV], start=True, stop=True)
                mm.then_inc(sem("ds_done"), 1)
                pe.wait_ge(sem("qt_made"), upto("qt_made", l, 1))
                pe.wait_ge(sem("kt_made"), upto("kt_made", l, 1))
                for n in range(NB):
                    for h in range(GH):
                        q, r = h // 2, h % 2
                        for i in range(NI):
                            rows = SUB * (i + 1)
                            k0 = SUB * i * (i + 1) // 2
                            c0 = (n % 2) * 256 + q * P + SUB * i
                            mm = pe.matmul(ps[0:rows, 4 + 2 * r + n // 2, c0:c0 + SUB],
                                           kt[64 * r:64 * r + 64, q, n, k0:k0 + rows],
                                           qt[64 * r:64 * r + 64, q, n * P + SUB * i:n * P + SUB * i + SUB],
                                           start=True, stop=True)
                mm.then_inc(sem("at_done"), 1)
                pe.wait_ge(sem("att_made"), upto("att_made", l, 1))
                pe.wait_ge(sem("S_made"), upto("S_made", l, NB))
                pe.wait_ge(sem("qe_made"), upto("qe_made", l, 1))
                for n in range(NB):
                    for h in range(GH):
                        q, r = h // 2, h % 2
                        mm = pe.matmul(ps[:, h, n * P:n * P + P], gvt[:, n, h * GV:h * GV + GV], att[:, n, h, :],
                                       start=True, stop=n == 0)
                        if n:
                            mm = pe.matmul(ps[:, h, n * P:n * P + P], S[:, n - 1, q, r, :], qe[:, q, n * P:n * P + P],
                                           start=False, stop=True)
                mm.then_inc(sem("o_done"), 1)
                pe.wait_ge(sem("o_read"), upto("o_read", l, 1))
                products8("w3", l, W3, Hh, Hl)
                for h in range(GH):
                    p = free_pair(jobs["gn", l], h)
                    pe.wait_ge(sem("osq_made"), upto("osq_made", l, h + 1))
                    plain(p, ones, mf[:, h, :], True, True).then_inc(acc_full[p], 1)
                pe.wait_ge(sem("B_made"), upto("B_made", l, 4))
                s0, j0 = base["br", l], jobs["br", l]
                for mp in range(4):
                    for br in range(2):
                        sl, before = slab_ready(s0, 2 * mp + br, 0)
                        for m in range(2):
                            p = free_pair(j0, 4 * mp + 2 * br + m)
                            blocks([(sl, 4 * m + k, Bh[:, 4 * br + k, :], Bl[:, 4 * br + k, :], p, k == 0, k == 3,
                                     before if m == 0 and k == 0 else None, acc_full[p]) for k in range(4)])
                pe.wait_ge(sem("M_made"), upto("M_made", l, KT))
                products8("wo", l, KT, Hh, Hl)
                norm_sum("n2", 1)
                pe.wait_ge(sem("H_made"), upto("H_made", l, 2 * KT))
                if l == 1:
                    for n in range(NB + 1):
                        rows = P if n < NB else NS
                        for k in range(KT):
                            mm = pe.matmul(ps[0:rows, 6, n * E:n * E + E], hf[:, k, n * P:n * P + rows],
                                           sm[:, S_RW + k * E:S_RW + k * E + E], start=k == 0, stop=k == KT - 1)
                    mm.then_inc(sem("rl_done"), 1)
                    pe.wait_ge(sem("gate_made"), upto("gate_made", l, 1))
                    for n in range(NB + 1):
                        rows = P if n < NB else NS
                        mm = pe.transpose(ps[0:E, 6 + (n == NB), (n % NB) * P:(n % NB) * P + rows], rr[7][0:rows, n, :],
                                          ident[0:rows, 0:rows])
                    mm.then_inc(sem("gT_done"), 1)
                    pe.wait_ge(sem("GTm_made"), upto("GTm_made", l, 1))
                    for e in range(E):
                        p = free_pair(jobs["rt", l], e)
                        plain(p, ones[0:E, :], GTm[:, e, :], True, True).then_inc(acc_full[p], 1)
                ne = 2 if l == 0 else E
                s0, j0 = base["ff", l], jobs["ff", l]
                with pe.Fori(0, ne) as e:
                    for k in range(2 * FE):
                        sl, before = slab_ready(s0, k, e * FE)
                        p, u = psj(j0, k)
                        pe.wait_ge(acc_free[p], u + e * 10)
                        blocks([(sl, b, Hh[:, b, :], Hl[:, b, :], p, b == 0, b == KT - 1,
                                 before if b == 0 else None, acc_full[p]) for b in range(KT)])
                    pe.wait_ge(sem("hid_made"), upto("hid_made", l, (e + 1) * FE))
                    for m in range(KT):
                        p, u = psj(j0, 2 * FE + m)
                        pe.wait_ge(acc_free[p], u + e * 10)
                        for k in range(FE):
                            bi = m * FE + k
                            if bi % KT == 0:
                                sl, before = slab_ready(s0, 2 * FE + bi // KT, e * FE)
                            blocks([(sl, bi % KT, hidh[:, k, :], hidl[:, k, :], p, k == 0, k == FE - 1,
                                     before if bi % KT == 0 else None, acc_full[p])])

        @block.scalar
        def _(act):
            steps = [0]

            def link(inst):
                steps[0] += 1
                inst.then_inc(sem("act_step"), 1)
                act.wait_ge(sem("act_step"), steps[0])

            def split_high(s0, k, i=0):
                sl, u = slot(s0, k + LEAD, i)
                r = r_use(s0, k + LEAD, i)
                act.wait_ge(raw_full[sl], 16 * (u + 1))
                if sl == SLOTS - 1:
                    act.wait_ge(split_used[sl], r + 1)
                elif not (isinstance(r, int) and r == 0):
                    act.wait_ge(split_used[sl], r)
                act.activation(wh[:, sl, :], raw[:, sl, :], ACT.Copy).then_inc(hi_made[sl], 1)

            def take(j0, k, i=0):
                p, u = psj(j0, k, i)
                act.wait_ge(acc_full[p], u + 1)
                return p

            act.wait_ge(sem("c_landed"), 16)
            act.activation(c_act[:], c_in[:], ACT.Silu).then_inc(sem("c_made"), 1)
            first = base["w1", 0]
            act.wait_ge(sem("x_in"), 16)
            for l in range(L):
                ne = 2 if l == 0 else E

                def norm(name, which):
                    if which:
                        products_read(act, "wo", l)
                    elif l:
                        products_read(act, "ff", l - 1)
                    for k in range(KT):
                        act.activation(sq[:, k, :], x[:, k, :], ACT.Square).then_inc(sem("sq_made"), 1)
                    if name == "n1" and l == 0:
                        act.wait_ge(sem("eps_made"), 1)
                    p = take(jobs[name, l], 0)
                    act.activation(two(rt[:]), pair(p), ACT.Sqrt, bias=eps[:], scale=1.0 / D).then_inc(acc_free[p], 1)
                    if name == "n1" and l == 0:
                        act.wait_ge(sem("mod_made"), 2 * L)
                    for k in range(KT):
                        act.wait_ge(sem("tn_made"), upto("tn_made", l, which * KT + k + 1))
                        act.activation(hf[:, k, 0:T], tn[:, k, 0:T], ACT.Identity, bias=mod[:, l, (3 * which) * KT + k, 0:1],
                                       scale=mod[:, l, (3 * which + 1) * KT + k, 0:1]).then_inc(sem("hf_made"), 1)
                    act.wait_ge(sem("hf_made"), upto("hf_made", l, (which + 1) * KT))
                    act.wait_ge(sem("hfs_made"), upto("hfs_made", l, which + 1))
                    for k in range(KT):
                        act.activation(Hh[:, k, :], hf[:, k, :], ACT.Copy).then_inc(sem("Hh_made"), 1)

                norm("n1", 0)
                if l == 0:
                    for k in range(LEAD):
                        split_high(first, k - LEAD)
                s0, j0 = base["w1", l], jobs["w1", l]
                with act.Fori(0, W1 // 3) as i:
                    for j in range(3):
                        split_high(s0, j, i)
                        p = take(j0, j, i)
                        act.activation(two(z[:, bass.ds(3 * i + j, 1), :].rearrange("p o n -> p (o n)")), pair(p), ACT.Copy
                                       ).then_inc(acc_free[p], 1)
                products_read(act, "w1", l)
                for i in range(5):
                    act.activation(qsq[:, i, :], z[:, Z_Q + i, :], ACT.Square).then_inc(sem("qsq_made"), 1)
                for i in range(5):
                    p = take(jobs["qk", l], i)
                    act.activation(two(qrt[:, i, :]), pair(p), ACT.Sqrt, bias=eps[:], scale=1.0 / HD
                                   ).then_inc(acc_free[p], 1)
                act.wait_ge(sem("vt_done"), upto("vt_done", l, 1))
                act.wait_ge(sem("qk_made"), upto("qk_made", l, 5))
                act.activation(vtok[:].rearrange("p a b -> p (a b)"), ps[:, 6, :], ACT.Copy).then_inc(sem("vtok_made"), 1)
                for n in range(NB):
                    W = 2 * P if n else P
                    act.wait_ge(sem("soft_in"), upto("soft_in", l, n + 1))
                    for h in range(NH):
                        act.activation(sc[:, h, 0:W], sc[:, h, 0:W], ACT.Exp, bias=nmx[:, h:h + 1], accum_out=rs[:, h:h + 1])
                    act.activation(esk[:], sk[:], ACT.Exp).then_inc(sem("exp_done"), 1)
                    act.wait_ge(sem("pt_done"), upto("pt_done", l, n + 1))
                    act.activation(PT[:, 0:2, :], ps[:, 4:6, :], ACT.Copy).then_inc(sem("pta_copied"), 1)
                    act.wait_ge(sem("av_done"), upto("av_done", l, n + 1))
                    act.activation(Bh[:, 0:4, n * P:n * P + P], ps[:, 0, :].rearrange("p (t c) -> p t c", t=4), ACT.Copy
                                   ).then_inc(sem("avh_made"), 1)
                act.wait_ge(sem("dsoft_in"), upto("dsoft_in", l, 1))
                link(act.activation(scs[:], scs[:], ACT.Exp))
                act.activation(ses[:], sts[:], ACT.Exp).then_inc(sem("dexp_done"), 1)
                act.wait_ge(sem("dpt_done"), upto("dpt_done", l, 1))
                act.activation(pT[:].rearrange("p b h -> p (b h)"), ps[:, 4, 0:NS * NH], ACT.Copy).then_inc(sem("pT_made"), 1)
                act.activation(prow[:].rearrange("p b h -> p (b h)"), ps[0:1, 5, 0:NS * NH], ACT.Copy
                               ).then_inc(sem("pT_made"), 1)
                act.wait_ge(sem("dav_done"), upto("dav_done", l, 1))
                dav = ps[:, 0, 0:NS * NH].rearrange("p (b k t) -> p k t b", b=NS, k=NKV)
                for kv in range(NKV):
                    hp = slice(64 * kv, 64 * kv + 64)
                    act.activation(Bh[hp, 0:4, T:N], dav[hp, kv], ACT.Copy).then_inc(sem("dah_made"), 1)
                act.wait_ge(sem("kvt_done"), upto("kvt_done", l, 1))
                act.activation(kts[:], ps[0:NS, 4, 0:256], ACT.Copy).then_inc(sem("kts_made"), 1)
                act.wait_ge(sem("dlg_made"), upto("dlg_made", l, 1))
                link(act.activation(lab[:], las[:], ACT.Abs))
                link(act.activation(lab[:], lab[:], ACT.Exp, scale=-1.0))
                act.activation(lab[:], lab[:], ACT.Ln, bias=1.0).then_inc(sem("lab_made"), 1)
                act.wait_ge(sem("dla_done"), upto("dla_done", l, 1))
                act.activation(dcs[:].rearrange("p q b -> p (q b)"), ps[:, 7, 0:2 * NS], ACT.Exp, scale=1.0 / 16
                               ).then_inc(sem("dcs_made"), 1)
                act.wait_ge(sem("do_done"), upto("do_done", l, 1))
                for r in range(2):
                    mm = act.activation(osmp[:].rearrange("p (q r) b -> p r q b", q=2)[:, r],
                                        ps[:, 4 + r, 0:2 * NS].rearrange("p (q b) -> p q b", q=2), ACT.Copy, scale=0.125)
                mm.then_inc(sem("osmp_made"), 1)
                act.wait_ge(sem("plg_made"), upto("plg_made", l, 1))
                link(act.activation(lt[:], la[:], ACT.Abs))
                link(act.activation(lt[:], lt[:], ACT.Exp, scale=-1.0))
                act.activation(lt[:], lt[:], ACT.Ln, bias=1.0).then_inc(sem("lt_made"), 1)
                act.wait_ge(sem("cum_done"), upto("cum_done", l, 1))
                act.wait_ge(sem("cache_out"), upto("cache_out", l, 6 * 16))
                link(act.activation(cum[:], ps[:, 2:4, :], ACT.Copy))
                act.activation(qe[:], cum[:], ACT.Exp).then_inc(sem("qe_exp"), 1)
                act.wait_ge(sem("qt_in"), upto("qt_in", l, 1))
                act.activation(qt[:], qt[:], ACT.Exp).then_inc(sem("qt_exp"), 1)
                for q in range(2):
                    for n in range(NB):
                        last = n * P + P - 1
                        act.activation(kd[:, q, n * P:n * P + P], cum[:, q, n * P:n * P + P], ACT.Exp, scale=-1.0,
                                       bias=cum[:, q, last:last + 1])
                mm = act.activation(dec[:], cum[:, :, P - 1::P], ACT.Exp)
                mm.then_inc(sem("kd_exp"), 1)
                for q in range(2):
                    for n in range(NB):
                        for i in range(NI):
                            k0 = SUB * i * (i + 1) // 2
                            ref = n * P + SUB * i + SUB // 2 - 1
                            mm = act.activation(kt[:, q, n, k0:k0 + SUB * (i + 1)], cum[:, q, n * P:n * P + SUB * (i + 1)],
                                                ACT.Exp, scale=-1.0, bias=cum[:, q, ref:ref + 1])
                mm.then_inc(sem("kt_exp"), 1)
                act.wait_ge(sem("gvt_done"), upto("gvt_done", l, 1))
                act.activation(gvt[:, 0:2, :], ps[:, 4:6, :], ACT.Copy).then_inc(sem("gvt_made"), 1)
                act.wait_ge(sem("kdt_done"), upto("kdt_done", l, 1))
                act.activation(kdt[:].rearrange("p (a b) c -> p a (b c)", a=2), ps[:, 0:2, :], ACT.Copy
                               ).then_inc(sem("kdt_made"), 1)
                act.wait_ge(sem("o_done"), upto("o_done", l, 1))
                act.activation(z[:, Z_Q:Z_Q + 4, 0:T], ps[:, 0:4, :], ACT.Copy, scale=0.125)
                act.activation(z[:, Z_Q:Z_Q + 4, T:N], osmp[:], ACT.Copy).then_inc(sem("o_read"), 1)
                s0, j0 = base["w3", l], jobs["w3", l]

                def w3_tile(k, i, m, f):
                    split_high(s0, k, i)
                    p = take(j0, k, i)
                    act.activation(two(g[:, bass.ds(m, 1), :].rearrange("p o n -> p (o n)")), pair(p), f
                                   ).then_inc(acc_free[p], 1)

                for k in range(4):
                    w3_tile(k, 0, k, ACT.Silu)
                with act.Fori(0, 5) as i:
                    for j in range(3):
                        w3_tile(4 + j, i, 3 * i + (4 + j), ACT.Sigmoid)
                w3_tile(19, 0, 19, ACT.Sigmoid)
                act.wait_ge(sem("o_read"), upto("o_read", l, 1))
                products_read(act, "w3", l)
                for h in range(GH):
                    act.activation(mf[:, h, :], z[:, Z_Q + h, :], ACT.Square).then_inc(sem("osq_made"), 1)
                for h in range(GH):
                    p = take(jobs["gn", l], h)
                    act.activation(two(mf[:, 4 + h, :]), pair(p), ACT.Sqrt, bias=eps[:], scale=1.0 / GV
                                   ).then_inc(acc_free[p], 1)
                for h in range(GH):
                    act.wait_ge(sem("og_made"), upto("og_made", l, h + 1))
                    act.activation(Bh[:, 4 + h, :], z[:, Z_Q + h, :], ACT.Copy).then_inc(sem("Bh_made"), 1)
                for k in range(8):
                    split_high(base["br", l], k)
                    if k % 2:
                        for m in (k - 1, k):
                            act.wait_ge(sem("mf_made"), upto("mf_made", l, m + 1))
                            act.activation(Hh[:, m, :], mf[:, m, :], ACT.Copy).then_inc(sem("Mh_made"), 1)
                for k in range(8):
                    split_high(base["wo", l], k)
                norm("n2", 1)
                s0, j0 = base["ff", l], jobs["ff", l]
                if l == 1:
                    act.wait_ge(sem("rt_exp_in"), upto("rt_exp_in", l, 1))
                    act.activation(r1[5][:], r1[4][:], ACT.Exp).then_inc(sem("rt_exp"), 1)
                    for e in range(E):
                        p = take(jobs["rt", l], e)
                        act.activation(two(gbc[:, e, :]), pair(p), ACT.Copy).then_inc(acc_free[p], 1)
                with act.Fori(0, ne) as e:
                    for m in range(FE):
                        split_high(s0, 2 * m, e * FE)
                        p, u = psj(j0, 2 * m)
                        act.wait_ge(acc_full[p], u + e * 10 + 1)
                        act.activation(two(sg[:, m % 2, :]), pair(p), ACT.Silu).then_inc(acc_free[p], 1)
                        split_high(s0, 2 * m + 1, e * FE)
                        p, u = psj(j0, 2 * m + 1)
                        act.wait_ge(acc_free[p], u + e * 10 + 1)
                        act.activation(hidh[:, m, :], hm[:, m % 3, :], ACT.Copy).then_inc(sem("hidh_made"), 1)
                    for k in range(FE):
                        split_high(s0, 2 * FE + k, e * FE)

        @block.vector
        def _(dve):
            steps = [0]

            def link(inst):
                steps[0] += 1
                inst.then_inc(sem("dve_step"), 1)
                dve.wait_ge(sem("dve_step"), steps[0])

            def split_low(s0, k, i=0):
                sl, _ = slot(s0, k + LEAD, i)
                dve.wait_ge(hi_made[sl], r_use(s0, k + LEAD, i) + 1)
                dve.tensor_tensor(wl[:, sl, :], raw[:, sl, :], wh[:, sl, :].bitcast(F32), ALU.subtract
                                  ).then_inc(split_made[sl], 1)

            def take(j0, k, i=0):
                p, u = psj(j0, k, i)
                dve.wait_ge(acc_full[p], u + 1)
                return p

            def bc(ap, n, axis=2):
                v = ap.unsqueeze(axis)
                return v.broadcast_to([n if i == axis else k for i, k in enumerate(v.shape)])

            dve.memset(eps[:], EPS).then_inc(sem("eps_made"), 1)
            dve.wait_ge(sem("small_in"), 16)
            dve.tensor_scalar(qg8[:], sm[:, S_QK:S_QK + 2 * L:2], 0.125, None, ALU.mult).then_inc(sem("qg8_made"), 1)
            for l in range(L):
                dve.wait_ge(ada_used[(l * ADA + ADA - 1) % SLOTS], (l * ADA + ADA - 1) // SLOTS + 1)
                link(dve.tensor_tensor(mod[:, l], ps[:, 6 + l, 0:9 * ADA].rearrange("p (m c) -> p m c", c=9),
                                       bc(sm[:, S_ADAB + l * ADA:S_ADAB + l * ADA + ADA], 9), ALU.add))
                for w in range(2):
                    sc1 = mod[:, l, (3 * w + 1) * KT:(3 * w + 2) * KT, :]
                    dve.scalar_tensor_tensor(out=sc1, in0=sc1, scalar=1.0,
                                             in1=bc(sm[:, S_N + (2 * l + w) * KT:S_N + (2 * l + w + 1) * KT], 9),
                                             op0=ALU.add, op1=ALU.mult).then_inc(sem("mod_made"), 1)

            def add_residual(l, p, m, which, n_tmp):
                gi = (2 + 3 * which) * KT + m
                dve.scalar_tensor_tensor(out=x[:, m, 0:HN], in0=ps[:, 2 * p, 0:HN], scalar=mod[:, l, gi, 0:1],
                                         in1=x[:, m, 0:HN], op0=ALU.mult, op1=ALU.add)
                dve.scalar_tensor_tensor(out=x[:, m, HN:T], in0=ps[:, 2 * p + 1, 0:T - HN], scalar=mod[:, l, gi, 0:1],
                                         in1=x[:, m, HN:T], op0=ALU.mult, op1=ALU.add)
                dve.tensor_tensor(xs_tmp[:, m % 2, :], ps[:, 2 * p + 1, T - HN:HN], mod[:, l, gi, 1:9], ALU.mult
                                  ).then_inc(sem("xs_made"), 1)
                dve.wait_ge(sem("xs_made"), n_tmp)
                dve.tensor_tensor(x[:, m, T:N], x[:, m, T:N], xs_tmp[:, m % 2, :], ALU.add).then_inc(acc_free[p], 1)

            dve.wait_ge(sem("x_in"), 16)
            dve.wait_ge(sem("const_in"), 16)
            dve.wait_ge(sem("mod_made"), 2 * L)
            dve.wait_ge(sem("qg8_made"), 1)
            for l in range(L):
                ne = 2 if l == 0 else E

                def norm(name, which):
                    p, u = psj(jobs[name, l], 0)
                    dve.wait_ge(acc_free[p], u + 1)
                    link(dve.reciprocal(ri[:], rt[:]))
                    for k in range(KT):
                        dve.tensor_tensor(tn[:, k, :], x[:, k, :], ri[:], ALU.mult).then_inc(sem("tn_made"), 1)
                    dve.wait_ge(sem("tn_made"), upto("tn_made", l, (which + 1) * KT))
                    link(dve.tensor_tensor(hf[:, :, T:N], tn[:, :, T:N], mod[:, l, (3 * which + 1) * KT:(3 * which + 2) * KT, 1:9], ALU.mult))
                    dve.tensor_tensor(hf[:, :, T:N], hf[:, :, T:N], mod[:, l, 3 * which * KT:(3 * which + 1) * KT, 1:9], ALU.add
                                      ).then_inc(sem("hfs_made"), 1)
                    for k in range(KT):
                        dve.wait_ge(sem("Hh_made"), upto("Hh_made", l, which * KT + k + 1))
                        dve.tensor_tensor(Hl[:, k, :], hf[:, k, :], Hh[:, k, :].bitcast(F32), ALU.subtract
                                          ).then_inc(sem("H_made"), 1)

                norm("n1", 0)
                if l == 0:
                    for k in range(LEAD):
                        split_low(base["w1", 0], k - LEAD)
                with dve.Fori(0, W1 // 3) as i:
                    for j in range(3):
                        split_low(base["w1", l], j, i)
                products_read(dve, "w1", l)
                dve.memset(z[BROW:BROW + 1, Z_GA, :], 1.0).then_inc(sem("ones_made"), 1)
                for i in range(5):
                    p, u = psj(jobs["qk", l], i)
                    dve.wait_ge(acc_free[p], u + 1)
                    link(dve.reciprocal(qrt[:, i, :], qrt[:, i, :]))
                    gain = qg8[:, l:l + 1] if i < 4 else sm[:, S_QK + 2 * l + 1:S_QK + 2 * l + 2]
                    dve.scalar_tensor_tensor(out=z[:, Z_Q + i, :], in0=z[:, Z_Q + i, :], scalar=gain, in1=qrt[:, i, :],
                                             op0=ALU.mult, op1=ALU.mult).then_inc(sem("qk_made"), 1)
                dve.wait_ge(sem("qk_made"), upto("qk_made", l, 5))
                for n in range(NB):
                    W = 2 * P if n else P
                    dve.wait_ge(sem("sc_done"), upto("sc_done", l, n + 1))
                    if n:
                        dve.wait_ge(sem("pt_done"), upto("pt_done", l, n))
                    for kv in range(NKV):
                        mm = dve.tensor_tensor(sc[:, 4 * kv:4 * kv + 4, 0:W],
                                               ps[:, 2 * kv:2 * kv + 2, :].rearrange("p a (b s) -> p (a b) s", b=2)[:, :, 0:W],
                                               biasT[:, 4 * kv:4 * kv + 4, 2 * P - W:2 * P], ALU.add)
                    link(mm)
                    link(dve.tensor_reduce(mx[:], sc[:, :, 0:W], AX, ALU.max))
                    link(dve.tensor_tensor(mx[:], mx[:], sm[:, S_SINK + l * NH:S_SINK + l * NH + NH], ALU.max))
                    dve.tensor_scalar(nmx[:], mx[:], -1.0, None, ALU.mult)
                    dve.tensor_tensor(sk[:], sm[:, S_SINK + l * NH:S_SINK + l * NH + NH], mx[:], ALU.subtract
                                      ).then_inc(sem("soft_in"), 1)
                    dve.wait_ge(sem("exp_done"), upto("exp_done", l, n + 1))
                    link(dve.tensor_tensor(den[:], rs[:], esk[:], ALU.add))
                    link(dve.reciprocal(rec[:], den[:]))
                    dve.tensor_tensor(sc[:, :, 0:W], sc[:, :, 0:W], bc(rec[:], W), ALU.mult).then_inc(sem("p_made"), 1)
                    dve.wait_ge(sem("pt_done"), upto("pt_done", l, n + 1))
                    if n:
                        dve.tensor_copy(PT[:, 2:4, :], ps[:, 6:8, :]).then_inc(sem("ptb_copied"), 1)
                    else:
                        dve.memset(den[:], 0.0).then_inc(sem("ptb_copied"), 1)
                    dve.wait_ge(sem("avh_made"), upto("avh_made", l, n + 1))
                    dve.tensor_tensor(Bl[:, 0:4, n * P:n * P + P], ps[:, 0, :].rearrange("p (t c) -> p t c", t=4),
                                      Bh[:, 0:4, n * P:n * P + P].bitcast(F32), ALU.subtract).then_inc(sem("av_read"), 1)
                link(dve.memset(qs[:], 0.0))
                for kv in range(NKV):
                    hp = slice(64 * kv, 64 * kv + 64)
                    mm = dve.tensor_copy(qs[hp, :, 4 * kv:4 * kv + 4].rearrange("p b t -> p t b"), z[hp, Z_Q:Z_Q + 4, T:N])
                mm.then_inc(sem("qs_made"), 1)
                dve.wait_ge(sem("kc_in"), upto("kc_in", l, 16))
                dve.tensor_copy(kc[:, :, P:P + 1].rearrange("p b o -> p (b o)"), z[:, Z_K, T:N]).then_inc(sem("kc_made"), 1)
                dve.wait_ge(sem("dsc_done"), upto("dsc_done", l, 1))
                link(dve.tensor_tensor(scs[:], ps[0:NS, 0:4, :].rearrange("p a (b s) -> p (a b) s", b=2)[:, :, 0:129],
                                       bc(biasS, NS, 1), ALU.add))
                link(dve.tensor_reduce(smx[:], scs[:], AX, ALU.max))
                sinkc = sm[0:NS, S_SINKC + l:S_SINKC + l + 1]
                link(dve.tensor_scalar(smx[:], smx[:], sinkc, None, ALU.max))
                dve.tensor_tensor(scs[:], scs[:], bc(smx[:], 129), ALU.subtract)
                dve.tensor_scalar(sts[:], smx[:], -1.0, sinkc, ALU.mult, ALU.add).then_inc(sem("dsoft_in"), 1)
                dve.wait_ge(sem("dexp_done"), upto("dexp_done", l, 1))
                link(dve.tensor_reduce(srs[:], scs[:], AX, ALU.add))
                link(dve.tensor_tensor(sdn[:], srs[:], ses[:], ALU.add))
                link(dve.reciprocal(srec[:], sdn[:]))
                dve.tensor_tensor(scs[:], scs[:], bc(srec[:], 129), ALU.mult).then_inc(sem("dp_made"), 1)
                dve.wait_ge(sem("dpt_done"), upto("dpt_done", l, 1))
                dve.tensor_copy(vrow[:].rearrange("p (a b) v -> p a (b v)", a=2), ps[0:1, 6:8, :]).then_inc(sem("vrow_made"), 1)
                dav = ps[:, 0, 0:NS * NH].rearrange("p (b k t) -> p k t b", b=NS, k=NKV)
                for kv in range(NKV):
                    hp = slice(64 * kv, 64 * kv + 64)
                    dve.wait_ge(sem("dah_made"), upto("dah_made", l, kv + 1))
                    mm = dve.tensor_tensor(Bl[hp, 0:4, T:N], dav[hp, kv], Bh[hp, 0:4, T:N].bitcast(F32), ALU.subtract)
                mm.then_inc(sem("da_read"), 1)
                dve.wait_ge(sem("dlg_done"), upto("dlg_done", l, 1))
                dve.tensor_copy(las[:], ps[0:NS, 6, 0:256]).then_inc(sem("dlg_made"), 1)
                dve.wait_ge(sem("kts_made"), upto("kts_made", l, 1))
                dve.tensor_tensor(kms[:], bc(kts[:], NS, 1), bc(ident[0:NS, 0:NS], 256), ALU.mult)
                dve.tensor_copy(vts[:], ps[0:NS, 5, :]).then_inc(sem("kms_made"), 1)
                dve.wait_ge(sem("lab_made"), upto("lab_made", l, 1))
                link(dve.tensor_scalar(lac[:], las[:], 0.0, None, ALU.min))
                dve.tensor_tensor(las[:], lac[:], lab[:], ALU.subtract).then_inc(sem("las_made"), 1)
                dve.wait_ge(sem("dcs_made"), upto("dcs_made", l, 1))
                dve.wait_ge(sem("st_in"), upto("st_in", l, 16))
                link(dve.tensor_tensor(Sst[:], Sst[:], bc(dcs[:].rearrange("p q b -> p b q"), GV, 3), ALU.mult))
                dve.wait_ge(sem("kv_done"), upto("kv_done", l, 1))
                dve.tensor_tensor(Sst[:].rearrange("p b q v -> p (b q v)"), Sst[:].rearrange("p b q v -> p (b q v)"),
                                  ps[:, 0:4, :].rearrange("p a c -> p (a c)"), ALU.add).then_inc(sem("Sst_made"), 1)
                dve.wait_ge(sem("lg_done"), upto("lg_done", l, 1))
                dve.tensor_copy(la[:].rearrange("p n c -> p (n c)"), ps[:, 0:2, :].rearrange("p a c -> p (a c)")
                                ).then_inc(sem("plg_made"), 1)
                dve.wait_ge(sem("lt_made"), upto("lt_made", l, 1))
                link(dve.tensor_scalar(la[:], la[:], 0.0, None, ALU.min))
                dve.tensor_tensor(la[:], la[:], lt[:], ALU.subtract).then_inc(sem("la_made"), 1)
                dve.wait_ge(sem("qe_exp"), upto("qe_exp", l, 1))
                refs = cum[:, :, SUB // 2 - 1::SUB]
                dve.tensor_tensor(qt[:].rearrange("p q (i c) -> p q i c", c=SUB), cum[:].rearrange("p q (i c) -> p q i c", c=SUB),
                                  bc(refs, SUB, 3), ALU.subtract).then_inc(sem("qt_in"), 1)
                dve.tensor_tensor(qe[:], qe[:], z[:, Z_GQ:Z_GQ + 2, 0:T], ALU.mult).then_inc(sem("qe_made"), 1)
                dve.memset(att[:], 0.0)
                dve.memset(S[:], 0.0)
                dve.wait_ge(sem("qt_exp"), upto("qt_exp", l, 1))
                dve.tensor_tensor(qt[:], qt[:], z[:, Z_GQ:Z_GQ + 2, 0:T], ALU.mult).then_inc(sem("qt_made"), 1)
                dve.wait_ge(sem("kd_exp"), upto("kd_exp", l, 1))
                dve.tensor_tensor(kd[:], kd[:], z[:, Z_GK:Z_GK + 2, 0:T], ALU.mult).then_inc(sem("kd_made"), 1)
                dve.wait_ge(sem("kt_exp"), upto("kt_exp", l, 1))
                for i in range(NI):
                    k0 = SUB * i * (i + 1) // 2
                    rows = SUB * (i + 1)
                    gk = z[:, Z_GK:Z_GK + 2, 0:T].rearrange("p q (n c) -> p q n c", n=NB)[:, :, :, 0:rows]
                    mm = dve.tensor_tensor(kt[:, :, :, k0:k0 + rows], kt[:, :, :, k0:k0 + rows], gk, ALU.mult)
                mm.then_inc(sem("kt_made"), 1)
                dve.wait_ge(sem("gvt_done"), upto("gvt_done", l, 1))
                dve.tensor_copy(gvt[:, 2:4, :], ps[:, 6:8, :]).then_inc(sem("gvt_made"), 1)
                dve.wait_ge(sem("ds_done"), upto("ds_done", l, 1))
                for n in range(NB):
                    for r in range(2):
                        hp = slice(64 * r, 64 * r + 64)
                        for q in range(2):
                            dsn = ps[hp, 2 + n // 2, (n % 2) * 256 + q * GV:(n % 2) * 256 + q * GV + GV]
                            if n == 0:
                                mm = dve.tensor_copy(S[hp, 0, q, r, :], dsn)
                            else:
                                mm = dve.scalar_tensor_tensor(out=S[hp, n, q, r, :], in0=S[hp, n - 1, q, r, :],
                                                              scalar=dec[hp, q, n:n + 1], in1=dsn, op0=ALU.mult, op1=ALU.add)
                    mm.then_inc(sem("S_made"), 1)
                    dve.wait_ge(sem("S_made"), upto("S_made", l, n + 1))
                dve.wait_ge(sem("at_done"), upto("at_done", l, 1))
                for r in range(2):
                    src = ps[:, 4 + 2 * r:6 + 2 * r, :].rearrange("p a (b q c) -> p (a b) q c", b=2, q=2)
                    dst = att[:].rearrange("p n (q r) c -> p r n q c", q=2)
                    for i in range(NI):
                        rows = SUB * (i + 1)
                        cols = slice(SUB * i, SUB * i + SUB)
                        mk = bc(bc(MSK[0:rows, cols], 2, 1), NB, 1)
                        mm = dve.tensor_tensor(dst[0:rows, r, :, :, cols], src[0:rows, :, :, cols], mk, ALU.mult)
                mm.then_inc(sem("att_made"), 1)
                with dve.Fori(0, 6) as i:
                    for j in range(3):
                        split_low(base["w3", l], j, i)
                for k in (18, 19):
                    split_low(base["w3", l], k)
                for h in range(GH):
                    p, u = psj(jobs["gn", l], h)
                    dve.wait_ge(acc_free[p], u + 1)
                    link(dve.reciprocal(mf[:, 4 + h, :], mf[:, 4 + h, :]))
                    link(dve.scalar_tensor_tensor(out=z[:, Z_Q + h, :], in0=z[:, Z_Q + h, :],
                                                  scalar=sm[:, S_GN + l:S_GN + l + 1], in1=mf[:, 4 + h, :],
                                                  op0=ALU.mult, op1=ALU.mult))
                    dve.tensor_tensor(z[:, Z_Q + h, :], z[:, Z_Q + h, :], g[:, h, :], ALU.mult).then_inc(sem("og_made"), 1)
                dve.wait_ge(sem("S_out"), upto("S_out", l, 32))
                for h in range(GH):
                    dve.wait_ge(sem("Bh_made"), upto("Bh_made", l, h + 1))
                    dve.tensor_tensor(Bl[:, 4 + h, :], z[:, Z_Q + h, :], Bh[:, 4 + h, :].bitcast(F32), ALU.subtract
                                      ).then_inc(sem("B_made"), 1)
                s0, j0 = base["br", l], jobs["br", l]
                for mp in range(4):
                    split_low(s0, 2 * mp)
                    for m in range(2):
                        p = take(j0, 4 * mp + m)
                        dve.tensor_tensor(two(ta[:, m, :]), two(g[:, 4 + 2 * mp + m, :]), pair(p), ALU.mult
                                          ).then_inc(acc_free[p], 1)
                    split_low(s0, 2 * mp + 1)
                    for m in range(2):
                        p = take(j0, 4 * mp + 2 + m)
                        dve.tensor_tensor(two(mf[:, 2 * mp + m, :]), two(g[:, 12 + 2 * mp + m, :]), pair(p), ALU.mult
                                          ).then_inc(acc_free[p], 1)
                    p, u = psj(j0, 4 * mp + 3)
                    dve.wait_ge(acc_free[p], u + 1)
                    for m in range(2):
                        dve.tensor_tensor(mf[:, 2 * mp + m, :], mf[:, 2 * mp + m, :], ta[:, m, :], ALU.add
                                          ).then_inc(sem("mf_made"), 1)
                    for m in range(2):
                        dve.wait_ge(sem("Mh_made"), upto("Mh_made", l, 2 * mp + m + 1))
                        dve.tensor_tensor(Hl[:, 2 * mp + m, :], mf[:, 2 * mp + m, :], Hh[:, 2 * mp + m, :].bitcast(F32),
                                          ALU.subtract).then_inc(sem("M_made"), 1)
                s0, j0 = base["wo", l], jobs["wo", l]
                for k in range(KT):
                    split_low(s0, k)
                    p = take(j0, k)
                    add_residual(l, p, k, 0, upto("xs_made", l, k + 1))
                norm("n2", 1)
                if l == 1:
                    link(dve.memset(lg[:], 0.0))
                    dve.wait_ge(sem("rl_done"), upto("rl_done", l, 1))
                    rb = sm[:, S_RB:S_RB + E]
                    dve.tensor_tensor(lg[:, 0:NB, :], ps[:, 6, 0:NB * E].rearrange("p (n e) -> p n e", e=E), bc(rb, NB, 1), ALU.add)
                    link(dve.tensor_tensor(lg[0:NS, NB, :], ps[0:NS, 6, NB * E:NB * E + E], rb[0:NS, :], ALU.add))
                    rk = bc(rank8, NB + 1, 1)

                    def col(i):
                        return r1[i][:].rearrange("p n o -> p (n o)")

                    def choose(logits, best, chosen, tmp, i):
                        link(dve.tensor_reduce(col(i), logits[:], AX, ALU.max))
                        link(dve.tensor_tensor(tmp[:], logits[:], bc(col(i), E), ALU.is_equal))
                        link(dve.tensor_tensor(tmp[:], tmp[:], rk, ALU.mult))
                        link(dve.tensor_reduce(col(i + 1), tmp[:], AX, ALU.max))
                        link(dve.tensor_tensor(chosen[:], tmp[:], bc(col(i + 1), E), ALU.is_equal))

                    choose(lg, None, rr[0], rr[1], 0)
                    link(dve.scalar_tensor_tensor(out=rr[2][:], in0=rr[0][:], scalar=-3.0e38, in1=lg[:], op0=ALU.mult, op1=ALU.add))
                    choose(rr[2], None, rr[3], rr[4], 2)
                    dve.tensor_tensor(col(4), col(2), col(0), ALU.subtract).then_inc(sem("rt_exp_in"), 1)
                    dve.wait_ge(sem("rt_exp"), upto("rt_exp", l, 1))
                    link(dve.tensor_scalar(col(6), col(5), 1.0, None, ALU.add))
                    link(dve.reciprocal(col(7), col(6)))
                    link(dve.tensor_tensor(col(8), col(5), col(7), ALU.mult))
                    dve.tensor_tensor(rr[5][:], rr[0][:], bc(col(7), E), ALU.mult)
                    link(dve.tensor_tensor(rr[6][:], rr[3][:], bc(col(8), E), ALU.mult))
                    dve.tensor_tensor(rr[7][:], rr[5][:], rr[6][:], ALU.add).then_inc(sem("gate_made"), 1)
                    dve.wait_ge(sem("gT_done"), upto("gT_done", l, 1))
                    dve.tensor_copy(GT[:, 0:T], ps[0:E, 6, :])
                    link(dve.tensor_copy(GT[:, T:N], ps[0:E, 7, 0:NS]))
                    for e in range(E):
                        mm = dve.tensor_scalar(GTm[:, e, :], GT[:], ident[0:E, e:e + 1], None, ALU.mult)
                    mm.then_inc(sem("GTm_made"), 1)
                    products_read(dve, "rt", l)
                s0, j0 = base["ff", l], jobs["ff", l]
                with dve.Fori(0, ne) as e:
                    for m in range(FE):
                        split_low(s0, 2 * m, e * FE)
                        p, u = psj(j0, 2 * m)
                        dve.wait_ge(acc_free[p], u + e * 10 + 1)
                        if l == 1:
                            dve.tensor_tensor(sg[:, m % 2, :], sg[:, m % 2, :],
                                              gbc[:, bass.ds(e, 1), :].rearrange("p o n -> p (o n)"), ALU.mult
                                              ).then_inc(sem("gated"), 1)
                            dve.wait_ge(sem("gated"), upto("gated", l, e * FE + m + 1))
                        split_low(s0, 2 * m + 1, e * FE)
                        p, u = psj(j0, 2 * m + 1)
                        dve.wait_ge(acc_full[p], u + e * 10 + 1)
                        dve.tensor_tensor(two(hm[:, m % 3, :]), two(sg[:, m % 2, :]), pair(p), ALU.mult
                                          ).then_inc(acc_free[p], 1)
                        dve.wait_ge(sem("hidh_made"), upto("hidh_made", l, e * FE + m + 1))
                        dve.tensor_tensor(hidl[:, m, :], hm[:, m % 3, :], hidh[:, m, :].bitcast(F32), ALU.subtract
                                          ).then_inc(sem("hid_made"), 1)
                    for k in range(FE):
                        split_low(s0, 2 * FE + k, e * FE)
                        for m in range(KT):
                            if (m * FE + FE - 1) // KT == k:
                                p, u = psj(j0, 2 * FE + m)
                                dve.wait_ge(acc_full[p], u + e * 10 + 1)
                                add_residual(l, p, m, 1, e * KT + upto("xs_made", l, KT + m + 1))


def slabs(inputs):
    def blocks(w, ms, kn):
        K, M = w.shape
        return w.reshape(K // P, P, M // P, P).transpose(2, 1, 0, 3).reshape(M // P, P, K)

    out = []
    for l in range(L):
        out.append(blocks(inputs["ada_w"][l], None, None))
    for l in range(L):
        w = inputs["w_in"][l]
        q = w[:, 0:512].reshape(D, 2, 4, HD).transpose(0, 2, 1, 3).reshape(D, 512)
        ga = np.zeros((D, P), np.float32)
        ga[:, 0:RANK] = w[:, 1792:1808]
        out.append(blocks(ga, None, None))
        out.append(blocks(q, None, None))
        out.append(blocks(w[:, 512:1792], None, None))
        out.append(blocks(w[:, 1808:4368], None, None))
        wa_ = inputs["w_branch_a"][l].reshape(2, 4, HD, D).transpose(1, 0, 2, 3).reshape(512, D)
        pa = blocks(wa_, None, None)
        pb = blocks(inputs["w_branch_b"][l], None, None)
        for mp in range(4):
            for w4 in (pa, pb):
                out.append(np.concatenate([w4[2 * mp], w4[2 * mp + 1]], axis=1)[None])
        out.append(blocks(inputs["w_out"][l], None, None))
        if l == 0:
            hw = FE * P
            ex = [(inputs["ffn_w_gate"][0][:, e * hw:e * hw + hw], inputs["ffn_w_up"][0][:, e * hw:e * hw + hw],
                   inputs["ffn_w_down"][0][e * hw:e * hw + hw]) for e in range(2)]
        else:
            ex = [(inputs["moe_w_gate"][0, e], inputs["moe_w_up"][0, e], inputs["moe_w_down"][0, e]) for e in range(E)]
        for wg, wu, wd in ex:
            out.append(np.stack([blocks(wg, None, None), blocks(wu, None, None)], axis=1).reshape(2 * FE, P, D))
            d = blocks(wd, None, None).reshape(KT, P, FE, P).transpose(0, 2, 1, 3).reshape(FE, KT, P, P)
            out.append(d.transpose(0, 2, 1, 3).reshape(FE, P, D))
    out.append(np.zeros((LEAD, P, D), np.float32))
    return np.concatenate(out, axis=0)


def constants():
    c = np.zeros((P, C_END), np.float32)
    i = np.arange(P)
    c[:, C_ID:C_ID + P] = np.eye(P)
    c[:, C_ONE:C_ONE + P] = 1.0
    c[:, C_BLK:C_BLK + P] = (i[:, None] // HD) == (i[None] // HD)
    c[:, C_U:C_U + P] = (i[:, None] <= i[None]) / 16.0
    c[:, C_M:C_M + P] = i[:, None] <= i[None]
    slope = 2.0 ** -(np.arange(1, NH + 1, dtype=np.float64))
    dist = P + i[:, None] - np.arange(2 * P)[None]
    ok = (dist >= 0) & (dist <= P)
    c[:, C_BIAS:C_BIAS + NH * 2 * P] = np.where(ok[:, None], -slope[None, :, None] * dist[:, None], -1.0e30).reshape(P, -1)
    c[0:NH, C_BS:C_BS + 129] = -slope[:, None] * (P - np.arange(129))[None]
    c[:, C_RANK:C_RANK + E] = E - np.arange(E)
    return c


def kernel(**inputs):
    import concourse.bacc as bacc
    from concourse.bass_utils import run_bass_kernel_spmd as run

    v = {k: np.asarray(a) for k, a in inputs.items()}

    def feat(a):
        return a.T.reshape(-1, P, a.shape[0]).transpose(1, 0, 2)

    small = np.concatenate(
        [v["ada_b"][l].reshape(ADA, P).T for l in range(L)]
        + [v[n][l].reshape(KT, P).T for l in range(L) for n in ("norm1_g", "norm2_g")]
        + [np.concatenate([v[n][l], v[n][l]])[:, None] for l in range(L) for n in ("q_norm_g", "k_norm_g")]
        + [v["gla_norm_g"][l][:, None] for l in range(L)]
        + [np.broadcast_to(v["attn_sinks"].reshape(1, L * NH), (P, L * NH))]
        + [np.concatenate([v["attn_sinks"].T, np.zeros((P - NH, L), np.float32)], axis=0)]
        + [v["router_w"][0].reshape(KT, P, E).transpose(1, 0, 2).reshape(P, KT * E)]
        + [np.broadcast_to(v["router_b"], (P, E))], axis=1)
    arrays = {
        "xT": feat(np.concatenate([v["x_prompt"][0], v["x_sample"][:, 0]], axis=0)),
        "cT": feat(np.concatenate([v["c_prompt"], v["c_sample"]], axis=0)),
        "weights": slabs(v),
        "constants": constants(),
        "small": small,
        "wa2": np.concatenate([v["gla_wa2"].transpose(1, 0, 2), np.zeros((BROW - RANK, L, 256), np.float32),
                               v["gla_ba"][None]], axis=0),
        "k_cache": v["cache_k"].transpose(0, 3, 4, 1, 2).reshape(L, P, NS, P),
        "v_cache": v["cache_v"].transpose(0, 2, 1, 3, 4).reshape(L, P, NS, P),
        "state": v["state_gla"].reshape(L, NS, 2, 2, GK, GV).transpose(0, 3, 4, 1, 2, 5).reshape(L, P, NS, 2, GV),
    }
    arrays = {k: np.ascontiguousarray(a) for k, a in arrays.items()}
    outs = {"yT": (P, KT, N), "kp": (L, P, P), "vp": (L, P, P), "sp": (L, P, 2, GV), "ks": (L, P, NS, P),
            "vs": (L, P, NS, P), "ss": (L, P, NS, 2, GV)}
    nc = bacc.Bacc("TRN2", target_bir_lowering=False, num_devices=1)
    args = [nc.dram_tensor(k, a.shape, mybir.dt.from_np(a.dtype), kind="ExternalInput").ap() for k, a in arrays.items()]
    args += [nc.dram_tensor(k, s, F32, kind="ExternalOutput").ap() for k, s in outs.items()]
    build(nc, *args)
    r = run(nc, [arrays], core_ids=[0]).results[0]
    y = r["yT"].transpose(2, 1, 0).reshape(N, D)

    def token_rows(a):
        return a.transpose(0, 2, 1).reshape(L, 1, P, NKV, HD)

    return (y[None, 0:T], y[T:N, None],
            token_rows(r["kp"]), token_rows(r["vp"]),
            r["sp"].reshape(L, 2, GK, 2, GV).transpose(0, 3, 1, 2, 4).reshape(L, 1, GH, GK, GV),
            r["ks"].transpose(0, 2, 3, 1).reshape(L, NS, P, NKV, HD),
            r["vs"].transpose(0, 2, 1, 3).reshape(L, NS, P, NKV, HD),
            r["ss"].reshape(L, 2, GK, NS, 2, GV).transpose(0, 3, 4, 1, 2, 5).reshape(L, NS, GH, GK, GV))
```

```python
from contextlib import ExitStack

import numpy as np

import concourse.bass as bass
from concourse import mybir

F32 = mybir.dt.float32
F32R = mybir.dt.float32r
I32 = mybir.dt.int32
ACT = mybir.ActivationFunctionType
ALU = mybir.AluOpType
AX = mybir.AxisListType.X

P = 128
D = 1024
KT = D // P
T = 512
NS = 8
N = T + NS
HN = N // 2
L = 2
NB = T // P
NH, NKV, HD = 8, 2, 64
GH, GK, GV = 4, 64, 128
RANK = 16
BROW = 32
E = 8
FE = 11
SUB = 32
NI = P // SUB
EPS = 1e-6
SLOTS = 3
PAIRS = 3
ADA = 6 * KT
W1 = 15
W3 = 20
Z_GA, Z_Q, Z_K, Z_V, Z_GQ, Z_GK, Z_GV = 0, 1, 5, 6, 7, 9, 11
EXP_SLABS = 3 * FE
CAP = 224
CT = CAP // 2
ITEM_JOBS = 1 + FE + 2 + KT + KT
RING = 11
LAYER_SLABS = [W1 + W3 + 8 + 8 + 2 * EXP_SLABS, W1 + W3 + 8 + 8 + E * EXP_SLABS]
TOTAL = L * ADA + sum(LAYER_SLABS)
LEAD = 2

C_ID, C_ONE, C_BLK, C_U, C_M, C_BIAS, C_BS, C_RANK, C_SLOT = 0, 128, 256, 384, 512, 640, 2688, 2824, 2832
C_END = C_SLOT + CAP
S_ADAB = 0
S_N = S_ADAB + L * ADA
S_QK = S_N + L * 2 * KT
S_GN = S_QK + L * 2
S_SINK = S_GN + L
S_SINKC = S_SINK + L * NH
S_RW = S_SINKC + L
S_RB = S_RW + KT * E
S_END = S_RB + E


def build(nc, xT, cT, wst, cst, sml, wa2, kcT, vc, st, yT, kp, vp, sp_, ks, vs, ss):
    ctx = ExitStack()
    with ctx:
        sems = {}
        def sem(name):
            if name not in sems:
                sems[name] = ctx.enter_context(nc.semaphore(name))
            return sems[name]

        pos = [(nc.sbuf_base + 31) // 32 * 32]

        def at(name, shape, dt, offset):
            return nc.alloc_sbuf_tensor_at(name, shape, dt, offset=offset)

        def fixed(name, shape, dt=F32):
            t = at(name, shape, dt, pos[0])
            n = 4 * int(np.prod(shape[1:]))
            pos[0] += (n + 31) // 32 * 32
            return t

        x = fixed("x", [P, KT, N])
        H0 = pos[0]
        Hh = fixed("Hh", [P, KT, N], F32R)
        Hl = fixed("Hl", [P, KT, N], F32R)
        raw = fixed("raw", [P, SLOTS, 1024])
        wh = fixed("wh", [P, SLOTS, 1024], F32R)
        wl = fixed("wl", [P, SLOTS, 1024], F32R)
        B0 = pos[0]
        Bh = fixed("Bh", [P, 8, N], F32R)
        Bl = fixed("Bl", [P, 8, N], F32R)
        Z0 = pos[0]
        z = fixed("z", [P, W1, N])
        G0 = pos[0]
        g = fixed("g", [P, W3, N])
        cs = fixed("cs", [P, C_END])
        sm = fixed("sm", [P, S_END])
        wa = fixed("wa", [BROW + 1, L, 256])
        mod = fixed("mod", [P, L, ADA, 9])
        eps = fixed("eps", [P, 1])
        qg8 = fixed("qg8", [P, L])
        osmp = fixed("osmp", [P, GH, NS])
        xs_tmp = fixed("xs_tmp", [P, 2, NS])
        mx = fixed("mx", [P, NH]); nmx = fixed("nmx", [P, NH]); sk = fixed("sk", [P, NH])
        esk = fixed("esk", [P, NH]); rs = fixed("rs", [P, NH]); den = fixed("den", [P, NH])
        rec = fixed("rec", [P, NH])
        assert pos[0] <= nc.sbuf_usable_end, pos[0]

        c_in = at("c_in", [P, KT, 9], F32, G0)
        c_act = at("c_act", [P, KT, 9], F32, G0 + 288)
        sq = at("sq", [P, KT, N], F32, Z0)
        rt = at("rt", [P, N], F32, Z0 + 16640)
        ri = at("ri", [P, N], F32, Z0 + 18720)
        tn = at("tn", [P, KT, N], F32, G0)
        hf = at("hf", [P, KT, N], F32, G0 + 16640)
        hidh = at("hidh", [P, FE, N], F32R, Z0)
        hidl = at("hidl", [P, FE, N], F32R, Z0 + 22880)
        sg = at("sg", [P, 2, N], F32, Z0 + 45760)
        hm = at("hm", [P, 3, N], F32, Z0 + 49920)
        XE = at("XE", [P, 2, KT, CAP], F32R, H0)
        ST = at("ST", [P, 2, N], F32R, H0 + 14336)
        Sel = at("Sel", [P, NB + 1, CAP], F32R, H0 + 18496)
        sgm = at("sgm", [P, 3, CAP], F32, H0 + 22976)
        hmm = at("hmm", [P, 3, CAP], F32, H0 + 25664)
        slotw = at("slotw", [P, 2], F32, H0 + 28352)
        slotpos = at("slotpos", [P, NB + 1, E + 1], F32, H0 + 28384)
        chosen = at("chosen", [P, NB + 1, E], F32, H0 + 28576)
        sweeps = at("sweeps", [P, 1], I32, H0 + 28736)
        cnt = [at(f"cnt{i}", [P, 1], F32, H0 + 28768 + 32 * i) for i in range(4)]
        more = at("more", [P, RING - SLOTS, 1024], F32, B0)
        hTh = at("hTh", [P, NB + 1, D], F32R, Z0)
        hTl = at("hTl", [P, NB + 1, D], F32R, Z0 + 20480)
        heh = at("heh", [P, FE, CAP], F32R, Z0 + 40960)
        hel = at("hel", [P, FE, CAP], F32R, Z0 + 50816)
        Yh = at("Yh", [P, 2, D], F32R, Z0 + 40960)
        Yl = at("Yl", [P, 2, D], F32R, Z0 + 49152)
        lg = at("lg", [P, 5, E], F32, Z0 + 65536)
        rr = [at(f"rr{i}", [P, 5, E], F32, Z0 + 65536 + 160 * (i + 1)) for i in range(8)]
        r1 = [at(f"r1{i}", [P, 5, 1], F32, Z0 + 65536 + 1440 + 32 * i) for i in range(10)]
        qsq = at("qsq", [P, 5, N], F32, G0)
        qrt = at("qrt", [P, 5, N], F32, G0 + 10400)
        sc = at("sc", [P, NH, 256], F32, G0)
        PT = at("PT", [P, 4, 512], F32, G0 + 8192)
        vtok = at("vtok", [P, NB, P], F32, G0 + 16384)
        kc = at("kc", [P, NS, 129], F32, G0 + 20800)
        vcs = at("vcs", [P, NS, P], F32, G0 + 24928)
        Sst = at("Sst", [P, NS, 2, GV], F32, G0 + 29024)
        scs = at("scs", [NS, NS, 129], F32, G0 + 37216)
        qs = at("qs", [P, NS, NH], F32, G0)
        pT = at("pT", [P, NS, NH], F32, G0 + 256)
        prow = at("prow", [1, NS, NH], F32, G0 + 512)
        vrow = at("vrow", [1, NS, P], F32, G0 + 768)
        smx = at("smx", [NS, NS], F32, G0 + 4864)
        sts = at("sts", [NS, NS], F32, G0 + 4896)
        ses = at("ses", [NS, NS], F32, G0 + 4928)
        srs = at("srs", [NS, NS], F32, G0 + 4960)
        sdn = at("sdn", [NS, NS], F32, G0 + 4992)
        srec = at("srec", [NS, NS], F32, G0 + 5024)
        kts = at("kts", [NS, 256], F32, G0 + 5120)
        vts = at("vts", [NS, 512], F32, G0 + 6144)
        kms = at("kms", [NS, NS, 256], F32, G0 + 8192)
        las = at("las", [NS, 256], F32, G0 + 16384)
        lab = at("lab", [NS, 256], F32, G0 + 17408)
        lac = at("lac", [NS, 256], F32, G0 + 18432)
        dcs = at("dcs", [P, 2, NS], F32, G0 + 19456)
        la = at("la", [P, NB, 256], F32, Z0 + 2080)
        lt = at("lt", [P, NB, 256], F32, Z0 + 2080 + 4096)
        cum = at("cum", [P, 2, T], F32, G0)
        qt = at("qt", [P, 2, T], F32, G0 + 4096)
        qe = at("qe", [P, 2, T], F32, G0 + 8192)
        KW = SUB * NI * (NI + 1) // 2
        kt = at("kt", [P, 2, NB, KW], F32, G0 + 12288)
        kd = at("kd", [P, 2, T], F32, G0 + 22528)
        kdt = at("kdt", [P, NB, 256], F32, G0 + 26624)
        att = at("att", [P, NB, GH, P], F32, G0 + 30720)
        dec = at("dec", [P, 2, NB], F32, G0 + 38912)
        gvt = at("gvt", [P, NB, 512], F32, B0 + 8320)
        S = at("S", [P, NB, 2, 2, GV], F32, B0 + 16640 + 8320)
        ta = at("ta", [P, 2, N], F32, Z0 + 27040)
        mf = at("mf", [P, KT, N], F32, Z0 + 10400)

        ident = cs[:, C_ID:C_ID + P]
        ones = cs[:, C_ONE:C_ONE + P]
        blk = cs[:, C_BLK:C_BLK + P]
        U16 = cs[:, C_U:C_U + P]
        MSK = cs[:, C_M:C_M + P]
        biasT = cs[:, C_BIAS:C_BIAS + 2048].rearrange("p (h s) -> p h s", h=NH)
        biasS = cs[0:NS, C_BS:C_BS + 129]
        rank8 = cs[:, C_RANK:C_RANK + E]
        slot_ids = cs[:, C_SLOT:C_SLOT + CAP]

        ps = ctx.enter_context(nc.psum_tensor("ps", [P, 8, 512], F32))

        def pair(p):
            return ps[:, 2 * p:2 * p + 2, 0:HN]

        def two(ap):
            return ap.rearrange("p (a b) -> p a b", a=2)

        base = {}
        jobs = {}
        njobs = {}
        s = L * ADA
        j = 0
        for l in range(L):
            ne = 2 if l == 0 else E
            for name, ns_, nj in (("n1", 0, 1), ("w1", W1, W1), ("qk", 0, 5), ("w3", W3, W3), ("gn", 0, 4),
                                  ("br", 8, 16), ("wo", 8, 8), ("n2", 0, 1), ("ht", 0, NB + 1 if l else 0),
                                  ("xe", 0, KT if l else 0), ("ff", ne * EXP_SLABS, ne * 30)):
                base[name, l] = s
                jobs[name, l] = j
                njobs[name, l] = nj
                s += ns_
                j += nj
        assert s == TOTAL

        def slot(s0, k, i=0):
            return (s0 + k) % SLOTS, (s0 + k) // SLOTS + i

        def r_use(s0, k, i=0):
            return (s0 - L * ADA + k) // SLOTS + i

        def psj(j0, k, i=0):
            return (j0 + k) % PAIRS, (j0 + k) // PAIRS + i

        def products_read(eng, name, l):
            end = jobs[name, l] + njobs[name, l]
            for p in range(PAIRS):
                if (end - p + 2) // PAIRS:
                    eng.wait_ge(acc_free[p], (end - p + 2) // PAIRS)

        raw_full = [sem(f"raw_full{i}") for i in range(SLOTS)]
        ada_used = [sem(f"ada_used{i}") for i in range(SLOTS)]
        hi_made = [sem(f"hi_made{i}") for i in range(SLOTS)]
        split_made = [sem(f"split_made{i}") for i in range(SLOTS)]
        split_used = [sem(f"split_used{i}") for i in range(SLOTS)]
        acc_full = [sem(f"acc_full{i}") for i in range(PAIRS)]
        acc_free = [sem(f"acc_free{i}") for i in range(PAIRS)]


        more_full = [sem(f"more_full{i}") for i in range(RING)]

        def ring(f):
            return raw[:, f, :] if f < SLOTS else more[:, f - SLOTS, :]

        PER_LAYER = dict(sq_made=2 * KT, tn_made=2 * KT, hf_made=2 * KT, hfs_made=2, Hh_made=2 * KT, H_made=2 * KT,
                         qsq_made=5, qk_made=5, kc_in=16, vc_in=16, st_in=16, cache_out=6 * 16, S_out=2 * 16,
                         sc_done=NB, soft_in=NB, exp_done=NB, p_made=NB, pt_done=NB, pta_copied=NB, ptb_copied=NB,
                         av_done=NB, avh_made=NB, av_read=NB, pT_made=2, dah_made=2, gvt_made=2, S_made=NB,
                         osq_made=GH, og_made=GH, Bh_made=GH, B_made=GH, mf_made=KT, Mh_made=KT, M_made=KT,
                         xs_made=3 * KT, hidh_made=2 * FE, hid_made=2 * FE,
                         rl_done=0, rt_exp_in=0, rt_exp=0)

        def upto(name, l, n):
            return n + l * PER_LAYER.get(name, 1)

        block = ctx.enter_context(nc.Block())

        @block.sync
        def _(sp):
            def slab(idx, j):
                sp.dma_start(raw[:, j, :], wst[idx, :, :]).then_inc(raw_full[j], 16)

            for j in range(SLOTS):
                slab(j, j)
            with sp.Fori(1, L * ADA // SLOTS) as i:
                for j in range(SLOTS):
                    sp.wait_ge(ada_used[j], i)
                    slab(i * SLOTS + j, j)
            n0 = L * ADA // SLOTS
            for j in range(SLOTS):
                sp.wait_ge(ada_used[j], n0)
                slab(L * ADA + j, j)
            ff = base["ff", L - 1]
            nr = (ff - L * ADA) // SLOTS
            with sp.Fori(1, nr) as i:
                for j in range(SLOTS):
                    sp.wait_ge(split_made[j], i)
                    slab((i + n0) * SLOTS + j, j)
            for j in range(LEAD):
                sp.wait_ge(split_made[j], nr)
                slab(ff + j, j)

            def expert_slab(e, k):
                sp.dma_start(ring(k % RING), wst[ff + LEAD + EXP_SLABS * e + k, :, :]).then_inc(more_full[k % RING], 16)

            def slot_split(k, i):
                sp.wait_ge(split_made[(k - RING + LEAD) % SLOTS], r_use(ff, k - RING + LEAD, i * FE) + 1)

            sp.wait_ge(sem("ring_open"), 1)
            for k in range(RING):
                expert_slab(0, k)
            for k in range(RING, EXP_SLABS):
                slot_split(k, 0)
                expert_slab(0, k)
            sp.wait_ge(sem("sweeps_made"), 1)
            n_sweeps = sp.value_load(sweeps[0:1, 0:1], min_val=1, max_val=3)
            with sp.Fori(1, n_sweeps * E) as i:
                for k in range(EXP_SLABS):
                    slot_split(k, i)
                    expert_slab(i % E, k)

        @block.gpsimd
        def _(pool):
            pool.dma_start(x[:], xT).then_inc(sem("x_in"), 16)
            pool.dma_start(c_in[:], cT).then_inc(sem("c_landed"), 16)
            pool.dma_start(sm[:], sml).then_inc(sem("small_in"), 16)
            pool.dma_start(cs[:], cst).then_inc(sem("const_in"), 16)
            pool.dma_start(wa[:], wa2).then_inc(sem("wa_in"), 16)
            outs = 0
            for l in range(L):
                pool.wait_ge(sem("Hh_made"), upto("Hh_made", l, KT))
                pool.wait_ge(sem("H_made"), upto("H_made", l, KT))
                pool.dma_start(kc[:, :, 0:P], kcT[l]).then_inc(sem("kc_in"), 16)
                pool.dma_start(vcs[:], vc[l]).then_inc(sem("vc_in"), 16)
                pool.dma_start(Sst[:], st[l]).then_inc(sem("st_in"), 16)
                pool.wait_ge(sem("qk_made"), upto("qk_made", l, 5))
                pool.dma_start(kp[l], z[:, Z_K, T - P:T]).then_inc(sem("cache_out"), 16)
                products_read(pool, "w1", l)
                pool.dma_start(vp[l], z[:, Z_V, T - P:T]).then_inc(sem("cache_out"), 16)
                pool.wait_ge(sem("kc_made"), upto("kc_made", l, 1))
                pool.dma_start(ks[l], kc[:, :, 1:1 + P]).then_inc(sem("cache_out"), 16)
                pool.wait_ge(sem("vc_in"), upto("vc_in", l, 16))
                pool.dma_start(vs[l, 0:P - 1], vcs[1:P, :, :]).then_inc(sem("cache_out"), 16)
                pool.wait_ge(sem("vrow_made"), upto("vrow_made", l, 1))
                pool.dma_start(vs[l, P - 1:P], vrow[:]).then_inc(sem("cache_out"), 16)
                pool.wait_ge(sem("Sst_made"), upto("Sst_made", l, 1))
                pool.dma_start(ss[l], Sst[:]).then_inc(sem("cache_out"), 16)
                pool.wait_ge(sem("S_made"), upto("S_made", l, NB))
                for r in range(2):
                    hp = slice(64 * r, 64 * r + 64)
                    pool.dma_start(sp_[l, hp], S[hp, NB - 1, :, r, :]).then_inc(sem("S_out"), 16)
            pool.wait_ge(sem("x_final"), 1)
            pool.dma_start(yT, x[:]).then_inc(sem("y_out"), 16)
            for l in range(L):
                pool.wait_ge(sem("cache_out"), upto("cache_out", l, 6 * 16))
                pool.wait_ge(sem("S_out"), upto("S_out", l, 32))
            pool.wait_ge(sem("y_out"), 16)

        @block.tensor
        def _(pe):
            def blocks(todo):
                for sl, b, xh, xl, p, first, last, s_first, s_last in todo:
                    w_h, w_l = wh[:, sl, b * P:b * P + P], wl[:, sl, b * P:b * P + P]
                    for h in range(2):
                        out = ps[:, 2 * p + h, 0:HN]
                        cols = slice(h * HN, h * HN + HN)
                        for q, (w, v) in enumerate(((w_h, xh), (w_h, xl), (w_l, xh))):
                            mm = pe.matmul(out, w, v[:, cols], start=first and q == 0, stop=last and q == 2)
                            if h == 0 and q == 0 and s_first is not None:
                                mm.then_inc(s_first, 1)
                    if last and s_last is not None:
                        mm.then_inc(s_last, 1)

            def slab_ready(s0, k, i):
                sl, _ = slot(s0, k)
                pe.wait_ge(split_made[sl], r_use(s0, k, i) + 1)
                return sl, split_used[(sl - 1) % SLOTS]

            def free_pair(j0, k, i=0):
                p, u = psj(j0, k, i)
                if not (isinstance(u, int) and u == 0):
                    pe.wait_ge(acc_free[p], u)
                return p

            def product8(s0, j0, k, i, xh, xl):
                sl, before = slab_ready(s0, k, i)
                p = free_pair(j0, k, i)
                blocks([(sl, b, xh[:, b, :], xl[:, b, :], p, b == 0, b == KT - 1, before if b == 0 else None, acc_full[p])
                        for b in range(KT)])

            def products8(name, l, n, xh, xl):
                s0, j0 = base[name, l], jobs[name, l]
                peel = 1 if j0 < PAIRS else 0
                for k in range(3 * peel):
                    product8(s0, j0, k, 0, xh, xl)
                with pe.Fori(peel, n // 3) as i:
                    for j in range(3):
                        product8(s0, j0, j, i, xh, xl)
                for k in range(n // 3 * 3, n):
                    product8(s0, j0, k, 0, xh, xl)

            def plain(out_pair, lhsT, rhs, first, last):
                for h in range(2):
                    mm = pe.matmul(ps[0:lhsT.shape[1], 2 * out_pair + h, 0:HN], lhsT, rhs[:, h * HN:h * HN + HN],
                                   start=first, stop=last)
                return mm

            def block_rows(n):
                return P if n < NB else NS

            def gather(job0, i, number):
                pe.wait_ge(sem("Sel_made"), number)
                for m in range(KT):
                    p, u = psj(job0, m)
                    pe.wait_ge(acc_free[p], u + i * (ITEM_JOBS // PAIRS))
                    for q, part in enumerate((hTh, hTl)):
                        for n in range(NB + 1):
                            rows = block_rows(n)
                            mm = pe.matmul(ps[:, 2 * p + q, 0:CAP], part[0:rows, n, m * P:m * P + P], Sel[0:rows, n, :],
                                           start=n == 0, stop=n == NB)
                    mm.then_inc(acc_full[p], 1)

            def experts(l):
                def to_tokens(n):
                    rows = block_rows(n)
                    p = free_pair(jobs["ht", l], n)
                    for k in range(KT):
                        mm = pe.transpose(ps[0:rows, 2 * p + k // 4, (k % 4) * P:(k % 4) * P + P],
                                          hf[:, k, n * P:n * P + rows], ident)
                    mm.then_inc(acc_full[p], 1)

                for n in range(PAIRS):
                    to_tokens(n)
                pe.wait_ge(sem("chosen_made"), 1)
                for n in range(NB + 1):
                    rows = block_rows(n)
                    for b in range(n):
                        pe.matmul(ps[0:rows, 7, n * E:n * E + E], ones[:, 0:rows], chosen[:, b, :], start=b == 0, stop=False)
                    pe.matmul(ps[0:rows, 7, n * E:n * E + E], MSK[0:rows, 0:rows], chosen[0:rows, n, :], start=n == 0, stop=True)
                for n in range(NB + 1):
                    rows = block_rows(n)
                    mm = pe.matmul(ps[:, 7, (NB + 1) * E:(NB + 2) * E], ones[0:rows, :], chosen[0:rows, n, :],
                                   start=n == 0, stop=n == NB)
                mm.then_inc(sem("rank_done"), 1)
                for n in range(PAIRS, NB + 1):
                    to_tokens(n)
                products_read(pe, "ht", l)
                gather(jobs["xe", l], 0, 1)
                products_read(pe, "xe", l)
                pe.wait_ge(sem("sweeps_made"), 1)
                n_sweeps = pe.value_load(sweeps[0:1, 0:1], min_val=1, max_val=3)
                s0, j0 = base["ff", l], jobs["ff", l]
                per_pair = ITEM_JOBS // PAIRS
                with pe.Fori(0, n_sweeps) as c, pe.Fori(0, E) as e:
                    i = c * E + e

                    def open_pair(k):
                        p, u = psj(j0, k)
                        pe.wait_ge(acc_free[p], u + i * per_pair)
                        return p

                    p = open_pair(0)
                    for t in range(2):
                        cols = slice(t * CT, t * CT + CT)
                        for n in range(NB + 1):
                            rows = block_rows(n)
                            pe.matmul(ps[0:CT, 7, t:t + 1], Sel[0:rows, n, cols].bitcast(F32),
                                      rr[7][0:rows, n, bass.ds(e, 1)], start=n == 0, stop=n == NB)
                        pe.transpose(ps[0:CT, 6, t * NS:t * NS + NS], Sel[0:NS, NB, cols].bitcast(F32), ident[0:NS, 0:NS])
                    for t in range(2):
                        for n in range(NB):
                            mm = pe.transpose(ps[0:CT, 2 * p + t, n * P:n * P + P],
                                              Sel[:, n, t * CT:t * CT + CT].bitcast(F32), ident)
                    mm.then_inc(acc_full[p], 1)
                    for m in range(FE):
                        p = open_pair(1 + m)
                        for q in range(2):
                            sl, before = slab_ready(s0, 2 * m + q, i * FE)
                            for b in range(KT):
                                for r, (w, v) in enumerate(((wh, 0), (wh, 1), (wl, 0))):
                                    mm = pe.matmul(ps[:, 2 * p + q, 0:CAP], w[:, sl, b * P:b * P + P], XE[:, v, b, :],
                                                   start=b == 0 and r == 0, stop=b == KT - 1 and r == 2)
                                    if b == 0 and r == 0:
                                        mm.then_inc(before, 1)
                        mm.then_inc(acc_full[p], 1)
                    p2 = [open_pair(1 + FE + t) for t in range(2)]
                    for k in range(FE):
                        pe.wait_ge(sem("hid_made"), upto("hid_made", l, i * FE + k + 1))
                        sl, before = slab_ready(s0, 2 * FE + k, i * FE)
                        for t in range(2):
                            for q in range(2):
                                for r, (v, w) in enumerate(((heh, wh), (heh, wl), (hel, wh))):
                                    mm = pe.matmul(ps[0:CT, 2 * p2[t] + q, :], v[:, k, t * CT:t * CT + CT],
                                                   w[:, sl, q * 512:q * 512 + 512], start=k == 0 and r == 0,
                                                   stop=k == FE - 1 and r == 2)
                                    if t == 0 and q == 0 and r == 0:
                                        mm.then_inc(before, 1)
                            if k == FE - 1:
                                mm.then_inc(acc_full[p2[t]], 1)
                    gather(j0 + 3 + FE, i, i + 2)
                    for m in range(KT):
                        p = open_pair(3 + FE + KT + m)
                        for h in range(2):
                            for t in range(2):
                                for r, v in enumerate((Yh, Yl)):
                                    mm = pe.matmul(ps[:, 2 * p + h, 0:HN], v[0:CT, t, m * P:m * P + P],
                                                   ST[0:CT, t, h * HN:h * HN + HN], start=t == 0 and r == 0,
                                                   stop=t == 1 and r == 1)
                        mm.then_inc(acc_full[p], 1)

            pe.wait_ge(sem("c_made"), 1)
            for l in range(L):
                with pe.Fori(0, ADA // SLOTS) as i:
                    for j in range(SLOTS):
                        pe.wait_ge(raw_full[j], 16 * i + 16 * (l * ADA // SLOTS + 1))
                        for b in range(KT):
                            mm = pe.matmul(ps[:, 6 + l, bass.ds(27 * i + 9 * j, 9)], raw[:, j, b * P:b * P + P],
                                           c_act[:, b, :], start=b == 0, stop=b == KT - 1)
                        mm.then_inc(ada_used[j], 1)

            pe.wait_ge(sem("const_in"), 16)
            for l in range(L):
                def norm_sum(name, which):
                    j0 = jobs[name, l]
                    p = free_pair(j0, 0)
                    for k in range(KT):
                        pe.wait_ge(sem("sq_made"), upto("sq_made", l, which * KT + k + 1))
                        mm = plain(p, ones, sq[:, k, :], k == 0, k == KT - 1)
                    mm.then_inc(acc_full[p], 1)

                norm_sum("n1", 0)
                pe.wait_ge(sem("H_made"), upto("H_made", l, KT))
                products8("w1", l, W1, Hh, Hl)
                for i in range(5):
                    p = free_pair(jobs["qk", l], i)
                    pe.wait_ge(sem("qsq_made"), upto("qsq_made", l, i + 1))
                    plain(p, blk, qsq[:, i, :], True, True).then_inc(acc_full[p], 1)
                products_read(pe, "w1", l)
                pe.wait_ge(sem("mod_made"), 2 * L)
                for n in range(NB):
                    mm = pe.transpose(ps[:, 6, n * P:n * P + P], z[:, Z_V, n * P:n * P + P], ident)
                mm.then_inc(sem("vt_done"), 1)
                pe.wait_ge(sem("qk_made"), upto("qk_made", l, 5))
                for n in range(NB):
                    W = 2 * P if n else P
                    if n:
                        pe.wait_ge(sem("av_read"), upto("av_read", l, n))
                    for kv in range(NKV):
                        hp = slice(64 * kv, 64 * kv + 64)
                        for t in range(4):
                            mm = pe.matmul(ps[:, 2 * kv + t // 2, (t % 2) * 256:(t % 2) * 256 + W],
                                           z[hp, Z_Q + t, n * P:n * P + P], z[hp, Z_K, (n + 1) * P - W:(n + 1) * P],
                                           start=True, stop=True)
                    mm.then_inc(sem("sc_done"), 1)
                    pe.wait_ge(sem("p_made"), upto("p_made", l, n + 1))
                    if n == 0:
                        pe.wait_ge(sem("vtok_made"), upto("vtok_made", l, 1))
                    else:
                        pe.wait_ge(sem("pta_copied"), upto("pta_copied", l, n))
                        pe.wait_ge(sem("ptb_copied"), upto("ptb_copied", l, n))
                    for c in range(2 if n else 1):
                        for h in range(NH):
                            mm = pe.transpose(ps[:, 4 + 2 * c + h // 4, (h % 4) * P:(h % 4) * P + P],
                                              sc[:, h, c * P:c * P + P], ident)
                    mm.then_inc(sem("pt_done"), 1)
                    pe.wait_ge(sem("pta_copied"), upto("pta_copied", l, n + 1))
                    pe.wait_ge(sem("ptb_copied"), upto("ptb_copied", l, n + 1))
                    nc_ = 2 if n else 1
                    for kv in range(NKV):
                        for c in range(nc_):
                            mm = pe.matmul(ps[64 * kv:64 * kv + 64, 0, :], vtok[:, n - (nc_ - 1) + c, 64 * kv:64 * kv + 64],
                                           PT[:, 2 * c + kv, :], start=c == 0, stop=c == nc_ - 1)
                    mm.then_inc(sem("av_done"), 1)
                pe.wait_ge(sem("av_read"), upto("av_read", l, NB))
                pe.wait_ge(sem("qs_made"), upto("qs_made", l, 1))
                pe.wait_ge(sem("kc_made"), upto("kc_made", l, 1))
                for b in range(NS):
                    mm = pe.matmul(ps[0:NS, b // 2, (b % 2) * 256:(b % 2) * 256 + 129], qs[:, b, :], kc[:, b, :],
                                   start=True, stop=True)
                mm.then_inc(sem("dsc_done"), 1)
                pe.wait_ge(sem("dp_made"), upto("dp_made", l, 1))
                for b in range(NS):
                    pe.transpose(ps[:, 4, b * NH:b * NH + NH], scs[:, b, 0:P], ident[0:NS, 0:NS])
                for b in range(NS):
                    pe.matmul(ps[0:1, 5, b * NH:b * NH + NH], scs[:, b, P:P + 1], ident[0:NS, 0:NS], start=True, stop=True)
                for b in range(NS):
                    mm = pe.matmul(ps[0:1, 6 + b // 4, (b % 4) * P:(b % 4) * P + P], z[:, Z_V, T + b:T + b + 1], ident,
                                   start=True, stop=True)
                mm.then_inc(sem("dpt_done"), 1)
                pe.wait_ge(sem("vrow_made"), upto("vrow_made", l, 1))
                pe.wait_ge(sem("pT_made"), upto("pT_made", l, 2))
                pe.wait_ge(sem("vc_in"), upto("vc_in", l, 16))
                for b in range(NS):
                    pe.matmul(ps[:, 0, b * NH:b * NH + NH], vcs[:, b, :], pT[:, b, :], start=True, stop=False)
                    mm = pe.matmul(ps[:, 0, b * NH:b * NH + NH], vrow[0:1, b, :], prow[0:1, b, :], start=False, stop=True)
                mm.then_inc(sem("dav_done"), 1)
                for q in range(2):
                    pe.transpose(ps[0:NS, 4, q * P:q * P + P], z[:, Z_GK + q, T:N], ident)
                for h in range(GH):
                    mm = pe.transpose(ps[0:NS, 5, h * P:h * P + P], z[:, Z_GV + h, T:N], ident)
                mm.then_inc(sem("kvt_done"), 1)
                if l == 0:
                    pe.wait_ge(sem("wa_in"), 16)
                pe.wait_ge(sem("ones_made"), upto("ones_made", l, 1))
                pe.matmul(ps[0:NS, 6, 0:256], z[0:BROW + 1, Z_GA, T:N], wa[:, l, :], start=True, stop=True
                          ).then_inc(sem("dlg_done"), 1)
                pe.wait_ge(sem("las_made"), upto("las_made", l, 1))
                for q in range(2):
                    mm = pe.matmul(ps[:, 7, q * NS:q * NS + NS], las[:, q * P:q * P + P], ident[0:NS, 0:NS],
                                   start=True, stop=True)
                mm.then_inc(sem("dla_done"), 1)
                pe.wait_ge(sem("kms_made"), upto("kms_made", l, 1))
                pe.wait_ge(sem("da_read"), upto("da_read", l, 1))
                for b in range(NS):
                    for h in range(GH):
                        q, r = h // 2, h % 2
                        c0 = (b * 2 + q) * GV
                        mm = pe.matmul(ps[64 * r:64 * r + 64, c0 // 512, c0 % 512:c0 % 512 + GV],
                                       kms[:, b, 64 * h:64 * h + 64], vts[:, h * GV:h * GV + GV], start=True, stop=True)
                mm.then_inc(sem("kv_done"), 1)
                pe.wait_ge(sem("Sst_made"), upto("Sst_made", l, 1))
                for r in range(2):
                    for q in range(2):
                        for b in range(NS):
                            mm = pe.matmul(ps[:, 4 + r, q * NS + b:q * NS + b + 1], Sst[64 * r:64 * r + 64, b, q, :],
                                           z[64 * r:64 * r + 64, Z_GQ + q, T + b:T + b + 1], start=True, stop=True)
                mm.then_inc(sem("do_done"), 1)
                for n in range(NB):
                    mm = pe.matmul(ps[:, n // 2, (n % 2) * 256:(n % 2) * 256 + 256], z[0:BROW + 1, Z_GA, n * P:n * P + P],
                                   wa[:, l, :], start=True, stop=True)
                mm.then_inc(sem("lg_done"), 1)
                pe.wait_ge(sem("la_made"), upto("la_made", l, 1))
                for q in range(2):
                    for n in range(NB):
                        mm = pe.matmul(ps[:, 2 + q, n * P:n * P + P], la[:, n, q * P:q * P + P], U16, start=True, stop=True)
                mm.then_inc(sem("cum_done"), 1)
                pe.wait_ge(sem("osmp_made"), upto("osmp_made", l, 1))
                for n in range(NB):
                    for h in range(GH):
                        mm = pe.transpose(ps[:, 4 + n, h * P:h * P + P], z[:, Z_GV + h, n * P:n * P + P], ident)
                mm.then_inc(sem("gvt_done"), 1)
                pe.wait_ge(sem("kd_made"), upto("kd_made", l, 1))
                for n in range(NB):
                    for q in range(2):
                        mm = pe.transpose(ps[:, n // 2, (n % 2) * 256 + q * P:(n % 2) * 256 + q * P + P],
                                          kd[:, q, n * P:n * P + P], ident)
                mm.then_inc(sem("kdt_done"), 1)
                pe.wait_ge(sem("kdt_made"), upto("kdt_made", l, 1))
                pe.wait_ge(sem("gvt_made"), upto("gvt_made", l, 2))
                for n in range(NB):
                    for h in range(GH):
                        q, r = h // 2, h % 2
                        c0 = (n % 2) * 256 + q * GV
                        mm = pe.matmul(ps[64 * r:64 * r + 64, 2 + n // 2, c0:c0 + GV], kdt[:, n, h * 64:h * 64 + 64],
                                       gvt[:, n, h * GV:h * GV + GV], start=True, stop=True)
                mm.then_inc(sem("ds_done"), 1)
                pe.wait_ge(sem("qt_made"), upto("qt_made", l, 1))
                pe.wait_ge(sem("kt_made"), upto("kt_made", l, 1))
                for n in range(NB):
                    for h in range(GH):
                        q, r = h // 2, h % 2
                        for i in range(NI):
                            rows = SUB * (i + 1)
                            k0 = SUB * i * (i + 1) // 2
                            c0 = (n % 2) * 256 + q * P + SUB * i
                            mm = pe.matmul(ps[0:rows, 4 + 2 * r + n // 2, c0:c0 + SUB],
                                           kt[64 * r:64 * r + 64, q, n, k0:k0 + rows],
                                           qt[64 * r:64 * r + 64, q, n * P + SUB * i:n * P + SUB * i + SUB],
                                           start=True, stop=True)
                mm.then_inc(sem("at_done"), 1)
                pe.wait_ge(sem("att_made"), upto("att_made", l, 1))
                pe.wait_ge(sem("S_made"), upto("S_made", l, NB))
                pe.wait_ge(sem("qe_made"), upto("qe_made", l, 1))
                for n in range(NB):
                    for h in range(GH):
                        q, r = h // 2, h % 2
                        mm = pe.matmul(ps[:, h, n * P:n * P + P], gvt[:, n, h * GV:h * GV + GV], att[:, n, h, :],
                                       start=True, stop=n == 0)
                        if n:
                            mm = pe.matmul(ps[:, h, n * P:n * P + P], S[:, n - 1, q, r, :], qe[:, q, n * P:n * P + P],
                                           start=False, stop=True)
                mm.then_inc(sem("o_done"), 1)
                pe.wait_ge(sem("o_read"), upto("o_read", l, 1))
                products8("w3", l, W3, Hh, Hl)
                for h in range(GH):
                    p = free_pair(jobs["gn", l], h)
                    pe.wait_ge(sem("osq_made"), upto("osq_made", l, h + 1))
                    plain(p, ones, mf[:, h, :], True, True).then_inc(acc_full[p], 1)
                pe.wait_ge(sem("B_made"), upto("B_made", l, 4))
                s0, j0 = base["br", l], jobs["br", l]
                for mp in range(4):
                    for br in range(2):
                        sl, before = slab_ready(s0, 2 * mp + br, 0)
                        for m in range(2):
                            p = free_pair(j0, 4 * mp + 2 * br + m)
                            blocks([(sl, 4 * m + k, Bh[:, 4 * br + k, :], Bl[:, 4 * br + k, :], p, k == 0, k == 3,
                                     before if m == 0 and k == 0 else None, acc_full[p]) for k in range(4)])
                pe.wait_ge(sem("M_made"), upto("M_made", l, KT))
                products8("wo", l, KT, Hh, Hl)
                norm_sum("n2", 1)
                if l == 0:
                    pe.wait_ge(sem("H_made"), upto("H_made", l, 2 * KT))
                else:
                    pe.wait_ge(sem("hf_made"), upto("hf_made", l, 2 * KT))
                    pe.wait_ge(sem("hfs_made"), upto("hfs_made", l, 2))
                    for n in range(NB + 1):
                        rows = P if n < NB else NS
                        for k in range(KT):
                            mm = pe.matmul(ps[0:rows, 6, n * E:n * E + E], hf[:, k, n * P:n * P + rows],
                                           sm[:, S_RW + k * E:S_RW + k * E + E], start=k == 0, stop=k == KT - 1)
                    mm.then_inc(sem("rl_done"), 1)
                    experts(l)
                    continue
                ne = 2
                s0, j0 = base["ff", l], jobs["ff", l]
                with pe.Fori(0, ne) as e:
                    for k in range(2 * FE):
                        sl, before = slab_ready(s0, k, e * FE)
                        p, u = psj(j0, k)
                        pe.wait_ge(acc_free[p], u + e * 10)
                        blocks([(sl, b, Hh[:, b, :], Hl[:, b, :], p, b == 0, b == KT - 1,
                                 before if b == 0 else None, acc_full[p]) for b in range(KT)])
                    pe.wait_ge(sem("hid_made"), upto("hid_made", l, (e + 1) * FE))
                    for m in range(KT):
                        p, u = psj(j0, 2 * FE + m)
                        pe.wait_ge(acc_free[p], u + e * 10)
                        for k in range(FE):
                            bi = m * FE + k
                            if bi % KT == 0:
                                sl, before = slab_ready(s0, 2 * FE + bi // KT, e * FE)
                            blocks([(sl, bi % KT, hidh[:, k, :], hidl[:, k, :], p, k == 0, k == FE - 1,
                                     before if bi % KT == 0 else None, acc_full[p])])

        @block.scalar
        def _(act):
            steps = [0]

            def link(inst):
                steps[0] += 1
                inst.then_inc(sem("act_step"), 1)
                act.wait_ge(sem("act_step"), steps[0])

            def split_high(s0, k, i=0):
                sl, u = slot(s0, k + LEAD, i)
                r = r_use(s0, k + LEAD, i)
                act.wait_ge(raw_full[sl], 16 * (u + 1))
                if sl == SLOTS - 1:
                    act.wait_ge(split_used[sl], r + 1)
                elif not (isinstance(r, int) and r == 0):
                    act.wait_ge(split_used[sl], r)
                act.activation(wh[:, sl, :], raw[:, sl, :], ACT.Copy).then_inc(hi_made[sl], 1)

            def take(j0, k, i=0):
                p, u = psj(j0, k, i)
                act.wait_ge(acc_full[p], u + 1)
                return p

            def experts(l):
                act.wait_ge(sem("rt_exp_in"), 1)
                act.activation(r1[5][:], r1[4][:], ACT.Exp).then_inc(sem("rt_exp"), 1)
                for n in range(NB + 1):
                    rows = P if n < NB else NS
                    p = take(jobs["ht", l], n)
                    act.activation(hTh[0:rows, n, :].rearrange("p (a c) -> p a c", a=2), ps[0:rows, 2 * p:2 * p + 2, :], ACT.Copy
                                   ).then_inc(sem("hTh_made"), 1)

                def gathered(job0, i, m):
                    p, u = psj(job0, m)
                    act.wait_ge(acc_full[p], u + i * (ITEM_JOBS // PAIRS) + 1)
                    act.activation(XE[:, :, m, :], ps[:, 2 * p:2 * p + 2, 0:CAP], ACT.Copy).then_inc(acc_free[p], 1)

                for m in range(0, KT, 2):
                    gathered(jobs["xe", l], 0, m)
                act.wait_ge(sem("sweeps_made"), 1)
                n_sweeps = act.value_load(sweeps[0:1, 0:1], min_val=1, max_val=3)
                s0, j0 = base["ff", l], jobs["ff", l]
                per_pair = ITEM_JOBS // PAIRS
                with act.Fori(0, n_sweeps) as c, act.Fori(0, E) as e:
                    i = c * E + e

                    def full(k):
                        p, u = psj(j0, k)
                        act.wait_ge(acc_full[p], u + i * per_pair + 1)
                        return p

                    def expert_high(k):
                        f = k % RING
                        sl, _ = slot(s0, k + LEAD)
                        act.wait_ge(more_full[f], 16 * (i * (EXP_SLABS // RING) + k // RING + 1))
                        act.wait_ge(split_used[sl], r_use(s0, k + LEAD, i * FE) + (sl == SLOTS - 1))
                        act.activation(wh[:, sl, :], ring(f), ACT.Copy).then_inc(hi_made[sl], 1)

                    def hidden_high(m):
                        p, u = psj(j0, 1 + m)
                        act.wait_ge(acc_free[p], u + i * per_pair + 1)
                        act.activation(heh[:, m, :], hmm[:, m % 3, :], ACT.Copy
                                       ).then_inc(sem("hidh_made"), 1)

                    p = full(0)
                    act.activation(ST[0:CT, :, T:N], ps[0:CT, 6, 0:2 * NS].rearrange("p (t c) -> p t c", t=2), ACT.Copy)
                    act.activation(ST[0:CT, :, 0:T], ps[0:CT, 2 * p:2 * p + 2, :], ACT.Copy).then_inc(acc_free[p], 1)
                    for m in range(FE):
                        expert_high(2 * m)
                        if m:
                            hidden_high(m - 1)
                        expert_high(2 * m + 1)
                        p = full(1 + m)
                        act.activation(sgm[:, m % 3, :], ps[:, 2 * p, 0:CAP], ACT.Silu).then_inc(sem("silu_made"), 1)
                    for k in range(FE):
                        expert_high(2 * FE + k)
                        if k == 0:
                            hidden_high(FE - 1)
                    act.wait_ge(sem("slotw_made"), i + 1)
                    p2 = [full(1 + FE + t) for t in range(2)]
                    for t, p in enumerate(p2):
                        act.activation(Yh[0:CT, t, :].rearrange("p (a c) -> p a c", a=2), ps[0:CT, 2 * p:2 * p + 2, :], ACT.Copy,
                                       scale=slotw[0:CT, t:t + 1]).then_inc(sem("Yh_made"), 1)
                    for m in range(0, KT, 2):
                        gathered(j0 + 3 + FE, i, m)

            act.wait_ge(sem("c_landed"), 16)
            act.activation(c_act[:], c_in[:], ACT.Silu).then_inc(sem("c_made"), 1)
            first = base["w1", 0]
            act.wait_ge(sem("x_in"), 16)
            for l in range(L):
                ne = 2 if l == 0 else E

                def norm(name, which):
                    if which:
                        products_read(act, "wo", l)
                    elif l:
                        products_read(act, "ff", l - 1)
                    for k in range(KT):
                        act.activation(sq[:, k, :], x[:, k, :], ACT.Square).then_inc(sem("sq_made"), 1)
                    if name == "n1" and l == 0:
                        act.wait_ge(sem("eps_made"), 1)
                    p = take(jobs[name, l], 0)
                    act.activation(two(rt[:]), pair(p), ACT.Sqrt, bias=eps[:], scale=1.0 / D).then_inc(acc_free[p], 1)
                    if name == "n1" and l == 0:
                        act.wait_ge(sem("mod_made"), 2 * L)
                    for k in range(KT):
                        act.wait_ge(sem("tn_made"), upto("tn_made", l, which * KT + k + 1))
                        act.activation(hf[:, k, 0:T], tn[:, k, 0:T], ACT.Identity, bias=mod[:, l, (3 * which) * KT + k, 0:1],
                                       scale=mod[:, l, (3 * which + 1) * KT + k, 0:1]).then_inc(sem("hf_made"), 1)
                    act.wait_ge(sem("hf_made"), upto("hf_made", l, (which + 1) * KT))
                    act.wait_ge(sem("hfs_made"), upto("hfs_made", l, which + 1))
                    if l == 1 and which == 1:
                        return
                    for k in range(KT):
                        act.activation(Hh[:, k, :], hf[:, k, :], ACT.Copy).then_inc(sem("Hh_made"), 1)

                norm("n1", 0)
                if l == 0:
                    for k in range(LEAD):
                        split_high(first, k - LEAD)
                s0, j0 = base["w1", l], jobs["w1", l]
                with act.Fori(0, W1 // 3) as i:
                    for j in range(3):
                        split_high(s0, j, i)
                        p = take(j0, j, i)
                        act.activation(two(z[:, bass.ds(3 * i + j, 1), :].rearrange("p o n -> p (o n)")), pair(p), ACT.Copy
                                       ).then_inc(acc_free[p], 1)
                products_read(act, "w1", l)
                for i in range(5):
                    act.activation(qsq[:, i, :], z[:, Z_Q + i, :], ACT.Square).then_inc(sem("qsq_made"), 1)
                for i in range(5):
                    p = take(jobs["qk", l], i)
                    act.activation(two(qrt[:, i, :]), pair(p), ACT.Sqrt, bias=eps[:], scale=1.0 / HD
                                   ).then_inc(acc_free[p], 1)
                act.wait_ge(sem("vt_done"), upto("vt_done", l, 1))
                act.wait_ge(sem("qk_made"), upto("qk_made", l, 5))
                act.activation(vtok[:].rearrange("p a b -> p (a b)"), ps[:, 6, :], ACT.Copy).then_inc(sem("vtok_made"), 1)
                for n in range(NB):
                    W = 2 * P if n else P
                    act.wait_ge(sem("soft_in"), upto("soft_in", l, n + 1))
                    for h in range(NH):
                        act.activation(sc[:, h, 0:W], sc[:, h, 0:W], ACT.Exp, bias=nmx[:, h:h + 1], accum_out=rs[:, h:h + 1])
                    act.activation(esk[:], sk[:], ACT.Exp).then_inc(sem("exp_done"), 1)
                    act.wait_ge(sem("pt_done"), upto("pt_done", l, n + 1))
                    act.activation(PT[:, 0:2, :], ps[:, 4:6, :], ACT.Copy).then_inc(sem("pta_copied"), 1)
                    act.wait_ge(sem("av_done"), upto("av_done", l, n + 1))
                    act.activation(Bh[:, 0:4, n * P:n * P + P], ps[:, 0, :].rearrange("p (t c) -> p t c", t=4), ACT.Copy
                                   ).then_inc(sem("avh_made"), 1)
                act.wait_ge(sem("dsoft_in"), upto("dsoft_in", l, 1))
                link(act.activation(scs[:], scs[:], ACT.Exp))
                act.activation(ses[:], sts[:], ACT.Exp).then_inc(sem("dexp_done"), 1)
                act.wait_ge(sem("dpt_done"), upto("dpt_done", l, 1))
                act.activation(pT[:].rearrange("p b h -> p (b h)"), ps[:, 4, 0:NS * NH], ACT.Copy).then_inc(sem("pT_made"), 1)
                act.activation(prow[:].rearrange("p b h -> p (b h)"), ps[0:1, 5, 0:NS * NH], ACT.Copy
                               ).then_inc(sem("pT_made"), 1)
                act.wait_ge(sem("dav_done"), upto("dav_done", l, 1))
                dav = ps[:, 0, 0:NS * NH].rearrange("p (b k t) -> p k t b", b=NS, k=NKV)
                for kv in range(NKV):
                    hp = slice(64 * kv, 64 * kv + 64)
                    act.activation(Bh[hp, 0:4, T:N], dav[hp, kv], ACT.Copy).then_inc(sem("dah_made"), 1)
                act.wait_ge(sem("kvt_done"), upto("kvt_done", l, 1))
                act.activation(kts[:], ps[0:NS, 4, 0:256], ACT.Copy).then_inc(sem("kts_made"), 1)
                act.wait_ge(sem("dlg_made"), upto("dlg_made", l, 1))
                link(act.activation(lab[:], las[:], ACT.Abs))
                link(act.activation(lab[:], lab[:], ACT.Exp, scale=-1.0))
                act.activation(lab[:], lab[:], ACT.Ln, bias=1.0).then_inc(sem("lab_made"), 1)
                act.wait_ge(sem("dla_done"), upto("dla_done", l, 1))
                act.activation(dcs[:].rearrange("p q b -> p (q b)"), ps[:, 7, 0:2 * NS], ACT.Exp, scale=1.0 / 16
                               ).then_inc(sem("dcs_made"), 1)
                act.wait_ge(sem("do_done"), upto("do_done", l, 1))
                for r in range(2):
                    mm = act.activation(osmp[:].rearrange("p (q r) b -> p r q b", q=2)[:, r],
                                        ps[:, 4 + r, 0:2 * NS].rearrange("p (q b) -> p q b", q=2), ACT.Copy, scale=0.125)
                mm.then_inc(sem("osmp_made"), 1)
                act.wait_ge(sem("plg_made"), upto("plg_made", l, 1))
                link(act.activation(lt[:], la[:], ACT.Abs))
                link(act.activation(lt[:], lt[:], ACT.Exp, scale=-1.0))
                act.activation(lt[:], lt[:], ACT.Ln, bias=1.0).then_inc(sem("lt_made"), 1)
                act.wait_ge(sem("cum_done"), upto("cum_done", l, 1))
                act.wait_ge(sem("cache_out"), upto("cache_out", l, 6 * 16))
                link(act.activation(cum[:], ps[:, 2:4, :], ACT.Copy))
                act.activation(qe[:], cum[:], ACT.Exp).then_inc(sem("qe_exp"), 1)
                act.wait_ge(sem("qt_in"), upto("qt_in", l, 1))
                act.activation(qt[:], qt[:], ACT.Exp).then_inc(sem("qt_exp"), 1)
                for q in range(2):
                    for n in range(NB):
                        last = n * P + P - 1
                        act.activation(kd[:, q, n * P:n * P + P], cum[:, q, n * P:n * P + P], ACT.Exp, scale=-1.0,
                                       bias=cum[:, q, last:last + 1])
                mm = act.activation(dec[:], cum[:, :, P - 1::P], ACT.Exp)
                mm.then_inc(sem("kd_exp"), 1)
                for q in range(2):
                    for n in range(NB):
                        for i in range(NI):
                            k0 = SUB * i * (i + 1) // 2
                            ref = n * P + SUB * i + SUB // 2 - 1
                            mm = act.activation(kt[:, q, n, k0:k0 + SUB * (i + 1)], cum[:, q, n * P:n * P + SUB * (i + 1)],
                                                ACT.Exp, scale=-1.0, bias=cum[:, q, ref:ref + 1])
                mm.then_inc(sem("kt_exp"), 1)
                act.wait_ge(sem("gvt_done"), upto("gvt_done", l, 1))
                act.activation(gvt[:, 0:2, :], ps[:, 4:6, :], ACT.Copy).then_inc(sem("gvt_made"), 1)
                act.wait_ge(sem("kdt_done"), upto("kdt_done", l, 1))
                act.activation(kdt[:].rearrange("p (a b) c -> p a (b c)", a=2), ps[:, 0:2, :], ACT.Copy
                               ).then_inc(sem("kdt_made"), 1)
                act.wait_ge(sem("o_done"), upto("o_done", l, 1))
                act.activation(z[:, Z_Q:Z_Q + 4, 0:T], ps[:, 0:4, :], ACT.Copy, scale=0.125)
                act.activation(z[:, Z_Q:Z_Q + 4, T:N], osmp[:], ACT.Copy).then_inc(sem("o_read"), 1)
                s0, j0 = base["w3", l], jobs["w3", l]

                def w3_tile(k, i, m, f):
                    split_high(s0, k, i)
                    p = take(j0, k, i)
                    act.activation(two(g[:, bass.ds(m, 1), :].rearrange("p o n -> p (o n)")), pair(p), f
                                   ).then_inc(acc_free[p], 1)

                for k in range(4):
                    w3_tile(k, 0, k, ACT.Silu)
                with act.Fori(0, 5) as i:
                    for j in range(3):
                        w3_tile(4 + j, i, 3 * i + (4 + j), ACT.Sigmoid)
                w3_tile(19, 0, 19, ACT.Sigmoid)
                act.wait_ge(sem("o_read"), upto("o_read", l, 1))
                products_read(act, "w3", l)
                for h in range(GH):
                    act.activation(mf[:, h, :], z[:, Z_Q + h, :], ACT.Square).then_inc(sem("osq_made"), 1)
                for h in range(GH):
                    p = take(jobs["gn", l], h)
                    act.activation(two(mf[:, 4 + h, :]), pair(p), ACT.Sqrt, bias=eps[:], scale=1.0 / GV
                                   ).then_inc(acc_free[p], 1)
                for h in range(GH):
                    act.wait_ge(sem("og_made"), upto("og_made", l, h + 1))
                    act.activation(Bh[:, 4 + h, :], z[:, Z_Q + h, :], ACT.Copy).then_inc(sem("Bh_made"), 1)
                for k in range(8):
                    split_high(base["br", l], k)
                    if k % 2:
                        for m in (k - 1, k):
                            act.wait_ge(sem("mf_made"), upto("mf_made", l, m + 1))
                            act.activation(Hh[:, m, :], mf[:, m, :], ACT.Copy).then_inc(sem("Mh_made"), 1)
                for k in range(8):
                    split_high(base["wo", l], k)
                norm("n2", 1)
                s0, j0 = base["ff", l], jobs["ff", l]
                if l == 1:
                    experts(l)
                    continue
                with act.Fori(0, ne) as e:
                    for m in range(FE):
                        split_high(s0, 2 * m, e * FE)
                        p, u = psj(j0, 2 * m)
                        act.wait_ge(acc_full[p], u + e * 10 + 1)
                        act.activation(two(sg[:, m % 2, :]), pair(p), ACT.Silu).then_inc(acc_free[p], 1)
                        split_high(s0, 2 * m + 1, e * FE)
                        p, u = psj(j0, 2 * m + 1)
                        act.wait_ge(acc_free[p], u + e * 10 + 1)
                        act.activation(hidh[:, m, :], hm[:, m % 3, :], ACT.Copy).then_inc(sem("hidh_made"), 1)
                    for k in range(FE):
                        split_high(s0, 2 * FE + k, e * FE)

        @block.vector
        def _(dve):
            steps = [0]

            def link(inst):
                steps[0] += 1
                inst.then_inc(sem("dve_step"), 1)
                dve.wait_ge(sem("dve_step"), steps[0])

            def split_low(s0, k, i=0):
                sl, _ = slot(s0, k + LEAD, i)
                dve.wait_ge(hi_made[sl], r_use(s0, k + LEAD, i) + 1)
                dve.tensor_tensor(wl[:, sl, :], raw[:, sl, :], wh[:, sl, :].bitcast(F32), ALU.subtract
                                  ).then_inc(split_made[sl], 1)

            def take(j0, k, i=0):
                p, u = psj(j0, k, i)
                dve.wait_ge(acc_full[p], u + 1)
                return p

            def bc(ap, n, axis=2):
                v = ap.unsqueeze(axis)
                return v.broadcast_to([n if i == axis else k for i, k in enumerate(v.shape)])

            dve.memset(eps[:], EPS).then_inc(sem("eps_made"), 1)
            dve.wait_ge(sem("small_in"), 16)
            dve.tensor_scalar(qg8[:], sm[:, S_QK:S_QK + 2 * L:2], 0.125, None, ALU.mult).then_inc(sem("qg8_made"), 1)
            for l in range(L):
                dve.wait_ge(ada_used[(l * ADA + ADA - 1) % SLOTS], (l * ADA + ADA - 1) // SLOTS + 1)
                link(dve.tensor_tensor(mod[:, l], ps[:, 6 + l, 0:9 * ADA].rearrange("p (m c) -> p m c", c=9),
                                       bc(sm[:, S_ADAB + l * ADA:S_ADAB + l * ADA + ADA], 9), ALU.add))
                for w in range(2):
                    sc1 = mod[:, l, (3 * w + 1) * KT:(3 * w + 2) * KT, :]
                    dve.scalar_tensor_tensor(out=sc1, in0=sc1, scalar=1.0,
                                             in1=bc(sm[:, S_N + (2 * l + w) * KT:S_N + (2 * l + w + 1) * KT], 9),
                                             op0=ALU.add, op1=ALU.mult).then_inc(sem("mod_made"), 1)

            def add_residual(l, p, m, which, n_tmp):
                gi = (2 + 3 * which) * KT + m
                dve.scalar_tensor_tensor(out=x[:, m, 0:HN], in0=ps[:, 2 * p, 0:HN], scalar=mod[:, l, gi, 0:1],
                                         in1=x[:, m, 0:HN], op0=ALU.mult, op1=ALU.add)
                dve.scalar_tensor_tensor(out=x[:, m, HN:T], in0=ps[:, 2 * p + 1, 0:T - HN], scalar=mod[:, l, gi, 0:1],
                                         in1=x[:, m, HN:T], op0=ALU.mult, op1=ALU.add)
                dve.tensor_tensor(xs_tmp[:, m % 2, :], ps[:, 2 * p + 1, T - HN:HN], mod[:, l, gi, 1:9], ALU.mult
                                  ).then_inc(sem("xs_made"), 1)
                dve.wait_ge(sem("xs_made"), n_tmp)
                dve.tensor_tensor(x[:, m, T:N], x[:, m, T:N], xs_tmp[:, m % 2, :], ALU.add).then_inc(acc_free[p], 1)

            def experts(l):
                dve.wait_ge(sem("rank_done"), 1)
                link(dve.memset(slotpos[:], -1.0))
                link(dve.tensor_tensor(slotpos[:, 0:NB, 0:E], chosen[:, 0:NB, :],
                                       ps[:, 7, 0:NB * E].rearrange("p (n e) -> p n e", e=E), ALU.mult))
                link(dve.tensor_tensor(slotpos[0:NS, NB, 0:E], chosen[0:NS, NB, :], ps[0:NS, 7, NB * E:NB * E + E], ALU.mult))
                dve.tensor_scalar(slotpos[:, 0:NB, 0:E], slotpos[:, 0:NB, 0:E], -1.0, None, ALU.add)
                link(dve.tensor_scalar(slotpos[0:NS, NB, 0:E], slotpos[0:NS, NB, 0:E], -1.0, None, ALU.add))
                link(dve.tensor_scalar(slotpos[:, :, E:E + 1], slotpos[:, :, 0:1], -float(CAP), None, ALU.add))
                link(dve.tensor_reduce(cnt[0][:], ps[:, 7, (NB + 1) * E:(NB + 2) * E], AX, ALU.max))
                dve.tensor_scalar(cnt[1][:], cnt[0][:], CAP + 0.5, 1.0, ALU.is_gt, ALU.add)
                link(dve.tensor_scalar(cnt[2][:], cnt[0][:], 2 * CAP + 0.5, None, ALU.is_gt))
                dve.tensor_tensor(sweeps[:], cnt[1][:], cnt[2][:], ALU.add).then_inc(sem("sweeps_made"), 1)

                def select(e):
                    dve.tensor_tensor(Sel[:], bc(slot_ids, NB + 1, 1),
                                      slotpos[:, :, bass.ds(e, 1)].broadcast_to([P, NB + 1, CAP]), ALU.is_equal
                                      ).then_inc(sem("Sel_made"), 1)

                select(0)
                for n in range(NB + 1):
                    rows = P if n < NB else NS
                    p = take(jobs["ht", l], n)
                    dve.wait_ge(sem("hTh_made"), n + 1)
                    dve.tensor_tensor(hTl[0:rows, n, :].rearrange("p (a c) -> p a c", a=2), ps[0:rows, 2 * p:2 * p + 2, :],
                                      hTh[0:rows, n, :].rearrange("p (a c) -> p a c", a=2).bitcast(F32), ALU.subtract
                                      ).then_inc(acc_free[p], 1)

                def gathered(job0, i, m):
                    p, u = psj(job0, m)
                    dve.wait_ge(acc_full[p], u + i * (ITEM_JOBS // PAIRS) + 1)
                    dve.tensor_copy(XE[:, :, m, :], ps[:, 2 * p:2 * p + 2, 0:CAP]).then_inc(acc_free[p], 1)

                for m in range(1, KT, 2):
                    gathered(jobs["xe", l], 0, m)
                dve.wait_ge(sem("sweeps_made"), 1)
                n_sweeps = dve.value_load(sweeps[0:1, 0:1], min_val=1, max_val=3)
                s0, j0 = base["ff", l], jobs["ff", l]
                per_pair = ITEM_JOBS // PAIRS
                with dve.Fori(0, n_sweeps) as c:
                    with dve.Fori(0, E) as e:
                        i = c * E + e

                        def full(k):
                            p, u = psj(j0, k)
                            dve.wait_ge(acc_full[p], u + i * per_pair + 1)
                            return p

                        def expert_low(k):
                            sl, _ = slot(s0, k + LEAD)
                            dve.wait_ge(hi_made[sl], r_use(s0, k + LEAD, i * FE) + 1)
                            dve.tensor_tensor(wl[:, sl, :], ring(k % RING), wh[:, sl, :].bitcast(F32), ALU.subtract
                                              ).then_inc(split_made[sl], 1)

                        def hidden_low(m):
                            dve.wait_ge(sem("hidh_made"), upto("hidh_made", l, i * FE + m + 1))
                            dve.tensor_tensor(hel[:, m, :], hmm[:, m % 3, :], heh[:, m, :].bitcast(F32), ALU.subtract
                                              ).then_inc(sem("hid_made"), 1)

                        full(0)
                        dve.tensor_copy(slotw[0:CT, :], ps[0:CT, 7, 0:2]).then_inc(sem("slotw_made"), 1)
                        for m in range(FE):
                            expert_low(2 * m)
                            if m:
                                hidden_low(m - 1)
                            if m == 2:
                                select(e + 1)
                            expert_low(2 * m + 1)
                            p = full(1 + m)
                            dve.wait_ge(sem("silu_made"), i * FE + m + 1)
                            dve.tensor_tensor(hmm[:, m % 3, :], sgm[:, m % 3, :], ps[:, 2 * p + 1, 0:CAP], ALU.mult
                                              ).then_inc(acc_free[p], 1)
                        for k in range(FE):
                            expert_low(2 * FE + k)
                            if k == 0:
                                hidden_low(FE - 1)
                        p2 = [full(1 + FE + t) for t in range(2)]
                        for t, p in enumerate(p2):
                            dve.wait_ge(sem("Yh_made"), i * 2 + t + 1)
                            dve.scalar_tensor_tensor(out=Yl[0:CT, t, :].rearrange("p (a c) -> p a c", a=2),
                                                     in0=ps[0:CT, 2 * p:2 * p + 2, :], scalar=slotw[0:CT, t:t + 1],
                                                     in1=Yh[0:CT, t, :].rearrange("p (a c) -> p a c", a=2).bitcast(F32),
                                                     op0=ALU.mult, op1=ALU.subtract).then_inc(acc_free[p], 1)
                        for m in range(1, KT, 2):
                            gathered(j0 + 3 + FE, i, m)
                        for m in range(KT):
                            p = full(3 + FE + KT + m)
                            add_residual(l, p, m, 1, i * KT + upto("xs_made", l, KT + m + 1))
                    dve.tensor_scalar(slotpos[:], slotpos[:], -float(CAP), None, ALU.add).then_inc(sem("slotpos_moved"), 1)
                    dve.wait_ge(sem("slotpos_moved"), c + 1)
                dve.memset(cnt[0][:], 0.0).then_inc(sem("x_final"), 1)

            dve.wait_ge(sem("x_in"), 16)
            dve.wait_ge(sem("const_in"), 16)
            dve.wait_ge(sem("mod_made"), 2 * L)
            dve.wait_ge(sem("qg8_made"), 1)
            for l in range(L):
                ne = 2 if l == 0 else E

                def norm(name, which):
                    p, u = psj(jobs[name, l], 0)
                    dve.wait_ge(acc_free[p], u + 1)
                    link(dve.reciprocal(ri[:], rt[:]))
                    for k in range(KT):
                        dve.tensor_tensor(tn[:, k, :], x[:, k, :], ri[:], ALU.mult).then_inc(sem("tn_made"), 1)
                    dve.wait_ge(sem("tn_made"), upto("tn_made", l, (which + 1) * KT))
                    link(dve.tensor_tensor(hf[:, :, T:N], tn[:, :, T:N], mod[:, l, (3 * which + 1) * KT:(3 * which + 2) * KT, 1:9], ALU.mult))
                    dve.tensor_tensor(hf[:, :, T:N], hf[:, :, T:N], mod[:, l, 3 * which * KT:(3 * which + 1) * KT, 1:9], ALU.add
                                      ).then_inc(sem("hfs_made"), 1)
                    if l == 1 and which == 1:
                        return
                    for k in range(KT):
                        dve.wait_ge(sem("Hh_made"), upto("Hh_made", l, which * KT + k + 1))
                        dve.tensor_tensor(Hl[:, k, :], hf[:, k, :], Hh[:, k, :].bitcast(F32), ALU.subtract
                                          ).then_inc(sem("H_made"), 1)

                norm("n1", 0)
                if l == 0:
                    for k in range(LEAD):
                        split_low(base["w1", 0], k - LEAD)
                with dve.Fori(0, W1 // 3) as i:
                    for j in range(3):
                        split_low(base["w1", l], j, i)
                products_read(dve, "w1", l)
                dve.memset(z[BROW:BROW + 1, Z_GA, :], 1.0).then_inc(sem("ones_made"), 1)
                for i in range(5):
                    p, u = psj(jobs["qk", l], i)
                    dve.wait_ge(acc_free[p], u + 1)
                    link(dve.reciprocal(qrt[:, i, :], qrt[:, i, :]))
                    gain = qg8[:, l:l + 1] if i < 4 else sm[:, S_QK + 2 * l + 1:S_QK + 2 * l + 2]
                    dve.scalar_tensor_tensor(out=z[:, Z_Q + i, :], in0=z[:, Z_Q + i, :], scalar=gain, in1=qrt[:, i, :],
                                             op0=ALU.mult, op1=ALU.mult).then_inc(sem("qk_made"), 1)
                dve.wait_ge(sem("qk_made"), upto("qk_made", l, 5))
                for n in range(NB):
                    W = 2 * P if n else P
                    dve.wait_ge(sem("sc_done"), upto("sc_done", l, n + 1))
                    if n:
                        dve.wait_ge(sem("pt_done"), upto("pt_done", l, n))
                    for kv in range(NKV):
                        mm = dve.tensor_tensor(sc[:, 4 * kv:4 * kv + 4, 0:W],
                                               ps[:, 2 * kv:2 * kv + 2, :].rearrange("p a (b s) -> p (a b) s", b=2)[:, :, 0:W],
                                               biasT[:, 4 * kv:4 * kv + 4, 2 * P - W:2 * P], ALU.add)
                    link(mm)
                    link(dve.tensor_reduce(mx[:], sc[:, :, 0:W], AX, ALU.max))
                    link(dve.tensor_tensor(mx[:], mx[:], sm[:, S_SINK + l * NH:S_SINK + l * NH + NH], ALU.max))
                    dve.tensor_scalar(nmx[:], mx[:], -1.0, None, ALU.mult)
                    dve.tensor_tensor(sk[:], sm[:, S_SINK + l * NH:S_SINK + l * NH + NH], mx[:], ALU.subtract
                                      ).then_inc(sem("soft_in"), 1)
                    dve.wait_ge(sem("exp_done"), upto("exp_done", l, n + 1))
                    link(dve.tensor_tensor(den[:], rs[:], esk[:], ALU.add))
                    link(dve.reciprocal(rec[:], den[:]))
                    dve.tensor_tensor(sc[:, :, 0:W], sc[:, :, 0:W], bc(rec[:], W), ALU.mult).then_inc(sem("p_made"), 1)
                    dve.wait_ge(sem("pt_done"), upto("pt_done", l, n + 1))
                    if n:
                        dve.tensor_copy(PT[:, 2:4, :], ps[:, 6:8, :]).then_inc(sem("ptb_copied"), 1)
                    else:
                        dve.memset(den[:], 0.0).then_inc(sem("ptb_copied"), 1)
                    dve.wait_ge(sem("avh_made"), upto("avh_made", l, n + 1))
                    dve.tensor_tensor(Bl[:, 0:4, n * P:n * P + P], ps[:, 0, :].rearrange("p (t c) -> p t c", t=4),
                                      Bh[:, 0:4, n * P:n * P + P].bitcast(F32), ALU.subtract).then_inc(sem("av_read"), 1)
                link(dve.memset(qs[:], 0.0))
                for kv in range(NKV):
                    hp = slice(64 * kv, 64 * kv + 64)
                    mm = dve.tensor_copy(qs[hp, :, 4 * kv:4 * kv + 4].rearrange("p b t -> p t b"), z[hp, Z_Q:Z_Q + 4, T:N])
                mm.then_inc(sem("qs_made"), 1)
                dve.wait_ge(sem("kc_in"), upto("kc_in", l, 16))
                dve.tensor_copy(kc[:, :, P:P + 1].rearrange("p b o -> p (b o)"), z[:, Z_K, T:N]).then_inc(sem("kc_made"), 1)
                dve.wait_ge(sem("dsc_done"), upto("dsc_done", l, 1))
                link(dve.tensor_tensor(scs[:], ps[0:NS, 0:4, :].rearrange("p a (b s) -> p (a b) s", b=2)[:, :, 0:129],
                                       bc(biasS, NS, 1), ALU.add))
                link(dve.tensor_reduce(smx[:], scs[:], AX, ALU.max))
                sinkc = sm[0:NS, S_SINKC + l:S_SINKC + l + 1]
                link(dve.tensor_scalar(smx[:], smx[:], sinkc, None, ALU.max))
                dve.tensor_tensor(scs[:], scs[:], bc(smx[:], 129), ALU.subtract)
                dve.tensor_scalar(sts[:], smx[:], -1.0, sinkc, ALU.mult, ALU.add).then_inc(sem("dsoft_in"), 1)
                dve.wait_ge(sem("dexp_done"), upto("dexp_done", l, 1))
                link(dve.tensor_reduce(srs[:], scs[:], AX, ALU.add))
                link(dve.tensor_tensor(sdn[:], srs[:], ses[:], ALU.add))
                link(dve.reciprocal(srec[:], sdn[:]))
                dve.tensor_tensor(scs[:], scs[:], bc(srec[:], 129), ALU.mult).then_inc(sem("dp_made"), 1)
                dve.wait_ge(sem("dpt_done"), upto("dpt_done", l, 1))
                dve.tensor_copy(vrow[:].rearrange("p (a b) v -> p a (b v)", a=2), ps[0:1, 6:8, :]).then_inc(sem("vrow_made"), 1)
                dav = ps[:, 0, 0:NS * NH].rearrange("p (b k t) -> p k t b", b=NS, k=NKV)
                for kv in range(NKV):
                    hp = slice(64 * kv, 64 * kv + 64)
                    dve.wait_ge(sem("dah_made"), upto("dah_made", l, kv + 1))
                    mm = dve.tensor_tensor(Bl[hp, 0:4, T:N], dav[hp, kv], Bh[hp, 0:4, T:N].bitcast(F32), ALU.subtract)
                mm.then_inc(sem("da_read"), 1)
                dve.wait_ge(sem("dlg_done"), upto("dlg_done", l, 1))
                dve.tensor_copy(las[:], ps[0:NS, 6, 0:256]).then_inc(sem("dlg_made"), 1)
                dve.wait_ge(sem("kts_made"), upto("kts_made", l, 1))
                dve.tensor_tensor(kms[:], bc(kts[:], NS, 1), bc(ident[0:NS, 0:NS], 256), ALU.mult)
                dve.tensor_copy(vts[:], ps[0:NS, 5, :]).then_inc(sem("kms_made"), 1)
                dve.wait_ge(sem("lab_made"), upto("lab_made", l, 1))
                link(dve.tensor_scalar(lac[:], las[:], 0.0, None, ALU.min))
                dve.tensor_tensor(las[:], lac[:], lab[:], ALU.subtract).then_inc(sem("las_made"), 1)
                dve.wait_ge(sem("dcs_made"), upto("dcs_made", l, 1))
                dve.wait_ge(sem("st_in"), upto("st_in", l, 16))
                link(dve.tensor_tensor(Sst[:], Sst[:], bc(dcs[:].rearrange("p q b -> p b q"), GV, 3), ALU.mult))
                dve.wait_ge(sem("kv_done"), upto("kv_done", l, 1))
                dve.tensor_tensor(Sst[:].rearrange("p b q v -> p (b q v)"), Sst[:].rearrange("p b q v -> p (b q v)"),
                                  ps[:, 0:4, :].rearrange("p a c -> p (a c)"), ALU.add).then_inc(sem("Sst_made"), 1)
                dve.wait_ge(sem("lg_done"), upto("lg_done", l, 1))
                dve.tensor_copy(la[:].rearrange("p n c -> p (n c)"), ps[:, 0:2, :].rearrange("p a c -> p (a c)")
                                ).then_inc(sem("plg_made"), 1)
                dve.wait_ge(sem("lt_made"), upto("lt_made", l, 1))
                link(dve.tensor_scalar(la[:], la[:], 0.0, None, ALU.min))
                dve.tensor_tensor(la[:], la[:], lt[:], ALU.subtract).then_inc(sem("la_made"), 1)
                dve.wait_ge(sem("qe_exp"), upto("qe_exp", l, 1))
                refs = cum[:, :, SUB // 2 - 1::SUB]
                dve.tensor_tensor(qt[:].rearrange("p q (i c) -> p q i c", c=SUB), cum[:].rearrange("p q (i c) -> p q i c", c=SUB),
                                  bc(refs, SUB, 3), ALU.subtract).then_inc(sem("qt_in"), 1)
                dve.tensor_tensor(qe[:], qe[:], z[:, Z_GQ:Z_GQ + 2, 0:T], ALU.mult).then_inc(sem("qe_made"), 1)
                dve.memset(att[:], 0.0)
                dve.memset(S[:], 0.0)
                dve.wait_ge(sem("qt_exp"), upto("qt_exp", l, 1))
                dve.tensor_tensor(qt[:], qt[:], z[:, Z_GQ:Z_GQ + 2, 0:T], ALU.mult).then_inc(sem("qt_made"), 1)
                dve.wait_ge(sem("kd_exp"), upto("kd_exp", l, 1))
                dve.tensor_tensor(kd[:], kd[:], z[:, Z_GK:Z_GK + 2, 0:T], ALU.mult).then_inc(sem("kd_made"), 1)
                dve.wait_ge(sem("kt_exp"), upto("kt_exp", l, 1))
                for i in range(NI):
                    k0 = SUB * i * (i + 1) // 2
                    rows = SUB * (i + 1)
                    gk = z[:, Z_GK:Z_GK + 2, 0:T].rearrange("p q (n c) -> p q n c", n=NB)[:, :, :, 0:rows]
                    mm = dve.tensor_tensor(kt[:, :, :, k0:k0 + rows], kt[:, :, :, k0:k0 + rows], gk, ALU.mult)
                mm.then_inc(sem("kt_made"), 1)
                dve.wait_ge(sem("gvt_done"), upto("gvt_done", l, 1))
                dve.tensor_copy(gvt[:, 2:4, :], ps[:, 6:8, :]).then_inc(sem("gvt_made"), 1)
                dve.wait_ge(sem("ds_done"), upto("ds_done", l, 1))
                for n in range(NB):
                    for r in range(2):
                        hp = slice(64 * r, 64 * r + 64)
                        for q in range(2):
                            dsn = ps[hp, 2 + n // 2, (n % 2) * 256 + q * GV:(n % 2) * 256 + q * GV + GV]
                            if n == 0:
                                mm = dve.tensor_copy(S[hp, 0, q, r, :], dsn)
                            else:
                                mm = dve.scalar_tensor_tensor(out=S[hp, n, q, r, :], in0=S[hp, n - 1, q, r, :],
                                                              scalar=dec[hp, q, n:n + 1], in1=dsn, op0=ALU.mult, op1=ALU.add)
                    mm.then_inc(sem("S_made"), 1)
                    dve.wait_ge(sem("S_made"), upto("S_made", l, n + 1))
                dve.wait_ge(sem("at_done"), upto("at_done", l, 1))
                for r in range(2):
                    src = ps[:, 4 + 2 * r:6 + 2 * r, :].rearrange("p a (b q c) -> p (a b) q c", b=2, q=2)
                    dst = att[:].rearrange("p n (q r) c -> p r n q c", q=2)
                    for i in range(NI):
                        rows = SUB * (i + 1)
                        cols = slice(SUB * i, SUB * i + SUB)
                        mk = bc(bc(MSK[0:rows, cols], 2, 1), NB, 1)
                        mm = dve.tensor_tensor(dst[0:rows, r, :, :, cols], src[0:rows, :, :, cols], mk, ALU.mult)
                mm.then_inc(sem("att_made"), 1)
                with dve.Fori(0, 6) as i:
                    for j in range(3):
                        split_low(base["w3", l], j, i)
                for k in (18, 19):
                    split_low(base["w3", l], k)
                for h in range(GH):
                    p, u = psj(jobs["gn", l], h)
                    dve.wait_ge(acc_free[p], u + 1)
                    link(dve.reciprocal(mf[:, 4 + h, :], mf[:, 4 + h, :]))
                    link(dve.scalar_tensor_tensor(out=z[:, Z_Q + h, :], in0=z[:, Z_Q + h, :],
                                                  scalar=sm[:, S_GN + l:S_GN + l + 1], in1=mf[:, 4 + h, :],
                                                  op0=ALU.mult, op1=ALU.mult))
                    dve.tensor_tensor(z[:, Z_Q + h, :], z[:, Z_Q + h, :], g[:, h, :], ALU.mult).then_inc(sem("og_made"), 1)
                dve.wait_ge(sem("S_out"), upto("S_out", l, 32))
                for h in range(GH):
                    dve.wait_ge(sem("Bh_made"), upto("Bh_made", l, h + 1))
                    dve.tensor_tensor(Bl[:, 4 + h, :], z[:, Z_Q + h, :], Bh[:, 4 + h, :].bitcast(F32), ALU.subtract
                                      ).then_inc(sem("B_made"), 1)
                s0, j0 = base["br", l], jobs["br", l]
                for mp in range(4):
                    split_low(s0, 2 * mp)
                    for m in range(2):
                        p = take(j0, 4 * mp + m)
                        dve.tensor_tensor(two(ta[:, m, :]), two(g[:, 4 + 2 * mp + m, :]), pair(p), ALU.mult
                                          ).then_inc(acc_free[p], 1)
                    split_low(s0, 2 * mp + 1)
                    for m in range(2):
                        p = take(j0, 4 * mp + 2 + m)
                        dve.tensor_tensor(two(mf[:, 2 * mp + m, :]), two(g[:, 12 + 2 * mp + m, :]), pair(p), ALU.mult
                                          ).then_inc(acc_free[p], 1)
                    p, u = psj(j0, 4 * mp + 3)
                    dve.wait_ge(acc_free[p], u + 1)
                    for m in range(2):
                        dve.tensor_tensor(mf[:, 2 * mp + m, :], mf[:, 2 * mp + m, :], ta[:, m, :], ALU.add
                                          ).then_inc(sem("mf_made"), 1)
                    for m in range(2):
                        dve.wait_ge(sem("Mh_made"), upto("Mh_made", l, 2 * mp + m + 1))
                        dve.tensor_tensor(Hl[:, 2 * mp + m, :], mf[:, 2 * mp + m, :], Hh[:, 2 * mp + m, :].bitcast(F32),
                                          ALU.subtract).then_inc(sem("M_made"), 1)
                s0, j0 = base["wo", l], jobs["wo", l]
                for k in range(KT):
                    split_low(s0, k)
                    p = take(j0, k)
                    add_residual(l, p, k, 0, upto("xs_made", l, k + 1))
                if l == 1:
                    dve.memset(cnt[0][:], 0.0).then_inc(sem("ring_open"), 1)
                norm("n2", 1)
                if l == 1:
                    link(dve.memset(lg[:], 0.0))
                    dve.wait_ge(sem("rl_done"), upto("rl_done", l, 1))
                    rb = sm[:, S_RB:S_RB + E]
                    dve.tensor_tensor(lg[:, 0:NB, :], ps[:, 6, 0:NB * E].rearrange("p (n e) -> p n e", e=E), bc(rb, NB, 1), ALU.add)
                    link(dve.tensor_tensor(lg[0:NS, NB, :], ps[0:NS, 6, NB * E:NB * E + E], rb[0:NS, :], ALU.add))
                    rk = bc(rank8, NB + 1, 1)

                    def col(i):
                        return r1[i][:].rearrange("p n o -> p (n o)")

                    def choose(logits, best, chosen, tmp, i):
                        link(dve.tensor_reduce(col(i), logits[:], AX, ALU.max))
                        link(dve.tensor_tensor(tmp[:], logits[:], bc(col(i), E), ALU.is_equal))
                        link(dve.tensor_tensor(tmp[:], tmp[:], rk, ALU.mult))
                        link(dve.tensor_reduce(col(i + 1), tmp[:], AX, ALU.max))
                        link(dve.tensor_tensor(chosen[:], tmp[:], bc(col(i + 1), E), ALU.is_equal))

                    choose(lg, None, rr[0], rr[1], 0)
                    link(dve.scalar_tensor_tensor(out=rr[2][:], in0=rr[0][:], scalar=-3.0e38, in1=lg[:], op0=ALU.mult, op1=ALU.add))
                    choose(rr[2], None, rr[3], rr[4], 2)
                    dve.tensor_tensor(chosen[:], rr[0][:], rr[3][:], ALU.add).then_inc(sem("chosen_made"), 1)
                    dve.tensor_tensor(col(4), col(2), col(0), ALU.subtract).then_inc(sem("rt_exp_in"), 1)
                    dve.wait_ge(sem("rt_exp"), upto("rt_exp", l, 1))
                    link(dve.tensor_scalar(col(6), col(5), 1.0, None, ALU.add))
                    link(dve.reciprocal(col(7), col(6)))
                    link(dve.tensor_tensor(col(8), col(5), col(7), ALU.mult))
                    dve.tensor_tensor(rr[5][:], rr[0][:], bc(col(7), E), ALU.mult)
                    link(dve.tensor_tensor(rr[6][:], rr[3][:], bc(col(8), E), ALU.mult))
                    link(dve.tensor_tensor(rr[7][:], rr[5][:], rr[6][:], ALU.add))
                    experts(l)
                    continue
                s0, j0 = base["ff", l], jobs["ff", l]
                with dve.Fori(0, ne) as e:
                    for m in range(FE):
                        split_low(s0, 2 * m, e * FE)
                        p, u = psj(j0, 2 * m)
                        dve.wait_ge(acc_free[p], u + e * 10 + 1)
                        split_low(s0, 2 * m + 1, e * FE)
                        p, u = psj(j0, 2 * m + 1)
                        dve.wait_ge(acc_full[p], u + e * 10 + 1)
                        dve.tensor_tensor(two(hm[:, m % 3, :]), two(sg[:, m % 2, :]), pair(p), ALU.mult
                                          ).then_inc(acc_free[p], 1)
                        dve.wait_ge(sem("hidh_made"), upto("hidh_made", l, e * FE + m + 1))
                        dve.tensor_tensor(hidl[:, m, :], hm[:, m % 3, :], hidh[:, m, :].bitcast(F32), ALU.subtract
                                          ).then_inc(sem("hid_made"), 1)
                    for k in range(FE):
                        split_low(s0, 2 * FE + k, e * FE)
                        for m in range(KT):
                            if (m * FE + FE - 1) // KT == k:
                                p, u = psj(j0, 2 * FE + m)
                                dve.wait_ge(acc_full[p], u + e * 10 + 1)
                                add_residual(l, p, m, 1, e * KT + upto("xs_made", l, KT + m + 1))


def slabs(inputs):
    def blocks(w, ms, kn):
        K, M = w.shape
        return w.reshape(K // P, P, M // P, P).transpose(2, 1, 0, 3).reshape(M // P, P, K)

    out = []
    for l in range(L):
        out.append(blocks(inputs["ada_w"][l], None, None))
    for l in range(L):
        w = inputs["w_in"][l]
        q = w[:, 0:512].reshape(D, 2, 4, HD).transpose(0, 2, 1, 3).reshape(D, 512)
        ga = np.zeros((D, P), np.float32)
        ga[:, 0:RANK] = w[:, 1792:1808]
        out.append(blocks(ga, None, None))
        out.append(blocks(q, None, None))
        out.append(blocks(w[:, 512:1792], None, None))
        out.append(blocks(w[:, 1808:4368], None, None))
        wa_ = inputs["w_branch_a"][l].reshape(2, 4, HD, D).transpose(1, 0, 2, 3).reshape(512, D)
        pa = blocks(wa_, None, None)
        pb = blocks(inputs["w_branch_b"][l], None, None)
        for mp in range(4):
            for w4 in (pa, pb):
                out.append(np.concatenate([w4[2 * mp], w4[2 * mp + 1]], axis=1)[None])
        out.append(blocks(inputs["w_out"][l], None, None))
        if l == 0:
            hw = FE * P
            ex = [(inputs["ffn_w_gate"][0][:, e * hw:e * hw + hw], inputs["ffn_w_up"][0][:, e * hw:e * hw + hw],
                   inputs["ffn_w_down"][0][e * hw:e * hw + hw]) for e in range(2)]
        else:
            ex = [(inputs["moe_w_gate"][0, e], inputs["moe_w_up"][0, e], inputs["moe_w_down"][0, e]) for e in range(E)]
        for wg, wu, wd in ex:
            out.append(np.stack([blocks(wg, None, None), blocks(wu, None, None)], axis=1).reshape(2 * FE, P, D))
            if l:
                out.append(wd.reshape(FE, P, D))
                continue
            d = blocks(wd, None, None).reshape(KT, P, FE, P).transpose(0, 2, 1, 3).reshape(FE, KT, P, P)
            out.append(d.transpose(0, 2, 1, 3).reshape(FE, P, D))
    experts = sum(a.shape[0] for a in out) - E * EXP_SLABS
    flat = np.concatenate(out, axis=0)
    return np.concatenate([flat, flat[experts:experts + LEAD]], axis=0)


def constants():
    c = np.zeros((P, C_END), np.float32)
    i = np.arange(P)
    c[:, C_ID:C_ID + P] = np.eye(P)
    c[:, C_ONE:C_ONE + P] = 1.0
    c[:, C_BLK:C_BLK + P] = (i[:, None] // HD) == (i[None] // HD)
    c[:, C_U:C_U + P] = (i[:, None] <= i[None]) / 16.0
    c[:, C_M:C_M + P] = i[:, None] <= i[None]
    slope = 2.0 ** -(np.arange(1, NH + 1, dtype=np.float64))
    dist = P + i[:, None] - np.arange(2 * P)[None]
    ok = (dist >= 0) & (dist <= P)
    c[:, C_BIAS:C_BIAS + NH * 2 * P] = np.where(ok[:, None], -slope[None, :, None] * dist[:, None], -1.0e30).reshape(P, -1)
    c[0:NH, C_BS:C_BS + 129] = -slope[:, None] * (P - np.arange(129))[None]
    c[:, C_RANK:C_RANK + E] = E - np.arange(E)
    c[:, C_SLOT:C_SLOT + CAP] = np.arange(CAP)
    return c


def kernel(**inputs):
    import concourse.bacc as bacc
    from concourse.bass_utils import run_bass_kernel_spmd as run

    v = {k: np.asarray(a) for k, a in inputs.items()}

    def feat(a):
        return a.T.reshape(-1, P, a.shape[0]).transpose(1, 0, 2)

    small = np.concatenate(
        [v["ada_b"][l].reshape(ADA, P).T for l in range(L)]
        + [v[n][l].reshape(KT, P).T for l in range(L) for n in ("norm1_g", "norm2_g")]
        + [np.concatenate([v[n][l], v[n][l]])[:, None] for l in range(L) for n in ("q_norm_g", "k_norm_g")]
        + [v["gla_norm_g"][l][:, None] for l in range(L)]
        + [np.broadcast_to(v["attn_sinks"].reshape(1, L * NH), (P, L * NH))]
        + [np.concatenate([v["attn_sinks"].T, np.zeros((P - NH, L), np.float32)], axis=0)]
        + [v["router_w"][0].reshape(KT, P, E).transpose(1, 0, 2).reshape(P, KT * E)]
        + [np.broadcast_to(v["router_b"], (P, E))], axis=1)
    arrays = {
        "xT": feat(np.concatenate([v["x_prompt"][0], v["x_sample"][:, 0]], axis=0)),
        "cT": feat(np.concatenate([v["c_prompt"], v["c_sample"]], axis=0)),
        "weights": slabs(v),
        "constants": constants(),
        "small": small,
        "wa2": np.concatenate([v["gla_wa2"].transpose(1, 0, 2), np.zeros((BROW - RANK, L, 256), np.float32),
                               v["gla_ba"][None]], axis=0),
        "k_cache": v["cache_k"].transpose(0, 3, 4, 1, 2).reshape(L, P, NS, P),
        "v_cache": v["cache_v"].transpose(0, 2, 1, 3, 4).reshape(L, P, NS, P),
        "state": v["state_gla"].reshape(L, NS, 2, 2, GK, GV).transpose(0, 3, 4, 1, 2, 5).reshape(L, P, NS, 2, GV),
    }
    arrays = {k: np.ascontiguousarray(a) for k, a in arrays.items()}
    outs = {"yT": (P, KT, N), "kp": (L, P, P), "vp": (L, P, P), "sp": (L, P, 2, GV), "ks": (L, P, NS, P),
            "vs": (L, P, NS, P), "ss": (L, P, NS, 2, GV)}
    nc = bacc.Bacc("TRN2", target_bir_lowering=False, num_devices=1)
    args = [nc.dram_tensor(k, a.shape, mybir.dt.from_np(a.dtype), kind="ExternalInput").ap() for k, a in arrays.items()]
    args += [nc.dram_tensor(k, s, F32, kind="ExternalOutput").ap() for k, s in outs.items()]
    build(nc, *args)
    r = run(nc, [arrays], core_ids=[0]).results[0]
    y = r["yT"].transpose(2, 1, 0).reshape(N, D)

    def token_rows(a):
        return a.transpose(0, 2, 1).reshape(L, 1, P, NKV, HD)

    return (y[None, 0:T], y[T:N, None],
            token_rows(r["kp"]), token_rows(r["vp"]),
            r["sp"].reshape(L, 2, GK, 2, GV).transpose(0, 3, 1, 2, 4).reshape(L, 1, GH, GK, GV),
            r["ks"].transpose(0, 2, 3, 1).reshape(L, NS, P, NKV, HD),
            r["vs"].transpose(0, 2, 1, 3).reshape(L, NS, P, NKV, HD),
            r["ss"].reshape(L, 2, GK, NS, 2, GV).transpose(0, 3, 4, 1, 2, 5).reshape(L, NS, GH, GK, GV))
```

```python
from contextlib import ExitStack

import numpy as np

import concourse.bass as bass
from concourse import mybir

F32 = mybir.dt.float32
F32R = mybir.dt.float32r
I32 = mybir.dt.int32
ACT = mybir.ActivationFunctionType
ALU = mybir.AluOpType
AX = mybir.AxisListType.X

P = 128
D = 1024
KT = D // P
T = 512
NS = 8
N = T + NS
HN = N // 2
L = 2
NB = T // P
NH, NKV, HD = 8, 2, 64
GH, GK, GV = 4, 64, 128
RANK = 16
BROW = 32
E = 8
FE = 11
SUB = 32
NI = P // SUB
EPS = 1e-6
SLOTS = 3
PAIRS = 3
ADA = 6 * KT
GRP = 3
GROUPS = ADA // GRP
ASLOTS = 4
CHUNK = 4
CYCLE = GRP * ASLOTS
W1 = 15
W1A = 6
W3 = 20
W3A = 6
Z_GA, Z_Q, Z_K, Z_V, Z_GQ, Z_GK, Z_GV = 0, 1, 5, 6, 7, 9, 11
EXP_SLABS = 3 * FE
CAP = 224
CT = CAP // 2
ITEM_JOBS = 1 + FE + 2 + KT + KT
RING = 11
LAYER_SLABS = [W1 + W3 + 8 + 8 + 2 * EXP_SLABS, W1 + W3 + 8 + 8 + E * EXP_SLABS]
TOTAL = L * ADA + sum(LAYER_SLABS)
LEAD = 2

C_ID, C_ONE, C_BLK, C_U, C_M, C_BIAS, C_BS, C_RANK, C_SLOT, C_J = 0, 128, 256, 384, 512, 640, 2688, 2824, 2832, 2832 + CAP
C_END = C_J + 9
S_ADAB = 0
S_N = S_ADAB + L * ADA
S_QK = S_N + L * 2 * KT
S_GN = S_QK + L * 2
S_SINK = S_GN + L
S_SINKC = S_SINK + L * NH
S_RW = S_SINKC + L
S_RB = S_RW + KT * E
S_END = S_RB + E


def build(nc, xT, cT, wst, cst, sml, wa2, kcT, vc, st, yT, kp, vp, sp_, ks, vs, ss):
    ctx = ExitStack()
    with ctx:
        sems = {}
        def sem(name):
            if name not in sems:
                sems[name] = ctx.enter_context(nc.semaphore(name))
            return sems[name]

        pos = [(nc.sbuf_base + 31) // 32 * 32]

        def at(name, shape, dt, offset):
            return nc.alloc_sbuf_tensor_at(name, shape, dt, offset=offset)

        def fixed(name, shape, dt=F32):
            t = at(name, shape, dt, pos[0])
            n = 4 * int(np.prod(shape[1:]))
            pos[0] += (n + 31) // 32 * 32
            return t

        x = fixed("x", [P, KT, N])
        H0 = pos[0]
        Hh = fixed("Hh", [P, KT, N], F32R)
        Hl = fixed("Hl", [P, KT, N], F32R)
        raw = fixed("raw", [P, SLOTS, 1024])
        wh = fixed("wh", [P, SLOTS, 1024], F32R)
        wl = fixed("wl", [P, SLOTS, 1024], F32R)
        B0 = pos[0]
        Bh = fixed("Bh", [P, 8, N], F32R)
        Bl = fixed("Bl", [P, 8, N], F32R)
        Z0 = pos[0]
        z = fixed("z", [P, W1, N])
        G0 = pos[0]
        g = fixed("g", [P, W3, N])
        cs = fixed("cs", [P, C_END])
        sm = fixed("sm", [P, S_END])
        wa = fixed("wa", [BROW + 1, L, 256])
        mod = fixed("mod", [P, L, ADA, 9])
        eps = fixed("eps", [P, 1])
        qg8 = fixed("qg8", [P, L])
        osmp = fixed("osmp", [P, GH, NS])
        xs_tmp = fixed("xs_tmp", [P, 2, NS])
        mx = fixed("mx", [P, NH]); nmx = fixed("nmx", [P, 2, NH]); sk = fixed("sk", [P, 2, NH])
        esk = fixed("esk", [P, 2, NH]); rs = fixed("rs", [P, 2, NH]); den = fixed("den", [P, NH])
        rec = fixed("rec", [P, NH])
        assert pos[0] <= nc.sbuf_usable_end, pos[0]

        c_in = at("c_in", [P, KT, 9], F32, Z0 + 71680)
        c_act = at("c_act", [P, KT, 9], F32, Z0 + 71968)
        c_parts = at("c_parts", [P, KT, 18], F32R, pos[0])
        assert pos[0] + 576 <= nc.sbuf_usable_end
        ada_split = [at(f"ada_split{j}", [P, 2, 1024], F32R, (B0, H0)[j] + 24576) for j in range(2)]
        ada_split = [(t[:, 0, :], t[:, 1, :]) for t in ada_split] + [(wh[:, SLOTS - 1, :], wl[:, SLOTS - 1, :])]
        ada_row = at("ada_row", [18, 3, 512], F32, Z0 + 65536)
        ada = [at(f"ada{j}", [P, GRP, 1024], F32, (H0 if j < 2 else B0) + j % 2 * 12288) for j in range(ASLOTS)]
        sq = at("sq", [P, KT, N], F32, Z0)
        rt = at("rt", [P, N], F32, Z0 + 16640)
        ri = at("ri", [P, N], F32, Z0 + 18720)
        tn = at("tn", [P, KT, N], F32, G0)
        hf = at("hf", [P, KT, N], F32, G0 + 16640)
        hidh = at("hidh", [P, FE, N], F32R, Z0)
        hidl = at("hidl", [P, FE, N], F32R, Z0 + 22880)
        sg = at("sg", [P, 2, N], F32, Z0 + 45760)
        hm = at("hm", [P, 3, N], F32, Z0 + 49920)
        XE = at("XE", [P, 2, KT, CAP], F32R, H0)
        ST = at("ST", [P, 2, N], F32R, H0 + 14336)
        Sel = at("Sel", [P, NB + 1, CAP], F32R, H0 + 18496)
        sgm = at("sgm", [P, 3, CAP], F32, H0 + 22976)
        hmm = at("hmm", [P, 3, CAP], F32, H0 + 25664)
        slotw = at("slotw", [P, 2], F32, H0 + 28352)
        slotpos = at("slotpos", [P, NB + 1, E + 1], F32, H0 + 28384)
        chosen = at("chosen", [P, NB + 1, E], F32, H0 + 28576)
        sweeps = at("sweeps", [P, 1], I32, H0 + 28736)
        cnt = [at(f"cnt{i}", [P, 1], F32, H0 + 28768 + 32 * i) for i in range(4)]
        more = at("more", [P, RING - SLOTS, 1024], F32, B0)
        hTh = at("hTh", [P, NB + 1, D], F32R, Z0)
        hTl = at("hTl", [P, NB + 1, D], F32R, Z0 + 20480)
        heh = at("heh", [P, FE, CAP], F32R, Z0 + 40960)
        hel = at("hel", [P, FE, CAP], F32R, Z0 + 50816)
        Yh = at("Yh", [P, 2, D], F32R, Z0 + 40960)
        Yl = at("Yl", [P, 2, D], F32R, Z0 + 49152)
        lg = at("lg", [P, 5, E], F32, Z0 + 65536)
        rr = [at(f"rr{i}", [P, 5, E], F32, Z0 + 65536 + 160 * (i + 1)) for i in range(8)]
        r1 = [at(f"r1{i}", [P, 5, 1], F32, Z0 + 65536 + 1440 + 32 * i) for i in range(10)]
        qsq = at("qsq", [P, 5, N], F32, G0)
        qrt = at("qrt", [P, 5, N], F32, G0 + 10400)
        sc = at("sc", [P, NH, 256], F32, G0)
        sc2 = at("sc2", [P, NH, 256], F32, B0 + 8320)
        scb = (sc, sc2)
        PT = at("PT", [P, 4, 512], F32, G0 + 8192)
        vtok = at("vtok", [P, NB, P], F32, G0 + 16384)
        kc = at("kc", [P, NS, 129], F32, G0 + 20800)
        vcs = at("vcs", [P, NS, P], F32, G0 + 24928)
        Sst = at("Sst", [P, NS, 2, GV], F32, G0 + 29024)
        scs = at("scs", [NS, NS, 129], F32, G0 + 37216)
        qs = at("qs", [P, NS, NH], F32, G0)
        pT = at("pT", [P, NS, NH], F32, G0 + 256)
        prow = at("prow", [1, NS, NH], F32, G0 + 512)
        vrow = at("vrow", [1, NS, P], F32, G0 + 768)
        smx = at("smx", [NS, NS], F32, G0 + 4864)
        sts = at("sts", [NS, NS], F32, G0 + 4896)
        ses = at("ses", [NS, NS], F32, G0 + 4928)
        srs = at("srs", [NS, NS], F32, G0 + 4960)
        sdn = at("sdn", [NS, NS], F32, G0 + 4992)
        srec = at("srec", [NS, NS], F32, G0 + 5024)
        kts = at("kts", [NS, 256], F32, G0 + 5120)
        vts = at("vts", [NS, 512], F32, G0 + 6144)
        kms = at("kms", [NS, NS, 256], F32, G0 + 8192)
        las = at("las", [NS, 256], F32, G0 + 16384)
        lab = at("lab", [NS, 256], F32, G0 + 17408)
        lac = at("lac", [NS, 256], F32, G0 + 18432)
        dcs = at("dcs", [P, 2, NS], F32, G0 + 19456)
        la = at("la", [P, NB, 256], F32, Z0 + 2080)
        lt = at("lt", [P, NB, 256], F32, Z0 + 2080 + 4096)
        cum = at("cum", [P, 2, T], F32, G0)
        qt = at("qt", [P, 2, T], F32, G0 + 4096)
        qe = at("qe", [P, 2, T], F32, G0 + 8192)
        KW = SUB * NI * (NI + 1) // 2
        kt = at("kt", [P, 2, NB, KW], F32, G0 + 12288)
        kd = at("kd", [P, 2, T], F32, G0 + 22528)
        kdt = at("kdt", [P, NB, 256], F32, G0 + 26624)
        att = at("att", [P, NB, GH, P], F32, G0 + 30720)
        dec = at("dec", [P, 2, NB], F32, G0 + 38912)
        gvt = at("gvt", [P, NB, 512], F32, B0 + 8320)
        S = at("S", [P, NB, 2, 2, GV], F32, B0 + 16640 + 8320)
        ta = at("ta", [P, 2, N], F32, Z0 + 27040)
        mf = at("mf", [P, KT, N], F32, Z0 + 10400)

        ident = cs[:, C_ID:C_ID + P]
        ones = cs[:, C_ONE:C_ONE + P]
        blk = cs[:, C_BLK:C_BLK + P]
        U16 = cs[:, C_U:C_U + P]
        MSK = cs[:, C_M:C_M + P]
        biasT = cs[:, C_BIAS:C_BIAS + 2048].rearrange("p (h s) -> p h s", h=NH)
        biasS = cs[0:NS, C_BS:C_BS + 129]
        rank8 = cs[:, C_RANK:C_RANK + E]
        fold = cs[0:18, C_J:C_J + 9]
        slot_ids = cs[:, C_SLOT:C_SLOT + CAP]

        ps = ctx.enter_context(nc.psum_tensor("ps", [P, 8, 512], F32))

        def pair(p):
            return ps[:, 2 * p:2 * p + 2, 0:HN]

        def two(ap):
            return ap.rearrange("p (a b) -> p a b", a=2)

        base = {}
        jobs = {}
        njobs = {}
        s = L * ADA
        j = 0
        for l in range(L):
            ne = 2 if l == 0 else E
            for name, ns_, nj in (("n1", 0, 1), ("w1", W1A, W1A), ("qk", 0, 5),
                                  ("w1b", W1 - W1A, W1 - W1A), ("w3", W3A, W3A), ("gn", 0, 4),
                                  ("w3b", W3 - W3A, W3 - W3A),
                                  ("br", 8, 16), ("wo", 8, 8), ("n2", 0, 0), ("ht", 0, NB + 1 if l else 0),
                                  ("xe", 0, KT if l else 0), ("ff", ne * EXP_SLABS, ne * 30)):
                base[name, l] = s
                jobs[name, l] = j
                njobs[name, l] = nj
                s += ns_
                j += nj
        assert s == TOTAL

        def slot(s0, k, i=0):
            return (s0 + k) % SLOTS, r_use(s0, k, i)

        def r_use(s0, k, i=0):
            return (s0 - L * ADA + k) // SLOTS + i

        def psj(j0, k, i=0):
            return (j0 + k) % PAIRS, (j0 + k) // PAIRS + i

        def products_read(eng, name, l):
            end = jobs[name, l] + njobs[name, l]
            for p in range(PAIRS):
                if (end - p + 2) // PAIRS:
                    eng.wait_ge(acc_free[p], (end - p + 2) // PAIRS)

        raw_full = [sem(f"raw_full{i}") for i in range(SLOTS)]
        ada_full = [sem(f"ada_full{i}") for i in range(ASLOTS)]
        ada_next = [sem(f"ada_next{i}") for i in range(2)]
        hi_made = [sem(f"hi_made{i}") for i in range(SLOTS)]
        split_made = [sem(f"split_made{i}") for i in range(SLOTS)]
        split_used = [sem(f"split_used{i}") for i in range(SLOTS)]
        acc_full = [sem(f"acc_full{i}") for i in range(PAIRS)]
        acc_free = [sem(f"acc_free{i}") for i in range(PAIRS)]


        more_full = [sem(f"more_full{i}") for i in range(RING)]

        def ring(f):
            return raw[:, f, :] if f < SLOTS else more[:, f - SLOTS, :]

        PER_LAYER = dict(sq_made=2 * KT, tn_made=2 * KT, hf_made=2 * KT, hfs_made=2, Hh_made=2 * KT, H_made=2 * KT,
                         qsq_made=5, qk_made=5, kc_in=16, vc_in=16, st_in=16, cache_out=5 * 16, state_out=16, S_out=2 * 16,
                         sc_done=NB, soft_in=NB, exp_done=NB, p_made=NB, sc_read=NB, pt_done=NB, pta_copied=NB, ptb_copied=NB - 1,
                         av_done=NB, avh_made=NB, av_read=NB, pT_made=2, dah_made=2, gvt_made=2, S_made=NB,
                         osq_made=GH, og_made=GH, Bh_made=GH, B_made=GH, mf_made=KT, Mh_made=KT, M_made=KT,
                         xs_made=3 * KT, hidh_made=2 * FE, hid_made=2 * FE,
                         rl_done=0, rt_exp_in=0, rt_exp=0)

        def upto(name, l, n):
            return n + l * PER_LAYER.get(name, 1)

        block = ctx.enter_context(nc.Block())

        PER = (CYCLE, ADA // 2)

        def ada_slot(l, m):
            return 2 + m // GRP % 2 if l else m // GRP % ASLOTS

        def ada_pair(l, m):
            return ada_split[0 if l else m % 3]

        def ada_bank(l, m):
            return 6 if l else (6, 4, 5)[m // CHUNK % 3]

        def ada_slabs(l, i, m):
            return i * PER[l] + (ADA * l + m)

        def ada_chunks(l, i, m):
            return i * (PER[l] // CHUNK) + (ADA // CHUNK * l + m // CHUNK)

        def ada_spot(k):
            return 3 * (k // 4) + k % 4 if k % 4 < 3 and k < 32 else None

        def ada_landed(l, j):
            return ada_next[j - 2] if l else ada_full[j]

        def load_ada(eng, l, group, j):
            first = group * GRP + l * ADA
            eng.dma_start(ada[j][:], wst[bass.ds(first, GRP), :, :].rearrange("s p c -> p s c")).then_inc(ada_landed(l, j), 16)

        @block.sync
        def _(sp):
            def slab(idx, j):
                sp.dma_start(raw[:, j, :], wst[idx, :, :]).then_inc(raw_full[j], 16)

            for j in range(ASLOTS):
                load_ada(sp, 0, j, j)
            with sp.Fori(1, GROUPS // ASLOTS) as i:
                for j in range(ASLOTS):
                    sp.wait_ge(sem("ada_low"), i * CYCLE + (GRP * (j + 1) - CYCLE))
                    load_ada(sp, 0, i * ASLOTS + j, j)
            for j in range(SLOTS):
                slab(L * ADA + j, j)
            ff = base["ff", L - 1]
            nr = (ff - L * ADA) // SLOTS
            with sp.Fori(1, nr) as i:
                for j in range(SLOTS):
                    sp.wait_ge(split_made[j], i)
                    slab(i * SLOTS + (L * ADA + j), j)
            for j in range(LEAD):
                sp.wait_ge(split_made[j], nr)
                slab(ff + j, j)

            def expert_slab(e, k):
                sp.dma_start(ring(k % RING), wst[ff + LEAD + EXP_SLABS * e + k, :, :]).then_inc(more_full[k % RING], 16)

            def slot_split(k, i):
                sp.wait_ge(split_made[(k - RING + LEAD) % SLOTS], r_use(ff, k - RING + LEAD, i * FE) + 1)

            sp.wait_ge(sem("ring_open"), 1)
            for k in range(RING):
                expert_slab(0, k)
            for k in range(RING, EXP_SLABS):
                slot_split(k, 0)
                expert_slab(0, k)
            sp.wait_ge(sem("sweeps_made"), 1)
            n_sweeps = sp.value_load(sweeps[0:1, 0:1], min_val=1, max_val=3)
            with sp.Fori(1, n_sweeps * E) as i:
                for k in range(EXP_SLABS):
                    slot_split(k, i)
                    expert_slab(i % E, k)

        @block.gpsimd
        def _(pool):
            pool.dma_start(c_in[:], cT).then_inc(sem("c_landed"), 16)
            pool.dma_start(x[:], xT).then_inc(sem("x_in"), 16)
            pool.dma_start(sm[:], sml).then_inc(sem("small_in"), 16)
            pool.dma_start(cs[:], cst).then_inc(sem("const_in"), 16)
            pool.dma_start(wa[:], wa2).then_inc(sem("wa_in"), 16)
            outs = 0
            for l in range(L):
                pool.wait_ge(sem("Hh_made"), upto("Hh_made", l, KT))
                pool.wait_ge(sem("H_made"), upto("H_made", l, KT))
                pool.dma_start(kc[:, :, 0:P], kcT[l]).then_inc(sem("kc_in"), 16)
                pool.dma_start(vcs[:], vc[l]).then_inc(sem("vc_in"), 16)
                pool.dma_start(Sst[:], st[l]).then_inc(sem("st_in"), 16)
                pool.wait_ge(sem("qk_made"), upto("qk_made", l, 5))
                pool.dma_start(kp[l], z[:, Z_K, T - P:T]).then_inc(sem("cache_out"), 16)
                products_read(pool, "w1b", l)
                pool.dma_start(vp[l], z[:, Z_V, T - P:T]).then_inc(sem("cache_out"), 16)
                pool.wait_ge(sem("kc_made"), upto("kc_made", l, 1))
                pool.dma_start(ks[l], kc[:, :, 1:1 + P]).then_inc(sem("cache_out"), 16)
                pool.wait_ge(sem("vc_in"), upto("vc_in", l, 16))
                pool.dma_start(vs[l, 0:P - 1], vcs[1:P, :, :]).then_inc(sem("cache_out"), 16)
                pool.wait_ge(sem("vrow_made"), upto("vrow_made", l, 1))
                pool.dma_start(vs[l, P - 1:P], vrow[:]).then_inc(sem("cache_out"), 16)
                pool.wait_ge(sem("Sst_made"), upto("Sst_made", l, 1))
                pool.dma_start(ss[l], Sst[:]).then_inc(sem("state_out"), 16)
                pool.wait_ge(sem("S_made"), upto("S_made", l, NB))
                for r in range(2):
                    hp = slice(64 * r, 64 * r + 64)
                    pool.dma_start(sp_[l, hp], S[hp, NB - 1, :, r, :]).then_inc(sem("S_out"), 16)
                if l == 0:
                    pool.wait_ge(sem("B_read"), 1)
                    for j in (2, 3):
                        load_ada(pool, 1, j - 2, j)
                    with pool.Fori(1, GROUPS // 2) as i:
                        for j in (2, 3):
                            pool.wait_ge(sem("ada_low"), i * (2 * GRP) + (ADA + GRP * (j - 1) - 2 * GRP))
                            load_ada(pool, 1, i * 2 + (j - 2), j)
            pool.wait_ge(sem("x_final"), 1)
            pool.dma_start(yT, x[:]).then_inc(sem("y_out"), 16)
            for l in range(L):
                pool.wait_ge(sem("cache_out"), upto("cache_out", l, 5 * 16))
                pool.wait_ge(sem("state_out"), upto("state_out", l, 16))
                pool.wait_ge(sem("S_out"), upto("S_out", l, 32))
            pool.wait_ge(sem("y_out"), 16)

        @block.tensor
        def _(pe):
            def blocks(todo):
                for sl, b, xh, xl, p, first, last, s_first, s_last in todo:
                    w_h, w_l = wh[:, sl, b * P:b * P + P], wl[:, sl, b * P:b * P + P]
                    for h in range(2):
                        out = ps[:, 2 * p + h, 0:HN]
                        cols = slice(h * HN, h * HN + HN)
                        for q, (w, v) in enumerate(((w_h, xh), (w_h, xl), (w_l, xh))):
                            mm = pe.matmul(out, w, v[:, cols], start=first and q == 0, stop=last and q == 2)
                            if h == 0 and q == 0 and s_first is not None:
                                mm.then_inc(s_first, 1)
                    if last and s_last is not None:
                        mm.then_inc(s_last, 1)

            def slab_ready(s0, k, i):
                sl, _ = slot(s0, k)
                pe.wait_ge(split_made[sl], r_use(s0, k, i) + 1)
                return sl, split_used[(sl - 1) % SLOTS]

            def free_pair(j0, k, i=0):
                p, u = psj(j0, k, i)
                if not (isinstance(u, int) and u == 0):
                    pe.wait_ge(acc_free[p], u)
                return p

            def product8(s0, j0, k, i, xh, xl):
                sl, before = slab_ready(s0, k, i)
                p = free_pair(j0, k, i)
                blocks([(sl, b, xh[:, b, :], xl[:, b, :], p, b == 0, b == KT - 1, before if b == 0 else None, acc_full[p])
                        for b in range(KT)])

            def first_product(s0, j0, xh, xl, made, seen):
                sl, before = slab_ready(s0, 0, 0)
                p = free_pair(j0, 0)
                for b in range(KT):
                    pe.wait_ge(sem(made), seen + b + 1)
                    blocks([(sl, b, xh[:, b, :], xl[:, b, :], p, b == 0, b == KT - 1, before if b == 0 else None, acc_full[p])])

            def products8(name, l, n, xh, xl, made=None, seen=0):
                s0, j0 = base[name, l], jobs[name, l]
                peel = 1 if made or j0 < PAIRS else 0
                for k in range(3 * peel):
                    if k == 0 and made:
                        first_product(s0, j0, xh, xl, made, upto(made, l, seen))
                    else:
                        product8(s0, j0, k, 0, xh, xl)
                with pe.Fori(peel, n // 3) as i:
                    for j in range(3):
                        product8(s0, j0, j, i, xh, xl)
                for k in range(n // 3 * 3, n):
                    product8(s0, j0, k, 0, xh, xl)

            def plain(out_pair, lhsT, rhs, first, last):
                for h in range(2):
                    mm = pe.matmul(ps[0:lhsT.shape[1], 2 * out_pair + h, 0:HN], lhsT, rhs[:, h * HN:h * HN + HN],
                                   start=first, stop=last)
                return mm

            def block_rows(n):
                return P if n < NB else NS

            def gather(job0, i, number):
                pe.wait_ge(sem("Sel_made"), number)
                for m in range(KT):
                    p, u = psj(job0, m)
                    pe.wait_ge(acc_free[p], u + i * (ITEM_JOBS // PAIRS))
                    for q, part in enumerate((hTh, hTl)):
                        for n in range(NB + 1):
                            rows = block_rows(n)
                            mm = pe.matmul(ps[:, 2 * p + q, 0:CAP], part[0:rows, n, m * P:m * P + P], Sel[0:rows, n, :],
                                           start=n == 0, stop=n == NB)
                    mm.then_inc(acc_full[p], 1)

            def experts(l):
                def to_tokens(n):
                    rows = block_rows(n)
                    p = free_pair(jobs["ht", l], n)
                    for k in range(KT):
                        mm = pe.transpose(ps[0:rows, 2 * p + k // 4, (k % 4) * P:(k % 4) * P + P],
                                          hf[:, k, n * P:n * P + rows], ident)
                    mm.then_inc(acc_full[p], 1)

                for n in range(PAIRS):
                    to_tokens(n)
                pe.wait_ge(sem("chosen_made"), 1)
                for n in range(NB + 1):
                    rows = block_rows(n)
                    for b in range(n):
                        pe.matmul(ps[0:rows, 7, n * E:n * E + E], ones[:, 0:rows], chosen[:, b, :], start=b == 0, stop=False)
                    pe.matmul(ps[0:rows, 7, n * E:n * E + E], MSK[0:rows, 0:rows], chosen[0:rows, n, :], start=n == 0, stop=True)
                for n in range(NB + 1):
                    rows = block_rows(n)
                    mm = pe.matmul(ps[:, 7, (NB + 1) * E:(NB + 2) * E], ones[0:rows, :], chosen[0:rows, n, :],
                                   start=n == 0, stop=n == NB)
                mm.then_inc(sem("rank_done"), 1)
                for n in range(PAIRS, NB + 1):
                    to_tokens(n)
                products_read(pe, "ht", l)
                gather(jobs["xe", l], 0, 1)
                products_read(pe, "xe", l)
                pe.wait_ge(sem("sweeps_made"), 1)
                n_sweeps = pe.value_load(sweeps[0:1, 0:1], min_val=1, max_val=3)
                s0, j0 = base["ff", l], jobs["ff", l]
                per_pair = ITEM_JOBS // PAIRS
                with pe.Fori(0, n_sweeps) as c, pe.Fori(0, E) as e:
                    i = c * E + e

                    def open_pair(k):
                        p, u = psj(j0, k)
                        pe.wait_ge(acc_free[p], u + i * per_pair)
                        return p

                    p = open_pair(0)
                    for t in range(2):
                        cols = slice(t * CT, t * CT + CT)
                        for n in range(NB + 1):
                            rows = block_rows(n)
                            pe.matmul(ps[0:CT, 7, t:t + 1], Sel[0:rows, n, cols].bitcast(F32),
                                      rr[7][0:rows, n, bass.ds(e, 1)], start=n == 0, stop=n == NB)
                        pe.transpose(ps[0:CT, 6, t * NS:t * NS + NS], Sel[0:NS, NB, cols].bitcast(F32), ident[0:NS, 0:NS])
                    for t in range(2):
                        for n in range(NB):
                            mm = pe.transpose(ps[0:CT, 2 * p + t, n * P:n * P + P],
                                              Sel[:, n, t * CT:t * CT + CT].bitcast(F32), ident)
                    mm.then_inc(acc_full[p], 1)
                    for m in range(FE):
                        p = open_pair(1 + m)
                        for q in range(2):
                            sl, before = slab_ready(s0, 2 * m + q, i * FE)
                            for b in range(KT):
                                for r, (w, v) in enumerate(((wh, 0), (wh, 1), (wl, 0))):
                                    mm = pe.matmul(ps[:, 2 * p + q, 0:CAP], w[:, sl, b * P:b * P + P], XE[:, v, b, :],
                                                   start=b == 0 and r == 0, stop=b == KT - 1 and r == 2)
                                    if b == 0 and r == 0:
                                        mm.then_inc(before, 1)
                        mm.then_inc(acc_full[p], 1)
                    p2 = [open_pair(1 + FE + t) for t in range(2)]
                    for k in range(FE):
                        pe.wait_ge(sem("hid_made"), upto("hid_made", l, i * FE + k + 1))
                        sl, before = slab_ready(s0, 2 * FE + k, i * FE)
                        for t in range(2):
                            for q in range(2):
                                for r, (v, w) in enumerate(((heh, wh), (heh, wl), (hel, wh))):
                                    mm = pe.matmul(ps[0:CT, 2 * p2[t] + q, :], v[:, k, t * CT:t * CT + CT],
                                                   w[:, sl, q * 512:q * 512 + 512], start=k == 0 and r == 0,
                                                   stop=k == FE - 1 and r == 2)
                                    if t == 0 and q == 0 and r == 0:
                                        mm.then_inc(before, 1)
                            if k == FE - 1:
                                mm.then_inc(acc_full[p2[t]], 1)
                    gather(j0 + 3 + FE, i, i + 2)
                    for m in range(KT):
                        p = open_pair(3 + FE + KT + m)
                        for h in range(2):
                            for t in range(2):
                                for r, v in enumerate((Yh, Yl)):
                                    mm = pe.matmul(ps[:, 2 * p + h, 0:HN], v[0:CT, t, m * P:m * P + P],
                                                   ST[0:CT, t, h * HN:h * HN + HN], start=t == 0 and r == 0,
                                                   stop=t == 1 and r == 1)
                        mm.then_inc(acc_full[p], 1)

            def modulation(l, i, m):
                bank = ada_bank(l, m)
                if m % CHUNK == 0 and (l or not isinstance(i, int)):
                    pe.wait_ge(sem("row_made"), ada_chunks(l, i, m) - (0 if l else 2))
                pe.wait_ge(sem("ada_low"), ada_slabs(l, i, m) + 1)
                for u in range(2):
                    for v in range(2):
                        first, last = m % CHUNK + u + v == 0, m % CHUNK + u + v == CHUNK + 1
                        mm = pe.matmul(ps[0:18, bank, :], c_parts[:, m % CHUNK * 2 + u, :],
                                       ada_pair(l, m)[v][:, u * 512:u * 512 + 512], start=first, stop=last)
                mm.then_inc(sem("ada_product"), 1)

            def turn(l, i, m):
                pe.wait_ge(sem("row_made"), ada_chunks(l, i, m) + 1)
                for q in range(4):
                    c0 = ada_chunks(0, i, m) * 36 if l == 0 else i * (36 * PER[1] // CHUNK) + 36 * (m // CHUNK)
                    mm = pe.matmul(ps[:, 7, bass.ds(c0 + 9 * q, 9)], ada_row[:, m // CHUNK % 3, q * P:q * P + P], fold,
                                   start=True, stop=True)
                mm.then_inc(sem("ada_turned"), 1)

            def modulation_cycle(i):
                for m in range(CYCLE):
                    modulation(0, i, m)
                    if m % CHUNK == 3 and not (m == 3 and isinstance(i, int)):
                        if m == 7 and isinstance(i, int):
                            pe.wait_ge(sem("const_in"), 16)
                        turn(0, i, m - 4)

            for l in range(L):
                def norm_sum(name, which):
                    j0 = jobs[name, l]
                    p = free_pair(j0, 0)
                    for k in range(KT):
                        pe.wait_ge(sem("sq_made"), upto("sq_made", l, which * KT + k + 1))
                        mm = plain(p, ones, sq[:, k, :], k == 0, k == KT - 1)
                    mm.then_inc(acc_full[p], 1)

                if l == 0:
                    pe.wait_ge(sem("c_made"), 1)
                    modulation_cycle(0)
                norm_sum("n1", 0)
                if l == 0:
                    with pe.Fori(1, GROUPS // ASLOTS) as i:
                        modulation_cycle(i)
                    turn(0, GROUPS // ASLOTS - 1, CYCLE - 1)
                products8("w1", l, W1A, Hh, Hl, "H_made", 0)
                for i in range(5):
                    p = free_pair(jobs["qk", l], i)
                    pe.wait_ge(sem("qsq_made"), upto("qsq_made", l, i + 1))
                    plain(p, blk, qsq[:, i, :], True, True).then_inc(acc_full[p], 1)
                products8("w1b", l, W1 - W1A, Hh, Hl)
                products_read(pe, "w1b", l)
                pe.wait_ge(sem("mod_made"), 2 * l + 2)
                for n in range(NB):
                    mm = pe.transpose(ps[:, 6, n * P:n * P + P], z[:, Z_V, n * P:n * P + P], ident)
                mm.then_inc(sem("vt_done"), 1)
                pe.wait_ge(sem("qk_made"), upto("qk_made", l, 5))
                def scores(n):
                    W = 2 * P if n else P
                    if n:
                        pe.wait_ge(sem("sc_read"), upto("sc_read", l, n))
                    for kv in range(NKV):
                        hp = slice(64 * kv, 64 * kv + 64)
                        for t in range(4):
                            mm = pe.matmul(ps[:, 2 * kv + t // 2, (t % 2) * 256:(t % 2) * 256 + W],
                                           z[hp, Z_Q + t, n * P:n * P + P], z[hp, Z_K, (n + 1) * P - W:(n + 1) * P],
                                           start=True, stop=True)
                    mm.then_inc(sem("sc_done"), 1)

                scores(0)
                scores(1)
                for n in range(NB):
                    pe.wait_ge(sem("p_made"), upto("p_made", l, n + 1))
                    if n:
                        pe.wait_ge(sem("av_read"), upto("av_read", l, n))
                    for c in range(2 if n else 1):
                        for h in range(NH):
                            mm = pe.transpose(ps[:, 4 + 2 * c + h // 4, (h % 4) * P:(h % 4) * P + P],
                                              scb[n % 2][:, h, c * P:c * P + P], ident)
                    mm.then_inc(sem("pt_done"), 1)
                    if n + 2 < NB:
                        scores(n + 2)
                    if n == 0:
                        pe.wait_ge(sem("vtok_made"), upto("vtok_made", l, 1))
                    pe.wait_ge(sem("pta_copied"), upto("pta_copied", l, n + 1))
                    if n:
                        pe.wait_ge(sem("ptb_copied"), upto("ptb_copied", l, n))
                    nc_ = 2 if n else 1
                    for kv in range(NKV):
                        for c in range(nc_):
                            mm = pe.matmul(ps[64 * kv:64 * kv + 64, 4, :], vtok[:, n - (nc_ - 1) + c, 64 * kv:64 * kv + 64],
                                           PT[:, 2 * c + kv, :], start=c == 0, stop=c == nc_ - 1)
                    mm.then_inc(sem("av_done"), 1)
                pe.wait_ge(sem("av_read"), upto("av_read", l, NB))
                pe.wait_ge(sem("qs_made"), upto("qs_made", l, 1))
                pe.wait_ge(sem("kc_made"), upto("kc_made", l, 1))
                for b in range(NS):
                    mm = pe.matmul(ps[0:NS, b // 2, (b % 2) * 256:(b % 2) * 256 + 129], qs[:, b, :], kc[:, b, :],
                                   start=True, stop=True)
                mm.then_inc(sem("dsc_done"), 1)
                for q in range(2):
                    pe.transpose(ps[0:NS, 4, q * P:q * P + P], z[:, Z_GK + q, T:N], ident)
                for h in range(GH):
                    mm = pe.transpose(ps[0:NS, 5, h * P:h * P + P], z[:, Z_GV + h, T:N], ident)
                mm.then_inc(sem("kvt_done"), 1)
                if l == 0:
                    pe.wait_ge(sem("wa_in"), 16)
                pe.wait_ge(sem("ones_made"), upto("ones_made", l, 1))
                pe.matmul(ps[0:NS, 6, 0:256], z[0:BROW + 1, Z_GA, T:N], wa[:, l, :], start=True, stop=True
                          ).then_inc(sem("dlg_done"), 1)
                pe.wait_ge(sem("dp_made"), upto("dp_made", l, 1))
                for b in range(NS):
                    pe.transpose(ps[:, 0, b * NH:b * NH + NH], scs[:, b, 0:P], ident[0:NS, 0:NS])
                for b in range(NS):
                    pe.matmul(ps[0:1, 1, b * NH:b * NH + NH], scs[:, b, P:P + 1], ident[0:NS, 0:NS], start=True, stop=True)
                for b in range(NS):
                    mm = pe.matmul(ps[0:1, 2 + b // 4, (b % 4) * P:(b % 4) * P + P], z[:, Z_V, T + b:T + b + 1], ident,
                                   start=True, stop=True)
                mm.then_inc(sem("dpt_done"), 1)
                pe.wait_ge(sem("dlg_made"), upto("dlg_made", l, 1))
                for n in range(NB):
                    mm = pe.matmul(ps[:, 6 + n // 2, (n % 2) * 256:(n % 2) * 256 + 256], z[0:BROW + 1, Z_GA, n * P:n * P + P],
                                   wa[:, l, :], start=True, stop=True)
                mm.then_inc(sem("lg_done"), 1)
                pe.wait_ge(sem("vrow_made"), upto("vrow_made", l, 1))
                pe.wait_ge(sem("pT_made"), upto("pT_made", l, 2))
                pe.wait_ge(sem("vc_in"), upto("vc_in", l, 16))
                for b in range(NS):
                    pe.matmul(ps[:, 0, b * NH:b * NH + NH], vcs[:, b, :], pT[:, b, :], start=True, stop=False)
                    mm = pe.matmul(ps[:, 0, b * NH:b * NH + NH], vrow[0:1, b, :], prow[0:1, b, :], start=False, stop=True)
                mm.then_inc(sem("dav_done"), 1)
                pe.wait_ge(sem("las_made"), upto("las_made", l, 1))
                for q in range(2):
                    mm = pe.matmul(ps[:, 1, 128 + q * NS:128 + q * NS + NS], las[:, q * P:q * P + P], ident[0:NS, 0:NS],
                                   start=True, stop=True)
                mm.then_inc(sem("dla_done"), 1)
                pe.wait_ge(sem("kms_made"), upto("kms_made", l, 1))
                pe.wait_ge(sem("da_read"), upto("da_read", l, 1))
                pe.wait_ge(sem("dcs_made"), upto("dcs_made", l, 1))
                for b in range(NS):
                    for h in range(GH):
                        q, r = h // 2, h % 2
                        c0 = (b * 2 + q) * GV
                        mm = pe.matmul(ps[64 * r:64 * r + 64, c0 // 512, c0 % 512:c0 % 512 + GV],
                                       kms[:, b, 64 * h:64 * h + 64], vts[:, h * GV:h * GV + GV], start=True, stop=True)
                mm.then_inc(sem("kv_done"), 1)
                pe.wait_ge(sem("la_made"), upto("la_made", l, 1))
                for q in range(2):
                    for n in range(NB):
                        mm = pe.matmul(ps[:, 6 + q, n * P:n * P + P], la[:, n, q * P:q * P + P], U16, start=True, stop=True)
                mm.then_inc(sem("cum_done"), 1)
                pe.wait_ge(sem("Sst_made"), upto("Sst_made", l, 1))
                for r in range(2):
                    for q in range(2):
                        for b in range(NS):
                            mm = pe.matmul(ps[:, 2 + r, q * NS + b:q * NS + b + 1], Sst[64 * r:64 * r + 64, b, q, :],
                                           z[64 * r:64 * r + 64, Z_GQ + q, T + b:T + b + 1], start=True, stop=True)
                mm.then_inc(sem("do_done"), 1)
                pe.wait_ge(sem("qe_exp"), upto("qe_exp", l, 1))
                for n in range(NB):
                    for h in range(GH):
                        mm = pe.transpose(ps[:, 4 + n, h * P:h * P + P], z[:, Z_GV + h, n * P:n * P + P], ident)
                mm.then_inc(sem("gvt_done"), 1)
                pe.wait_ge(sem("kd_made"), upto("kd_made", l, 1))
                for n in range(NB):
                    for q in range(2):
                        mm = pe.transpose(ps[:, n // 2, (n % 2) * 256 + q * P:(n % 2) * 256 + q * P + P],
                                          kd[:, q, n * P:n * P + P], ident)
                mm.then_inc(sem("kdt_done"), 1)
                pe.wait_ge(sem("osmp_made"), upto("osmp_made", l, 1))
                pe.wait_ge(sem("kdt_made"), upto("kdt_made", l, 1))
                pe.wait_ge(sem("gvt_made"), upto("gvt_made", l, 2))
                for n in range(NB):
                    for h in range(GH):
                        q, r = h // 2, h % 2
                        c0 = (n % 2) * 256 + q * GV
                        mm = pe.matmul(ps[64 * r:64 * r + 64, 2 + n // 2, c0:c0 + GV], kdt[:, n, h * 64:h * 64 + 64],
                                       gvt[:, n, h * GV:h * GV + GV], start=True, stop=True)
                mm.then_inc(sem("ds_done"), 1)
                pe.wait_ge(sem("qt_made"), upto("qt_made", l, 1))
                pe.wait_ge(sem("kt_made"), upto("kt_made", l, 1))
                for n in range(NB):
                    for h in range(GH):
                        q, r = h // 2, h % 2
                        for i in range(NI):
                            rows = SUB * (i + 1)
                            k0 = SUB * i * (i + 1) // 2
                            c0 = (n % 2) * 256 + q * P + SUB * i
                            mm = pe.matmul(ps[0:rows, 4 + 2 * r + n // 2, c0:c0 + SUB],
                                           kt[64 * r:64 * r + 64, q, n, k0:k0 + rows],
                                           qt[64 * r:64 * r + 64, q, n * P + SUB * i:n * P + SUB * i + SUB],
                                           start=True, stop=True)
                mm.then_inc(sem("at_done"), 1)
                pe.wait_ge(sem("att_made"), upto("att_made", l, 1))
                pe.wait_ge(sem("S_made"), upto("S_made", l, NB))
                pe.wait_ge(sem("qe_made"), upto("qe_made", l, 1))
                for n in range(NB):
                    for h in range(GH):
                        q, r = h // 2, h % 2
                        mm = pe.matmul(ps[:, h, n * P:n * P + P], gvt[:, n, h * GV:h * GV + GV], att[:, n, h, :],
                                       start=True, stop=n == 0)
                        if n:
                            mm = pe.matmul(ps[:, h, n * P:n * P + P], S[:, n - 1, q, r, :], qe[:, q, n * P:n * P + P],
                                           start=False, stop=True)
                mm.then_inc(sem("o_done"), 1)
                pe.wait_ge(sem("o_read"), upto("o_read", l, 1))
                products8("w3", l, W3A, Hh, Hl)
                for h in range(GH):
                    p = free_pair(jobs["gn", l], h)
                    pe.wait_ge(sem("osq_made"), upto("osq_made", l, h + 1))
                    plain(p, ones, mf[:, h, :], True, True).then_inc(acc_full[p], 1)
                products8("w3b", l, W3 - W3A, Hh, Hl)
                pe.wait_ge(sem("B_made"), upto("B_made", l, 4))
                s0, j0 = base["br", l], jobs["br", l]
                for mp in range(4):
                    for br in range(2):
                        sl, before = slab_ready(s0, 2 * mp + br, 0)
                        for m in range(2):
                            p = free_pair(j0, 4 * mp + 2 * br + m)
                            blocks([(sl, 4 * m + k, Bh[:, 4 * br + k, :], Bl[:, 4 * br + k, :], p, k == 0, k == 3,
                                     before if m == 0 and k == 0 else None, acc_full[p]) for k in range(4)])
                def square_sum(k):
                    pe.wait_ge(sem("sq_made"), upto("sq_made", l, KT + k + 1))
                    return plain(3, ones, sq[:, k, :], k == 0, k == KT - 1)

                first_product(base["wo", l], jobs["wo", l], Hh, Hl, "M_made", upto("M_made", l, 0))
                for k in range(1, KT):
                    product8(base["wo", l], jobs["wo", l], k, 0, Hh, Hl)
                    if k > 1:
                        square_sum(k - 2)
                square_sum(KT - 2)
                square_sum(KT - 1).then_inc(sem("norm_summed"), 1)
                if l == 0:
                    pe.wait_ge(sem("H_made"), upto("H_made", l, 2 * KT))
                else:
                    pe.wait_ge(sem("hf_made"), upto("hf_made", l, 2 * KT))
                    pe.wait_ge(sem("hfs_made"), upto("hfs_made", l, 2))
                    for n in range(NB + 1):
                        rows = P if n < NB else NS
                        for k in range(KT):
                            mm = pe.matmul(ps[0:rows, 6, n * E:n * E + E], hf[:, k, n * P:n * P + rows],
                                           sm[:, S_RW + k * E:S_RW + k * E + E], start=k == 0, stop=k == KT - 1)
                    mm.then_inc(sem("rl_done"), 1)
                    experts(l)
                    continue
                ne = 2
                s0, j0 = base["ff", l], jobs["ff", l]

                def next_modulation(e, k):
                    m = ada_spot(k)
                    if m is not None:
                        modulation(1, e, m)
                        if m % CHUNK == 0 and m:
                            turn(1, e, m - 1)
                    elif k == 31:
                        turn(1, e, PER[1] - 1)

                with pe.Fori(0, ne) as e:
                    for k in range(2 * FE):
                        sl, before = slab_ready(s0, k, e * FE)
                        p, u = psj(j0, k)
                        pe.wait_ge(acc_free[p], u + e * 10)
                        blocks([(sl, b, Hh[:, b, :], Hl[:, b, :], p, b == 0, b == KT - 1,
                                 before if b == 0 else None, acc_full[p]) for b in range(KT)])
                        next_modulation(e, k)
                    pe.wait_ge(sem("hid_made"), upto("hid_made", l, (e + 1) * FE))
                    for m in range(KT):
                        p, u = psj(j0, 2 * FE + m)
                        pe.wait_ge(acc_free[p], u + e * 10)
                        for k in range(FE):
                            bi = m * FE + k
                            if bi % KT == 0:
                                sl, before = slab_ready(s0, 2 * FE + bi // KT, e * FE)
                            blocks([(sl, bi % KT, hidh[:, k, :], hidl[:, k, :], p, k == 0, k == FE - 1,
                                     before if bi % KT == 0 else None, acc_full[p])])
                            if bi % KT == KT - 1:
                                next_modulation(e, 2 * FE + bi // KT)

        @block.scalar
        def _(act):
            steps = [0]

            def link(inst):
                steps[0] += 1
                inst.then_inc(sem("act_step"), 1)
                act.wait_ge(sem("act_step"), steps[0])

            def split_high(s0, k, i=0):
                sl, u = slot(s0, k + LEAD, i)
                r = r_use(s0, k + LEAD, i)
                act.wait_ge(raw_full[sl], 16 * (u + 1))
                if sl == SLOTS - 1:
                    act.wait_ge(split_used[sl], r + 1)
                elif not (isinstance(r, int) and r == 0):
                    act.wait_ge(split_used[sl], r)
                act.activation(wh[:, sl, :], raw[:, sl, :], ACT.Copy).then_inc(hi_made[sl], 1)

            def take(j0, k, i=0):
                p, u = psj(j0, k, i)
                act.wait_ge(acc_full[p], u + 1)
                return p

            def experts(l):
                act.wait_ge(sem("rt_exp_in"), 1)
                act.activation(r1[5][:], r1[4][:], ACT.Exp).then_inc(sem("rt_exp"), 1)
                for n in range(NB + 1):
                    rows = P if n < NB else NS
                    p = take(jobs["ht", l], n)
                    act.activation(hTh[0:rows, n, :].rearrange("p (a c) -> p a c", a=2), ps[0:rows, 2 * p:2 * p + 2, :], ACT.Copy
                                   ).then_inc(sem("hTh_made"), 1)

                def gathered(job0, i, m):
                    p, u = psj(job0, m)
                    act.wait_ge(acc_full[p], u + i * (ITEM_JOBS // PAIRS) + 1)
                    act.activation(XE[:, :, m, :], ps[:, 2 * p:2 * p + 2, 0:CAP], ACT.Copy).then_inc(acc_free[p], 1)

                for m in range(0, KT, 2):
                    gathered(jobs["xe", l], 0, m)
                act.wait_ge(sem("sweeps_made"), 1)
                n_sweeps = act.value_load(sweeps[0:1, 0:1], min_val=1, max_val=3)
                s0, j0 = base["ff", l], jobs["ff", l]
                per_pair = ITEM_JOBS // PAIRS
                with act.Fori(0, n_sweeps) as c, act.Fori(0, E) as e:
                    i = c * E + e

                    def full(k):
                        p, u = psj(j0, k)
                        act.wait_ge(acc_full[p], u + i * per_pair + 1)
                        return p

                    def expert_high(k):
                        f = k % RING
                        sl, _ = slot(s0, k + LEAD)
                        act.wait_ge(more_full[f], 16 * (i * (EXP_SLABS // RING) + k // RING + 1))
                        act.wait_ge(split_used[sl], r_use(s0, k + LEAD, i * FE) + (sl == SLOTS - 1))
                        act.activation(wh[:, sl, :], ring(f), ACT.Copy).then_inc(hi_made[sl], 1)

                    def hidden_high(m):
                        p, u = psj(j0, 1 + m)
                        act.wait_ge(acc_free[p], u + i * per_pair + 1)
                        act.activation(heh[:, m, :], hmm[:, m % 3, :], ACT.Copy
                                       ).then_inc(sem("hidh_made"), 1)

                    p = full(0)
                    act.activation(ST[0:CT, :, T:N], ps[0:CT, 6, 0:2 * NS].rearrange("p (t c) -> p t c", t=2), ACT.Copy)
                    act.activation(ST[0:CT, :, 0:T], ps[0:CT, 2 * p:2 * p + 2, :], ACT.Copy).then_inc(acc_free[p], 1)
                    for m in range(FE):
                        expert_high(2 * m)
                        if m:
                            hidden_high(m - 1)
                        expert_high(2 * m + 1)
                        p = full(1 + m)
                        act.activation(sgm[:, m % 3, :], ps[:, 2 * p, 0:CAP], ACT.Silu).then_inc(sem("silu_made"), 1)
                    for k in range(FE):
                        expert_high(2 * FE + k)
                        if k == 0:
                            hidden_high(FE - 1)
                    act.wait_ge(sem("slotw_made"), i + 1)
                    p2 = [full(1 + FE + t) for t in range(2)]
                    for t, p in enumerate(p2):
                        act.activation(Yh[0:CT, t, :].rearrange("p (a c) -> p a c", a=2), ps[0:CT, 2 * p:2 * p + 2, :], ACT.Copy,
                                       scale=slotw[0:CT, t:t + 1]).then_inc(sem("Yh_made"), 1)
                    for m in range(0, KT, 2):
                        gathered(j0 + 3 + FE, i, m)

            act.wait_ge(sem("c_landed"), 16)
            link(act.activation(c_act[:], c_in[:], ACT.Silu))
            act.activation(c_parts[:, :, 0:9], c_act[:], ACT.Copy).then_inc(sem("c_high"), 1)

            def ada_high(l, i, m):
                j = ada_slot(l, m)
                act.wait_ge(ada_landed(l, j), 16 * (i * 4 + m // (2 * GRP)) + 16 if l else 16 * i + 16)
                if l or not isinstance(i, int) or m > 2:
                    act.wait_ge(sem("ada_product"), ada_slabs(l, i, m) - (0 if l else 2))
                act.activation(ada_pair(l, m)[0], ada[j][:, m % GRP, :], ACT.Copy).then_inc(sem("ada_high"), 1)

            def ada_rows(l, i, m):
                act.wait_ge(sem("ada_product"), ada_slabs(l, i, m) + 1)
                act.activation(ada_row[:, m // CHUNK % 3, :], ps[0:18, ada_bank(l, m), :], ACT.Copy).then_inc(sem("row_made"), 1)

            def modulation_cycle(i):
                for m in range(CYCLE):
                    if m % CHUNK == 2 and not (m == 2 and isinstance(i, int)):
                        ada_rows(0, i, m - 3)
                    ada_high(0, i, m)

            def next_modulation(e, k):
                m = ada_spot(k)
                if m is not None:
                    if m % CHUNK == 0 and m:
                        ada_rows(1, e, m - 1)
                    ada_high(1, e, m)
                elif k == 31:
                    ada_rows(1, e, PER[1] - 1)

            modulation_cycle(0)
            first = base["w1", 0]
            act.wait_ge(sem("x_in"), 16)
            for l in range(L):
                ne = 2 if l == 0 else E

                def norm(name, which):
                    if which == 0:
                        if l:
                            products_read(act, "ff", l - 1)
                        for k in range(KT):
                            act.activation(sq[:, k, :], x[:, k, :], ACT.Square).then_inc(sem("sq_made"), 1)
                    if name == "n1" and l == 0:
                        act.wait_ge(sem("eps_made"), 1)
                    if which:
                        act.wait_ge(sem("norm_summed"), upto("norm_summed", l, 1))
                        act.activation(two(rt[:]), pair(3), ACT.Sqrt, bias=eps[:], scale=1.0 / D).then_inc(sem("rt_made"), 1)
                    else:
                        p = take(jobs[name, l], 0)
                        act.activation(two(rt[:]), pair(p), ACT.Sqrt, bias=eps[:], scale=1.0 / D).then_inc(acc_free[p], 1)
                    if name == "n1" and l == 0:
                        with act.Fori(1, GROUPS // ASLOTS) as i:
                            modulation_cycle(i)
                        ada_rows(0, GROUPS // ASLOTS - 1, CYCLE - 1)
                        for k in range(LEAD):
                            split_high(first, k - LEAD)
                    if name == "n1":
                        act.wait_ge(sem("mod_made"), 2 * l + 2)
                    for k in range(KT):
                        act.wait_ge(sem("tn_made"), upto("tn_made", l, which * KT + k + 1))
                        act.activation(hf[:, k, 0:T], tn[:, k, 0:T], ACT.Identity, bias=mod[:, l, (3 * which) * KT + k, 0:1],
                                       scale=mod[:, l, (3 * which + 1) * KT + k, 0:1]).then_inc(sem("hf_made"), 1)
                    act.wait_ge(sem("hf_made"), upto("hf_made", l, (which + 1) * KT))
                    act.wait_ge(sem("hfs_made"), upto("hfs_made", l, which + 1))
                    if l == 1 and which == 1:
                        return
                    for k in range(KT):
                        act.activation(Hh[:, k, :], hf[:, k, :], ACT.Copy).then_inc(sem("Hh_made"), 1)

                norm("n1", 0)
                s0, j0 = base["w1", l], jobs["w1", l]

                def w1_tiles(name, first, cycles):
                    with act.Fori(0, cycles) as i:
                        for j in range(3):
                            split_high(base[name, l], j, i)
                            p = take(jobs[name, l], j, i)
                            act.activation(two(z[:, bass.ds(3 * i + (first + j), 1), :].rearrange("p o n -> p (o n)")), pair(p),
                                           ACT.Copy).then_inc(acc_free[p], 1)

                w1_tiles("w1", 0, W1A // 3)
                products_read(act, "w1", l)
                for i in range(5):
                    act.activation(qsq[:, i, :], z[:, Z_Q + i, :], ACT.Square).then_inc(sem("qsq_made"), 1)
                for i in range(5):
                    p = take(jobs["qk", l], i)
                    act.activation(two(qrt[:, i, :]), pair(p), ACT.Sqrt, bias=eps[:], scale=1.0 / HD
                                   ).then_inc(acc_free[p], 1)
                w1_tiles("w1b", W1A, (W1 - W1A) // 3)
                act.wait_ge(sem("vt_done"), upto("vt_done", l, 1))
                act.wait_ge(sem("qk_made"), upto("qk_made", l, 5))
                act.activation(vtok[:].rearrange("p a b -> p (a b)"), ps[:, 6, :], ACT.Copy).then_inc(sem("vtok_made"), 1)
                def exps(n):
                    W = 2 * P if n else P
                    r = n % 2
                    act.wait_ge(sem("soft_in"), upto("soft_in", l, n + 1))
                    for h in range(NH):
                        act.activation(scb[r][:, h, 0:W], scb[r][:, h, 0:W], ACT.Exp, bias=nmx[:, r, h:h + 1],
                                       accum_out=rs[:, r, h:h + 1])
                    act.activation(esk[:, r, :], sk[:, r, :], ACT.Exp).then_inc(sem("exp_done"), 1)

                exps(0)
                for n in range(NB):
                    act.wait_ge(sem("pt_done"), upto("pt_done", l, n + 1))
                    act.activation(PT[:, 0:2, :], ps[:, 4:6, :], ACT.Copy).then_inc(sem("pta_copied"), 1)
                    if n + 1 < NB:
                        exps(n + 1)
                    act.wait_ge(sem("av_done"), upto("av_done", l, n + 1))
                    act.activation(Bh[:, 0:4, n * P:n * P + P], ps[:, 4, :].rearrange("p (t c) -> p t c", t=4), ACT.Copy
                                   ).then_inc(sem("avh_made"), 1)
                act.wait_ge(sem("kvt_done"), upto("kvt_done", l, 1))
                act.activation(kts[:], ps[0:NS, 4, 0:256], ACT.Copy).then_inc(sem("kts_made"), 1)
                act.wait_ge(sem("dsoft_in"), upto("dsoft_in", l, 1))
                link(act.activation(scs[:], scs[:], ACT.Exp))
                act.activation(ses[:], sts[:], ACT.Exp).then_inc(sem("dexp_done"), 1)
                act.wait_ge(sem("dlg_made"), upto("dlg_made", l, 1))
                link(act.activation(lab[:], las[:], ACT.Abs))
                link(act.activation(lab[:], lab[:], ACT.Exp, scale=-1.0))
                act.activation(lab[:], lab[:], ACT.Ln, bias=1.0).then_inc(sem("lab_made"), 1)
                act.wait_ge(sem("dpt_done"), upto("dpt_done", l, 1))
                act.activation(pT[:].rearrange("p b h -> p (b h)"), ps[:, 0, 0:NS * NH], ACT.Copy).then_inc(sem("pT_made"), 1)
                act.activation(prow[:].rearrange("p b h -> p (b h)"), ps[0:1, 1, 0:NS * NH], ACT.Copy
                               ).then_inc(sem("pT_made"), 1)
                act.wait_ge(sem("dav_done"), upto("dav_done", l, 1))
                dav = ps[:, 0, 0:NS * NH].rearrange("p (b k t) -> p k t b", b=NS, k=NKV)
                for kv in range(NKV):
                    hp = slice(64 * kv, 64 * kv + 64)
                    act.activation(Bh[hp, 0:4, T:N], dav[hp, kv], ACT.Copy).then_inc(sem("dah_made"), 1)
                act.wait_ge(sem("dla_done"), upto("dla_done", l, 1))
                act.activation(dcs[:].rearrange("p q b -> p (q b)"), ps[:, 1, 128:128 + 2 * NS], ACT.Exp, scale=1.0 / 16
                               ).then_inc(sem("dcs_made"), 1)
                act.wait_ge(sem("plg_made"), upto("plg_made", l, 1))
                link(act.activation(lt[:], la[:], ACT.Abs))
                link(act.activation(lt[:], lt[:], ACT.Exp, scale=-1.0))
                act.activation(lt[:], lt[:], ACT.Ln, bias=1.0).then_inc(sem("lt_made"), 1)
                act.wait_ge(sem("cum_done"), upto("cum_done", l, 1))
                act.wait_ge(sem("cache_out"), upto("cache_out", l, 5 * 16))
                link(act.activation(cum[:], ps[:, 6:8, :], ACT.Copy))
                act.activation(qe[:], cum[:], ACT.Exp).then_inc(sem("qe_exp"), 1)
                act.wait_ge(sem("qt_in"), upto("qt_in", l, 1))
                act.activation(qt[:], qt[:], ACT.Exp).then_inc(sem("qt_exp"), 1)
                for q in range(2):
                    for n in range(NB):
                        last = n * P + P - 1
                        act.activation(kd[:, q, n * P:n * P + P], cum[:, q, n * P:n * P + P], ACT.Exp, scale=-1.0,
                                       bias=cum[:, q, last:last + 1])
                mm = act.activation(dec[:], cum[:, :, P - 1::P], ACT.Exp)
                mm.then_inc(sem("kd_exp"), 1)
                for q in range(2):
                    for n in range(NB):
                        for i in range(NI):
                            k0 = SUB * i * (i + 1) // 2
                            ref = n * P + SUB * i + SUB // 2 - 1
                            mm = act.activation(kt[:, q, n, k0:k0 + SUB * (i + 1)], cum[:, q, n * P:n * P + SUB * (i + 1)],
                                                ACT.Exp, scale=-1.0, bias=cum[:, q, ref:ref + 1])
                mm.then_inc(sem("kt_exp"), 1)
                act.wait_ge(sem("do_done"), upto("do_done", l, 1))
                for r in range(2):
                    mm = act.activation(osmp[:].rearrange("p (q r) b -> p r q b", q=2)[:, r],
                                        ps[:, 2 + r, 0:2 * NS].rearrange("p (q b) -> p q b", q=2), ACT.Copy, scale=0.125)
                mm.then_inc(sem("osmp_made"), 1)
                act.wait_ge(sem("gvt_done"), upto("gvt_done", l, 1))
                act.activation(gvt[:, 0:2, :], ps[:, 4:6, :], ACT.Copy).then_inc(sem("gvt_made"), 1)
                act.wait_ge(sem("kdt_done"), upto("kdt_done", l, 1))
                act.wait_ge(sem("state_out"), upto("state_out", l, 16))
                act.activation(kdt[:].rearrange("p (a b) c -> p a (b c)", a=2), ps[:, 0:2, :], ACT.Copy
                               ).then_inc(sem("kdt_made"), 1)
                act.wait_ge(sem("o_done"), upto("o_done", l, 1))
                act.activation(z[:, Z_Q:Z_Q + 4, 0:T], ps[:, 0:4, :], ACT.Copy, scale=0.125)
                act.activation(z[:, Z_Q:Z_Q + 4, T:N], osmp[:], ACT.Copy).then_inc(sem("o_read"), 1)
                act.wait_ge(sem("o_read"), upto("o_read", l, 1))
                for h in range(GH):
                    act.activation(mf[:, h, :], z[:, Z_Q + h, :], ACT.Square).then_inc(sem("osq_made"), 1)

                def w3_tile(name, k, i, m, f):
                    split_high(base[name, l], k, i)
                    p = take(jobs[name, l], k, i)
                    act.activation(two(g[:, bass.ds(m, 1), :].rearrange("p o n -> p (o n)")), pair(p), f
                                   ).then_inc(acc_free[p], 1)

                for k in range(W3A):
                    w3_tile("w3", k, 0, k, ACT.Silu if k < GH else ACT.Sigmoid)
                for h in range(GH):
                    p = take(jobs["gn", l], h)
                    act.activation(two(mf[:, 4 + h, :]), pair(p), ACT.Sqrt, bias=eps[:], scale=1.0 / GV
                                   ).then_inc(acc_free[p], 1)
                with act.Fori(0, 3) as i:
                    for j in range(3):
                        w3_tile("w3b", j, i, 3 * i + (W3A + j), ACT.Sigmoid)
                for h in range(GH):
                    act.wait_ge(sem("og_made"), upto("og_made", l, h + 1))
                    act.activation(Bh[:, 4 + h, :], z[:, Z_Q + h, :], ACT.Copy).then_inc(sem("Bh_made"), 1)
                for k in range(9, W3 - W3A):
                    w3_tile("w3b", k, 0, W3A + k, ACT.Sigmoid)
                for k in range(8):
                    split_high(base["br", l], k)
                    if k % 2:
                        for m in (k - 1, k):
                            act.wait_ge(sem("mf_made"), upto("mf_made", l, m + 1))
                            act.activation(Hh[:, m, :], mf[:, m, :], ACT.Copy).then_inc(sem("Mh_made"), 1)
                def square(k):
                    p, u = psj(jobs["wo", l], k)
                    act.wait_ge(acc_free[p], u + 1)
                    act.activation(sq[:, k, :], x[:, k, :], ACT.Square).then_inc(sem("sq_made"), 1)

                for k in range(KT):
                    split_high(base["wo", l], k)
                    if k:
                        square(k - 1)
                square(KT - 1)
                norm("n2", 1)
                s0, j0 = base["ff", l], jobs["ff", l]
                if l == 1:
                    experts(l)
                    continue
                with act.Fori(0, ne) as e:
                    for m in range(FE):
                        split_high(s0, 2 * m, e * FE)
                        next_modulation(e, 2 * m)
                        p, u = psj(j0, 2 * m)
                        act.wait_ge(acc_full[p], u + e * 10 + 1)
                        act.activation(two(sg[:, m % 2, :]), pair(p), ACT.Silu).then_inc(acc_free[p], 1)
                        split_high(s0, 2 * m + 1, e * FE)
                        next_modulation(e, 2 * m + 1)
                        p, u = psj(j0, 2 * m + 1)
                        act.wait_ge(acc_free[p], u + e * 10 + 1)
                        act.activation(hidh[:, m, :], hm[:, m % 3, :], ACT.Copy).then_inc(sem("hidh_made"), 1)
                    for k in range(FE):
                        split_high(s0, 2 * FE + k, e * FE)
                        next_modulation(e, 2 * FE + k)

        @block.vector
        def _(dve):
            steps = [0]

            def link(inst):
                steps[0] += 1
                inst.then_inc(sem("dve_step"), 1)
                dve.wait_ge(sem("dve_step"), steps[0])

            def split_low(s0, k, i=0):
                sl, _ = slot(s0, k + LEAD, i)
                dve.wait_ge(hi_made[sl], r_use(s0, k + LEAD, i) + 1)
                dve.tensor_tensor(wl[:, sl, :], raw[:, sl, :], wh[:, sl, :].bitcast(F32), ALU.subtract
                                  ).then_inc(split_made[sl], 1)

            def take(j0, k, i=0):
                p, u = psj(j0, k, i)
                dve.wait_ge(acc_full[p], u + 1)
                return p

            def bc(ap, n, axis=2):
                v = ap.unsqueeze(axis)
                return v.broadcast_to([n if i == axis else k for i, k in enumerate(v.shape)])

            dve.memset(eps[:], EPS).then_inc(sem("eps_made"), 1)

            def ada_low(l, i, m):
                dve.wait_ge(sem("ada_high"), ada_slabs(l, i, m) + 1)
                pr = ada_pair(l, m)
                dve.tensor_tensor(pr[1], ada[ada_slot(l, m)][:, m % GRP, :], pr[0].bitcast(F32), ALU.subtract
                                  ).then_inc(sem("ada_low"), 1)

            dve.wait_ge(sem("c_high"), 1)
            dve.tensor_tensor(c_parts[:, :, 9:18], c_act[:], c_parts[:, :, 0:9].bitcast(F32), ALU.subtract
                              ).then_inc(sem("c_made"), 1)
            for m in range(CYCLE):
                ada_low(0, 0, m)
            dve.wait_ge(sem("small_in"), 16)
            link(dve.tensor_scalar(qg8[:], sm[:, S_QK:S_QK + 2 * L:2], 0.125, None, ALU.mult))
            def modulation(l):
                dve.wait_ge(sem("ada_turned"), (l + 1) * ADA // CHUNK)
                link(dve.tensor_tensor(mod[:, l], ps[:, 7, 0:9 * ADA].rearrange("p (m c) -> p m c", c=9),
                                       bc(sm[:, S_ADAB + l * ADA:S_ADAB + l * ADA + ADA], 9), ALU.add))
                for w in range(2):
                    sc1 = mod[:, l, (3 * w + 1) * KT:(3 * w + 2) * KT, :]
                    dve.scalar_tensor_tensor(out=sc1, in0=sc1, scalar=1.0,
                                             in1=bc(sm[:, S_N + (2 * l + w) * KT:S_N + (2 * l + w + 1) * KT], 9),
                                             op0=ALU.add, op1=ALU.mult).then_inc(sem("mod_made"), 1)

            def add_residual(l, p, m, which, n_tmp):
                gi = (2 + 3 * which) * KT + m
                dve.scalar_tensor_tensor(out=x[:, m, 0:HN], in0=ps[:, 2 * p, 0:HN], scalar=mod[:, l, gi, 0:1],
                                         in1=x[:, m, 0:HN], op0=ALU.mult, op1=ALU.add)
                dve.scalar_tensor_tensor(out=x[:, m, HN:T], in0=ps[:, 2 * p + 1, 0:T - HN], scalar=mod[:, l, gi, 0:1],
                                         in1=x[:, m, HN:T], op0=ALU.mult, op1=ALU.add)
                dve.tensor_tensor(xs_tmp[:, m % 2, :], ps[:, 2 * p + 1, T - HN:HN], mod[:, l, gi, 1:9], ALU.mult
                                  ).then_inc(sem("xs_made"), 1)
                dve.wait_ge(sem("xs_made"), n_tmp)
                dve.tensor_tensor(x[:, m, T:N], x[:, m, T:N], xs_tmp[:, m % 2, :], ALU.add).then_inc(acc_free[p], 1)

            def experts(l):
                dve.wait_ge(sem("rank_done"), 1)
                link(dve.memset(slotpos[:], -1.0))
                link(dve.tensor_tensor(slotpos[:, 0:NB, 0:E], chosen[:, 0:NB, :],
                                       ps[:, 7, 0:NB * E].rearrange("p (n e) -> p n e", e=E), ALU.mult))
                link(dve.tensor_tensor(slotpos[0:NS, NB, 0:E], chosen[0:NS, NB, :], ps[0:NS, 7, NB * E:NB * E + E], ALU.mult))
                dve.tensor_scalar(slotpos[:, 0:NB, 0:E], slotpos[:, 0:NB, 0:E], -1.0, None, ALU.add)
                link(dve.tensor_scalar(slotpos[0:NS, NB, 0:E], slotpos[0:NS, NB, 0:E], -1.0, None, ALU.add))
                link(dve.tensor_scalar(slotpos[:, :, E:E + 1], slotpos[:, :, 0:1], -float(CAP), None, ALU.add))
                link(dve.tensor_reduce(cnt[0][:], ps[:, 7, (NB + 1) * E:(NB + 2) * E], AX, ALU.max))
                dve.tensor_scalar(cnt[1][:], cnt[0][:], CAP + 0.5, 1.0, ALU.is_gt, ALU.add)
                link(dve.tensor_scalar(cnt[2][:], cnt[0][:], 2 * CAP + 0.5, None, ALU.is_gt))
                dve.tensor_tensor(sweeps[:], cnt[1][:], cnt[2][:], ALU.add).then_inc(sem("sweeps_made"), 1)

                def select(e):
                    dve.tensor_tensor(Sel[:], bc(slot_ids, NB + 1, 1),
                                      slotpos[:, :, bass.ds(e, 1)].broadcast_to([P, NB + 1, CAP]), ALU.is_equal
                                      ).then_inc(sem("Sel_made"), 1)

                select(0)
                for n in range(NB + 1):
                    rows = P if n < NB else NS
                    p = take(jobs["ht", l], n)
                    dve.wait_ge(sem("hTh_made"), n + 1)
                    dve.tensor_tensor(hTl[0:rows, n, :].rearrange("p (a c) -> p a c", a=2), ps[0:rows, 2 * p:2 * p + 2, :],
                                      hTh[0:rows, n, :].rearrange("p (a c) -> p a c", a=2).bitcast(F32), ALU.subtract
                                      ).then_inc(acc_free[p], 1)

                def gathered(job0, i, m):
                    p, u = psj(job0, m)
                    dve.wait_ge(acc_full[p], u + i * (ITEM_JOBS // PAIRS) + 1)
                    dve.tensor_copy(XE[:, :, m, :], ps[:, 2 * p:2 * p + 2, 0:CAP]).then_inc(acc_free[p], 1)

                for m in range(1, KT, 2):
                    gathered(jobs["xe", l], 0, m)
                dve.wait_ge(sem("sweeps_made"), 1)
                n_sweeps = dve.value_load(sweeps[0:1, 0:1], min_val=1, max_val=3)
                s0, j0 = base["ff", l], jobs["ff", l]
                per_pair = ITEM_JOBS // PAIRS
                with dve.Fori(0, n_sweeps) as c:
                    with dve.Fori(0, E) as e:
                        i = c * E + e

                        def full(k):
                            p, u = psj(j0, k)
                            dve.wait_ge(acc_full[p], u + i * per_pair + 1)
                            return p

                        def expert_low(k):
                            sl, _ = slot(s0, k + LEAD)
                            dve.wait_ge(hi_made[sl], r_use(s0, k + LEAD, i * FE) + 1)
                            dve.tensor_tensor(wl[:, sl, :], ring(k % RING), wh[:, sl, :].bitcast(F32), ALU.subtract
                                              ).then_inc(split_made[sl], 1)

                        def hidden_low(m):
                            dve.wait_ge(sem("hidh_made"), upto("hidh_made", l, i * FE + m + 1))
                            dve.tensor_tensor(hel[:, m, :], hmm[:, m % 3, :], heh[:, m, :].bitcast(F32), ALU.subtract
                                              ).then_inc(sem("hid_made"), 1)

                        full(0)
                        dve.tensor_copy(slotw[0:CT, :], ps[0:CT, 7, 0:2]).then_inc(sem("slotw_made"), 1)
                        for m in range(FE):
                            expert_low(2 * m)
                            if m:
                                hidden_low(m - 1)
                            if m == 2:
                                select(e + 1)
                            expert_low(2 * m + 1)
                            p = full(1 + m)
                            dve.wait_ge(sem("silu_made"), i * FE + m + 1)
                            dve.tensor_tensor(hmm[:, m % 3, :], sgm[:, m % 3, :], ps[:, 2 * p + 1, 0:CAP], ALU.mult
                                              ).then_inc(acc_free[p], 1)
                        for k in range(FE):
                            expert_low(2 * FE + k)
                            if k == 0:
                                hidden_low(FE - 1)
                        p2 = [full(1 + FE + t) for t in range(2)]
                        for t, p in enumerate(p2):
                            dve.wait_ge(sem("Yh_made"), i * 2 + t + 1)
                            dve.scalar_tensor_tensor(out=Yl[0:CT, t, :].rearrange("p (a c) -> p a c", a=2),
                                                     in0=ps[0:CT, 2 * p:2 * p + 2, :], scalar=slotw[0:CT, t:t + 1],
                                                     in1=Yh[0:CT, t, :].rearrange("p (a c) -> p a c", a=2).bitcast(F32),
                                                     op0=ALU.mult, op1=ALU.subtract).then_inc(acc_free[p], 1)
                        for m in range(1, KT, 2):
                            gathered(j0 + 3 + FE, i, m)
                        for m in range(KT):
                            p = full(3 + FE + KT + m)
                            add_residual(l, p, m, 1, i * KT + upto("xs_made", l, KT + m + 1))
                    dve.tensor_scalar(slotpos[:], slotpos[:], -float(CAP), None, ALU.add).then_inc(sem("slotpos_moved"), 1)
                    dve.wait_ge(sem("slotpos_moved"), c + 1)
                dve.memset(cnt[0][:], 0.0).then_inc(sem("x_final"), 1)

            dve.wait_ge(sem("x_in"), 16)
            dve.wait_ge(sem("const_in"), 16)
            for l in range(L):
                ne = 2 if l == 0 else E

                def norm(name, which):
                    if which:
                        dve.wait_ge(sem("rt_made"), upto("rt_made", l, 1))
                    else:
                        p, u = psj(jobs[name, l], 0)
                        dve.wait_ge(acc_free[p], u + 1)
                    link(dve.reciprocal(ri[:], rt[:]))
                    for k in range(KT):
                        dve.tensor_tensor(tn[:, k, :], x[:, k, :], ri[:], ALU.mult).then_inc(sem("tn_made"), 1)
                    if name == "n1":
                        if l == 0:
                            with dve.Fori(1, GROUPS // ASLOTS) as i:
                                for m in range(CYCLE):
                                    ada_low(0, i, m)
                            for k in range(LEAD):
                                split_low(base["w1", 0], k - LEAD)
                        modulation(l)
                        dve.wait_ge(sem("mod_made"), 2 * l + 2)
                    dve.wait_ge(sem("tn_made"), upto("tn_made", l, (which + 1) * KT))
                    link(dve.tensor_tensor(hf[:, :, T:N], tn[:, :, T:N], mod[:, l, (3 * which + 1) * KT:(3 * which + 2) * KT, 1:9], ALU.mult))
                    dve.tensor_tensor(hf[:, :, T:N], hf[:, :, T:N], mod[:, l, 3 * which * KT:(3 * which + 1) * KT, 1:9], ALU.add
                                      ).then_inc(sem("hfs_made"), 1)
                    if l == 1 and which == 1:
                        return
                    for k in range(KT):
                        dve.wait_ge(sem("Hh_made"), upto("Hh_made", l, which * KT + k + 1))
                        dve.tensor_tensor(Hl[:, k, :], hf[:, k, :], Hh[:, k, :].bitcast(F32), ALU.subtract
                                          ).then_inc(sem("H_made"), 1)

                norm("n1", 0)
                with dve.Fori(0, W1A // 3) as i:
                    for j in range(3):
                        split_low(base["w1", l], j, i)
                for i in range(5):
                    split_low(base["w1b", l], i)
                    p, u = psj(jobs["qk", l], i)
                    dve.wait_ge(acc_free[p], u + 1)
                    link(dve.reciprocal(qrt[:, i, :], qrt[:, i, :]))
                    gain = qg8[:, l:l + 1] if i < 4 else sm[:, S_QK + 2 * l + 1:S_QK + 2 * l + 2]
                    dve.scalar_tensor_tensor(out=z[:, Z_Q + i, :], in0=z[:, Z_Q + i, :], scalar=gain, in1=qrt[:, i, :],
                                             op0=ALU.mult, op1=ALU.mult).then_inc(sem("qk_made"), 1)
                for k in range(5, W1 - W1A):
                    split_low(base["w1b", l], k)
                products_read(dve, "w1b", l)
                dve.memset(z[BROW:BROW + 1, Z_GA, :], 1.0).then_inc(sem("ones_made"), 1)
                dve.wait_ge(sem("qk_made"), upto("qk_made", l, 5))
                def soft_in(n):
                    W = 2 * P if n else P
                    r = n % 2
                    dve.wait_ge(sem("sc_done"), upto("sc_done", l, n + 1))
                    for kv in range(NKV):
                        mm = dve.tensor_tensor(scb[r][:, 4 * kv:4 * kv + 4, 0:W],
                                               ps[:, 2 * kv:2 * kv + 2, :].rearrange("p a (b s) -> p (a b) s", b=2)[:, :, 0:W],
                                               biasT[:, 4 * kv:4 * kv + 4, 2 * P - W:2 * P], ALU.add)
                    mm.then_inc(sem("sc_read"), 1)
                    dve.wait_ge(sem("sc_read"), upto("sc_read", l, n + 1))
                    link(dve.tensor_reduce(mx[:], scb[r][:, :, 0:W], AX, ALU.max))
                    link(dve.tensor_tensor(mx[:], mx[:], sm[:, S_SINK + l * NH:S_SINK + l * NH + NH], ALU.max))
                    dve.tensor_scalar(nmx[:, r, :], mx[:], -1.0, None, ALU.mult)
                    dve.tensor_tensor(sk[:, r, :], sm[:, S_SINK + l * NH:S_SINK + l * NH + NH], mx[:], ALU.subtract
                                      ).then_inc(sem("soft_in"), 1)

                def weights(n):
                    W = 2 * P if n else P
                    r = n % 2
                    dve.wait_ge(sem("exp_done"), upto("exp_done", l, n + 1))
                    link(dve.tensor_tensor(den[:], rs[:, r, :], esk[:, r, :], ALU.add))
                    link(dve.reciprocal(rec[:], den[:]))
                    dve.tensor_tensor(scb[r][:, :, 0:W], scb[r][:, :, 0:W], bc(rec[:], W), ALU.mult).then_inc(sem("p_made"), 1)

                def attended_low(n):
                    dve.wait_ge(sem("avh_made"), upto("avh_made", l, n + 1))
                    dve.tensor_tensor(Bl[:, 0:4, n * P:n * P + P], ps[:, 4, :].rearrange("p (t c) -> p t c", t=4),
                                      Bh[:, 0:4, n * P:n * P + P].bitcast(F32), ALU.subtract).then_inc(sem("av_read"), 1)

                soft_in(0)
                weights(0)
                for n in range(NB):
                    if n + 1 < NB:
                        soft_in(n + 1)
                    if n:
                        dve.wait_ge(sem("pt_done"), upto("pt_done", l, n + 1))
                        dve.tensor_copy(PT[:, 2:4, :], ps[:, 6:8, :]).then_inc(sem("ptb_copied"), 1)
                    if n + 1 < NB:
                        weights(n + 1)
                    attended_low(n)
                link(dve.memset(qs[:], 0.0))
                for kv in range(NKV):
                    hp = slice(64 * kv, 64 * kv + 64)
                    mm = dve.tensor_copy(qs[hp, :, 4 * kv:4 * kv + 4].rearrange("p b t -> p t b"), z[hp, Z_Q:Z_Q + 4, T:N])
                mm.then_inc(sem("qs_made"), 1)
                dve.wait_ge(sem("kc_in"), upto("kc_in", l, 16))
                dve.tensor_copy(kc[:, :, P:P + 1].rearrange("p b o -> p (b o)"), z[:, Z_K, T:N]).then_inc(sem("kc_made"), 1)
                dve.wait_ge(sem("dsc_done"), upto("dsc_done", l, 1))
                link(dve.tensor_tensor(scs[:], ps[0:NS, 0:4, :].rearrange("p a (b s) -> p (a b) s", b=2)[:, :, 0:129],
                                       bc(biasS, NS, 1), ALU.add))
                link(dve.tensor_reduce(smx[:], scs[:], AX, ALU.max))
                sinkc = sm[0:NS, S_SINKC + l:S_SINKC + l + 1]
                link(dve.tensor_scalar(smx[:], smx[:], sinkc, None, ALU.max))
                dve.tensor_tensor(scs[:], scs[:], bc(smx[:], 129), ALU.subtract)
                dve.tensor_scalar(sts[:], smx[:], -1.0, sinkc, ALU.mult, ALU.add).then_inc(sem("dsoft_in"), 1)
                dve.wait_ge(sem("dlg_done"), upto("dlg_done", l, 1))
                dve.tensor_copy(las[:], ps[0:NS, 6, 0:256]).then_inc(sem("dlg_made"), 1)
                dve.wait_ge(sem("kts_made"), upto("kts_made", l, 1))
                dve.tensor_tensor(kms[:], bc(kts[:], NS, 1), bc(ident[0:NS, 0:NS], 256), ALU.mult)
                dve.tensor_copy(vts[:], ps[0:NS, 5, :]).then_inc(sem("kms_made"), 1)
                dve.wait_ge(sem("dexp_done"), upto("dexp_done", l, 1))
                link(dve.tensor_reduce(srs[:], scs[:], AX, ALU.add))
                link(dve.tensor_tensor(sdn[:], srs[:], ses[:], ALU.add))
                link(dve.reciprocal(srec[:], sdn[:]))
                dve.tensor_tensor(scs[:], scs[:], bc(srec[:], 129), ALU.mult).then_inc(sem("dp_made"), 1)
                dve.wait_ge(sem("lab_made"), upto("lab_made", l, 1))
                link(dve.tensor_scalar(lac[:], las[:], 0.0, None, ALU.min))
                dve.tensor_tensor(las[:], lac[:], lab[:], ALU.subtract).then_inc(sem("las_made"), 1)
                dve.wait_ge(sem("dpt_done"), upto("dpt_done", l, 1))
                dve.tensor_copy(vrow[:].rearrange("p (a b) v -> p a (b v)", a=2), ps[0:1, 2:4, :]).then_inc(sem("vrow_made"), 1)
                dve.wait_ge(sem("lg_done"), upto("lg_done", l, 1))
                dve.tensor_copy(la[:].rearrange("p n c -> p (n c)"), ps[:, 6:8, :].rearrange("p a c -> p (a c)")
                                ).then_inc(sem("plg_made"), 1)
                dav = ps[:, 0, 0:NS * NH].rearrange("p (b k t) -> p k t b", b=NS, k=NKV)
                for kv in range(NKV):
                    hp = slice(64 * kv, 64 * kv + 64)
                    dve.wait_ge(sem("dah_made"), upto("dah_made", l, kv + 1))
                    mm = dve.tensor_tensor(Bl[hp, 0:4, T:N], dav[hp, kv], Bh[hp, 0:4, T:N].bitcast(F32), ALU.subtract)
                mm.then_inc(sem("da_read"), 1)
                dve.wait_ge(sem("dcs_made"), upto("dcs_made", l, 1))
                dve.wait_ge(sem("st_in"), upto("st_in", l, 16))
                link(dve.tensor_tensor(Sst[:], Sst[:], bc(dcs[:].rearrange("p q b -> p b q"), GV, 3), ALU.mult))
                dve.wait_ge(sem("lt_made"), upto("lt_made", l, 1))
                link(dve.tensor_scalar(la[:], la[:], 0.0, None, ALU.min))
                dve.tensor_tensor(la[:], la[:], lt[:], ALU.subtract).then_inc(sem("la_made"), 1)
                dve.wait_ge(sem("kv_done"), upto("kv_done", l, 1))
                dve.tensor_tensor(Sst[:].rearrange("p b q v -> p (b q v)"), Sst[:].rearrange("p b q v -> p (b q v)"),
                                  ps[:, 0:4, :].rearrange("p a c -> p (a c)"), ALU.add).then_inc(sem("Sst_made"), 1)
                dve.wait_ge(sem("qe_exp"), upto("qe_exp", l, 1))
                refs = cum[:, :, SUB // 2 - 1::SUB]
                dve.tensor_tensor(qt[:].rearrange("p q (i c) -> p q i c", c=SUB), cum[:].rearrange("p q (i c) -> p q i c", c=SUB),
                                  bc(refs, SUB, 3), ALU.subtract).then_inc(sem("qt_in"), 1)
                dve.tensor_tensor(qe[:], qe[:], z[:, Z_GQ:Z_GQ + 2, 0:T], ALU.mult).then_inc(sem("qe_made"), 1)
                dve.memset(S[:], 0.0)
                dve.wait_ge(sem("qt_exp"), upto("qt_exp", l, 1))
                dve.tensor_tensor(qt[:], qt[:], z[:, Z_GQ:Z_GQ + 2, 0:T], ALU.mult).then_inc(sem("qt_made"), 1)
                dve.wait_ge(sem("kd_exp"), upto("kd_exp", l, 1))
                dve.tensor_tensor(kd[:], kd[:], z[:, Z_GK:Z_GK + 2, 0:T], ALU.mult).then_inc(sem("kd_made"), 1)
                dve.wait_ge(sem("kt_exp"), upto("kt_exp", l, 1))
                for i in range(NI):
                    k0 = SUB * i * (i + 1) // 2
                    rows = SUB * (i + 1)
                    gk = z[:, Z_GK:Z_GK + 2, 0:T].rearrange("p q (n c) -> p q n c", n=NB)[:, :, :, 0:rows]
                    mm = dve.tensor_tensor(kt[:, :, :, k0:k0 + rows], kt[:, :, :, k0:k0 + rows], gk, ALU.mult)
                mm.then_inc(sem("kt_made"), 1)
                dve.wait_ge(sem("state_out"), upto("state_out", l, 16))
                dve.wait_ge(sem("do_done"), upto("do_done", l, 1))
                dve.memset(att[:], 0.0)
                dve.wait_ge(sem("gvt_done"), upto("gvt_done", l, 1))
                dve.tensor_copy(gvt[:, 2:4, :], ps[:, 6:8, :]).then_inc(sem("gvt_made"), 1)
                dve.wait_ge(sem("ds_done"), upto("ds_done", l, 1))
                for n in range(NB):
                    for r in range(2):
                        hp = slice(64 * r, 64 * r + 64)
                        for q in range(2):
                            dsn = ps[hp, 2 + n // 2, (n % 2) * 256 + q * GV:(n % 2) * 256 + q * GV + GV]
                            if n == 0:
                                mm = dve.tensor_copy(S[hp, 0, q, r, :], dsn)
                            else:
                                mm = dve.scalar_tensor_tensor(out=S[hp, n, q, r, :], in0=S[hp, n - 1, q, r, :],
                                                              scalar=dec[hp, q, n:n + 1], in1=dsn, op0=ALU.mult, op1=ALU.add)
                    mm.then_inc(sem("S_made"), 1)
                    dve.wait_ge(sem("S_made"), upto("S_made", l, n + 1))
                dve.wait_ge(sem("at_done"), upto("at_done", l, 1))
                for r in range(2):
                    src = ps[:, 4 + 2 * r:6 + 2 * r, :].rearrange("p a (b q c) -> p (a b) q c", b=2, q=2)
                    dst = att[:].rearrange("p n (q r) c -> p r n q c", q=2)
                    for i in range(NI):
                        rows = SUB * (i + 1)
                        cols = slice(SUB * i, SUB * i + SUB)
                        mk = bc(bc(MSK[0:rows, cols], 2, 1), NB, 1)
                        mm = dve.tensor_tensor(dst[0:rows, r, :, :, cols], src[0:rows, :, :, cols], mk, ALU.mult)
                mm.then_inc(sem("att_made"), 1)
                for k in range(W3A):
                    split_low(base["w3", l], k)
                for h in range(GH):
                    split_low(base["w3b", l], h)
                    p, u = psj(jobs["gn", l], h)
                    dve.wait_ge(acc_free[p], u + 1)
                    link(dve.reciprocal(mf[:, 4 + h, :], mf[:, 4 + h, :]))
                    link(dve.scalar_tensor_tensor(out=z[:, Z_Q + h, :], in0=z[:, Z_Q + h, :],
                                                  scalar=sm[:, S_GN + l:S_GN + l + 1], in1=mf[:, 4 + h, :],
                                                  op0=ALU.mult, op1=ALU.mult))
                    dve.tensor_tensor(z[:, Z_Q + h, :], z[:, Z_Q + h, :], g[:, h, :], ALU.mult).then_inc(sem("og_made"), 1)
                for k in range(GH, 9):
                    split_low(base["w3b", l], k)
                dve.wait_ge(sem("S_out"), upto("S_out", l, 32))
                for h in range(GH):
                    dve.wait_ge(sem("Bh_made"), upto("Bh_made", l, h + 1))
                    dve.tensor_tensor(Bl[:, 4 + h, :], z[:, Z_Q + h, :], Bh[:, 4 + h, :].bitcast(F32), ALU.subtract
                                      ).then_inc(sem("B_made"), 1)
                for k in range(9, W3 - W3A):
                    split_low(base["w3b", l], k)
                s0, j0 = base["br", l], jobs["br", l]
                for mp in range(4):
                    split_low(s0, 2 * mp)
                    for m in range(2):
                        p = take(j0, 4 * mp + m)
                        dve.tensor_tensor(two(ta[:, m, :]), two(g[:, 4 + 2 * mp + m, :]), pair(p), ALU.mult
                                          ).then_inc(acc_free[p], 1)
                    split_low(s0, 2 * mp + 1)
                    for m in range(2):
                        p = take(j0, 4 * mp + 2 + m)
                        dve.tensor_tensor(two(mf[:, 2 * mp + m, :]), two(g[:, 12 + 2 * mp + m, :]), pair(p), ALU.mult
                                          ).then_inc(acc_free[p], 1)
                    p, u = psj(j0, 4 * mp + 3)
                    dve.wait_ge(acc_free[p], u + 1)
                    for m in range(2):
                        dve.tensor_tensor(mf[:, 2 * mp + m, :], mf[:, 2 * mp + m, :], ta[:, m, :], ALU.add
                                          ).then_inc(sem("mf_made"), 1)
                    for m in range(2):
                        dve.wait_ge(sem("Mh_made"), upto("Mh_made", l, 2 * mp + m + 1))
                        dve.tensor_tensor(Hl[:, 2 * mp + m, :], mf[:, 2 * mp + m, :], Hh[:, 2 * mp + m, :].bitcast(F32),
                                          ALU.subtract).then_inc(sem("M_made"), 1)
                s0, j0 = base["wo", l], jobs["wo", l]
                for k in range(KT):
                    split_low(s0, k)
                    p = take(j0, k)
                    add_residual(l, p, k, 0, upto("xs_made", l, k + 1))
                dve.memset(den[:], 0.0).then_inc(sem("ring_open" if l else "B_read"), 1)
                norm("n2", 1)
                if l == 1:
                    link(dve.memset(lg[:], 0.0))
                    dve.wait_ge(sem("rl_done"), upto("rl_done", l, 1))
                    rb = sm[:, S_RB:S_RB + E]
                    dve.tensor_tensor(lg[:, 0:NB, :], ps[:, 6, 0:NB * E].rearrange("p (n e) -> p n e", e=E), bc(rb, NB, 1), ALU.add)
                    link(dve.tensor_tensor(lg[0:NS, NB, :], ps[0:NS, 6, NB * E:NB * E + E], rb[0:NS, :], ALU.add))
                    rk = bc(rank8, NB + 1, 1)

                    def col(i):
                        return r1[i][:].rearrange("p n o -> p (n o)")

                    def choose(logits, first, tmp, i):
                        link(dve.tensor_reduce(col(i), logits[:], AX, ALU.max))
                        link(dve.tensor_tensor(tmp[:], logits[:], bc(col(i), E), ALU.is_equal))
                        link(dve.tensor_tensor(tmp[:], tmp[:], rk, ALU.mult))
                        link(dve.tensor_reduce(col(i + 1), tmp[:], AX, ALU.max))
                        link(dve.tensor_tensor(first[:], tmp[:], bc(col(i + 1), E), ALU.is_equal))

                    choose(lg, rr[0], rr[1], 0)
                    link(dve.scalar_tensor_tensor(out=rr[2][:], in0=rr[0][:], scalar=-3.0e38, in1=lg[:], op0=ALU.mult, op1=ALU.add))
                    choose(rr[2], rr[3], rr[4], 2)
                    dve.tensor_tensor(chosen[:], rr[0][:], rr[3][:], ALU.add).then_inc(sem("chosen_made"), 1)
                    dve.tensor_tensor(col(4), col(2), col(0), ALU.subtract).then_inc(sem("rt_exp_in"), 1)
                    dve.wait_ge(sem("rt_exp"), upto("rt_exp", l, 1))
                    link(dve.tensor_scalar(col(6), col(5), 1.0, None, ALU.add))
                    link(dve.reciprocal(col(7), col(6)))
                    link(dve.tensor_tensor(col(8), col(5), col(7), ALU.mult))
                    dve.tensor_tensor(rr[5][:], rr[0][:], bc(col(7), E), ALU.mult)
                    link(dve.tensor_tensor(rr[6][:], rr[3][:], bc(col(8), E), ALU.mult))
                    link(dve.tensor_tensor(rr[7][:], rr[5][:], rr[6][:], ALU.add))
                    experts(l)
                    continue
                s0, j0 = base["ff", l], jobs["ff", l]
                def next_low(e, k):
                    if ada_spot(k) is not None:
                        ada_low(1, e, ada_spot(k))

                with dve.Fori(0, ne) as e:
                    for m in range(FE):
                        split_low(s0, 2 * m, e * FE)
                        next_low(e, 2 * m)
                        p, u = psj(j0, 2 * m)
                        dve.wait_ge(acc_free[p], u + e * 10 + 1)
                        split_low(s0, 2 * m + 1, e * FE)
                        next_low(e, 2 * m + 1)
                        p, u = psj(j0, 2 * m + 1)
                        dve.wait_ge(acc_full[p], u + e * 10 + 1)
                        dve.tensor_tensor(two(hm[:, m % 3, :]), two(sg[:, m % 2, :]), pair(p), ALU.mult
                                          ).then_inc(acc_free[p], 1)
                        dve.wait_ge(sem("hidh_made"), upto("hidh_made", l, e * FE + m + 1))
                        dve.tensor_tensor(hidl[:, m, :], hm[:, m % 3, :], hidh[:, m, :].bitcast(F32), ALU.subtract
                                          ).then_inc(sem("hid_made"), 1)
                    for k in range(FE):
                        split_low(s0, 2 * FE + k, e * FE)
                        next_low(e, 2 * FE + k)
                        for m in range(KT):
                            if (m * FE + FE - 1) // KT == k:
                                p, u = psj(j0, 2 * FE + m)
                                dve.wait_ge(acc_full[p], u + e * 10 + 1)
                                add_residual(l, p, m, 1, e * KT + upto("xs_made", l, KT + m + 1))


def slabs(inputs):
    def blocks(w):
        K, M = w.shape
        return w.reshape(K // P, P, M // P, P).transpose(2, 1, 0, 3).reshape(M // P, P, K)

    out = []
    for l in range(L):
        out.append(inputs["ada_w"][l].reshape(CHUNK, 2, P, ADA // CHUNK, 512).transpose(3, 0, 2, 1, 4).reshape(ADA, P, D))
    for l in range(L):
        w = inputs["w_in"][l]
        q = w[:, 0:512].reshape(D, 2, 4, HD).transpose(0, 2, 1, 3).reshape(D, 512)
        ga = np.zeros((D, P), np.float32)
        ga[:, 0:RANK] = w[:, 1792:1808]
        out.append(blocks(ga))
        out.append(blocks(q))
        out.append(blocks(w[:, 512:1792]))
        out.append(blocks(w[:, 1808:4368]))
        wa_ = inputs["w_branch_a"][l].reshape(2, 4, HD, D).transpose(1, 0, 2, 3).reshape(512, D)
        pa = blocks(wa_)
        pb = blocks(inputs["w_branch_b"][l])
        for mp in range(4):
            for w4 in (pa, pb):
                out.append(np.concatenate([w4[2 * mp], w4[2 * mp + 1]], axis=1)[None])
        out.append(blocks(inputs["w_out"][l]))
        if l == 0:
            hw = FE * P
            ex = [(inputs["ffn_w_gate"][0][:, e * hw:e * hw + hw], inputs["ffn_w_up"][0][:, e * hw:e * hw + hw],
                   inputs["ffn_w_down"][0][e * hw:e * hw + hw]) for e in range(2)]
        else:
            ex = [(inputs["moe_w_gate"][0, e], inputs["moe_w_up"][0, e], inputs["moe_w_down"][0, e]) for e in range(E)]
        for wg, wu, wd in ex:
            out.append(np.stack([blocks(wg), blocks(wu)], axis=1).reshape(2 * FE, P, D))
            if l:
                out.append(wd.reshape(FE, P, D))
                continue
            d = blocks(wd).reshape(KT, P, FE, P).transpose(0, 2, 1, 3).reshape(FE, KT, P, P)
            out.append(d.transpose(0, 2, 1, 3).reshape(FE, P, D))
    experts = sum(a.shape[0] for a in out) - E * EXP_SLABS
    flat = np.concatenate(out, axis=0)
    return np.concatenate([flat, flat[experts:experts + LEAD]], axis=0)

def constants():
    c = np.zeros((P, C_END), np.float32)
    i = np.arange(P)
    c[:, C_ID:C_ID + P] = np.eye(P)
    c[:, C_ONE:C_ONE + P] = 1.0
    c[:, C_BLK:C_BLK + P] = (i[:, None] // HD) == (i[None] // HD)
    c[:, C_U:C_U + P] = (i[:, None] <= i[None]) / 16.0
    c[:, C_M:C_M + P] = i[:, None] <= i[None]
    slope = 2.0 ** -(np.arange(1, NH + 1, dtype=np.float64))
    dist = P + i[:, None] - np.arange(2 * P)[None]
    ok = (dist >= 0) & (dist <= P)
    c[:, C_BIAS:C_BIAS + NH * 2 * P] = np.where(ok[:, None], -slope[None, :, None] * dist[:, None], -1.0e30).reshape(P, -1)
    c[0:NH, C_BS:C_BS + 129] = -slope[:, None] * (P - np.arange(129))[None]
    c[:, C_RANK:C_RANK + E] = E - np.arange(E)
    c[:, C_J:C_J + 9] = i[:, None] % 9 == np.arange(9)
    c[:, C_SLOT:C_SLOT + CAP] = np.arange(CAP)
    return c


def kernel(**inputs):
    import concourse.bacc as bacc
    from concourse.bass_utils import run_bass_kernel_spmd as run

    v = {k: np.asarray(a) for k, a in inputs.items()}

    def feat(a):
        return a.T.reshape(-1, P, a.shape[0]).transpose(1, 0, 2)

    small = np.concatenate(
        [v["ada_b"][l].reshape(ADA, P).T for l in range(L)]
        + [v[n][l].reshape(KT, P).T for l in range(L) for n in ("norm1_g", "norm2_g")]
        + [np.concatenate([v[n][l], v[n][l]])[:, None] for l in range(L) for n in ("q_norm_g", "k_norm_g")]
        + [v["gla_norm_g"][l][:, None] for l in range(L)]
        + [np.broadcast_to(v["attn_sinks"].reshape(1, L * NH), (P, L * NH))]
        + [np.concatenate([v["attn_sinks"].T, np.zeros((P - NH, L), np.float32)], axis=0)]
        + [v["router_w"][0].reshape(KT, P, E).transpose(1, 0, 2).reshape(P, KT * E)]
        + [np.broadcast_to(v["router_b"], (P, E))], axis=1)
    arrays = {
        "xT": feat(np.concatenate([v["x_prompt"][0], v["x_sample"][:, 0]], axis=0)),
        "cT": feat(np.concatenate([v["c_prompt"], v["c_sample"]], axis=0)),
        "weights": slabs(v),
        "constants": constants(),
        "small": small,
        "wa2": np.concatenate([v["gla_wa2"].transpose(1, 0, 2), np.zeros((BROW - RANK, L, 256), np.float32),
                               v["gla_ba"][None]], axis=0),
        "k_cache": v["cache_k"].transpose(0, 3, 4, 1, 2).reshape(L, P, NS, P),
        "v_cache": v["cache_v"].transpose(0, 2, 1, 3, 4).reshape(L, P, NS, P),
        "state": v["state_gla"].reshape(L, NS, 2, 2, GK, GV).transpose(0, 3, 4, 1, 2, 5).reshape(L, P, NS, 2, GV),
    }
    arrays = {k: np.ascontiguousarray(a) for k, a in arrays.items()}
    outs = {"yT": (P, KT, N), "kp": (L, P, P), "vp": (L, P, P), "sp": (L, P, 2, GV), "ks": (L, P, NS, P),
            "vs": (L, P, NS, P), "ss": (L, P, NS, 2, GV)}
    nc = bacc.Bacc("TRN2", target_bir_lowering=False, num_devices=1)
    args = [nc.dram_tensor(k, a.shape, mybir.dt.from_np(a.dtype), kind="ExternalInput").ap() for k, a in arrays.items()]
    args += [nc.dram_tensor(k, s, F32, kind="ExternalOutput").ap() for k, s in outs.items()]
    build(nc, *args)
    r = run(nc, [arrays], core_ids=[0]).results[0]
    y = r["yT"].transpose(2, 1, 0).reshape(N, D)

    def token_rows(a):
        return a.transpose(0, 2, 1).reshape(L, 1, P, NKV, HD)

    return (y[None, 0:T], y[T:N, None],
            token_rows(r["kp"]), token_rows(r["vp"]),
            r["sp"].reshape(L, 2, GK, 2, GV).transpose(0, 3, 1, 2, 4).reshape(L, 1, GH, GK, GV),
            r["ks"].transpose(0, 2, 3, 1).reshape(L, NS, P, NKV, HD),
            r["vs"].transpose(0, 2, 1, 3).reshape(L, NS, P, NKV, HD),
            r["ss"].reshape(L, 2, GK, NS, 2, GV).transpose(0, 3, 4, 1, 2, 5).reshape(L, NS, GH, GK, GV))
```
